# Optimizing a Trainium2 kernel written in Bass

```python
import math
import jax, jax.numpy as jnp
from jax import lax
import numpy as np

D_MODEL = 1024
BATCH = 1
SEQ = 512
DEPTH = 1

MIX_WIDTH = D_MODEL
HEAD_DIM = 64
NSA_HEADS = 8
NSA_KV_GROUPS = 2
HEADS_PER_GROUP = NSA_HEADS // NSA_KV_GROUPS
NSA_WIDTH = NSA_HEADS * HEAD_DIM
KV_WIDTH = NSA_KV_GROUPS * HEAD_DIM
CONV_WIDTH = MIX_WIDTH - NSA_WIDTH
CONV_GROUPS = CONV_WIDTH // HEAD_DIM
CONV_K = 3
CMP_STRIDE = 16
CMP_BLOCK = 2 * CMP_STRIDE
CMP_HIDDEN = 128
SLC_BLOCK = 64
SLC_TOPK = 8
WINDOW = 256
Q_BLOCK = 64
FORCE_BONUS = 1.0e4
N_BUCKETS = 32
MAX_DISTANCE = 128
MEM_HEADS = 4
MEM_HEAD_DIM = 64
MEM_WIDTH = MEM_HEADS * MEM_HEAD_DIM
MEM_LEN = 256
FFN_HIDDEN = -(-8 * D_MODEL // (3 * 256)) * 256
RMS_EPS = 1e-6
NEG_INF = -1e30
IN_SIZES = (NSA_WIDTH,) + (KV_WIDTH,) * 6 + (3 * NSA_HEADS,) + (CONV_WIDTH,) * 3
IN_WIDTH = sum(IN_SIZES)
IN_SPLITS = tuple(int(s) for s in np.cumsum(IN_SIZES)[:-1])


def rmsnorm(x, g):
    xf = x.astype(jnp.float32)
    y = xf * lax.rsqrt(jnp.mean(xf * xf, axis=-1, keepdims=True) + RMS_EPS)
    return (y * g.astype(jnp.float32)).astype(x.dtype)

def t5_bucket(dist):
    n = jnp.maximum(dist, 0)
    max_exact = N_BUCKETS // 2
    nf = jnp.maximum(n, 1).astype(jnp.float32)
    large = max_exact + (jnp.log(nf / max_exact) / math.log(MAX_DISTANCE / max_exact)
                         * (N_BUCKETS - max_exact)).astype(jnp.int32)
    large = jnp.minimum(large, N_BUCKETS - 1)
    return jnp.where(n < max_exact, n, large)

def masked_softmax(logits, mask, axis):
    maskf = mask.astype(jnp.float32)
    logits = jnp.where(mask, logits, NEG_INF)
    m = jnp.max(logits, axis=axis, keepdims=True)
    e = jnp.exp(logits - m) * maskf
    return e / jnp.maximum(jnp.sum(e, axis=axis, keepdims=True), 1e-30)

def compress_blocks(kv, pe, w1, w2):
    B, S, G, Dh = kv.shape
    ch = kv.reshape(B, S // CMP_STRIDE, CMP_STRIDE, G, Dh)
    blocks = jnp.concatenate([ch[:, :-1], ch[:, 1:]], axis=2)
    blocks = blocks + pe[None, None, :, None, :]
    n = blocks.shape[1]
    flat = blocks.transpose(0, 1, 3, 2, 4).reshape(B, n, G, CMP_BLOCK * Dh)
    return jax.nn.gelu(flat @ w1) @ w2

def nsa_attention(q, k_c, v_c, k_s, v_s, k_w, v_w, gates, rel_bias, pe, ck1, ck2, cv1, cv2):
    B, S, G, HPG, Dh = q.shape
    scale = Dh ** -0.5
    kcmp = compress_blocks(k_c, pe, ck1, ck2)
    vcmp = compress_blocks(v_c, pe, cv1, cv2)
    n_cmp = kcmp.shape[1]
    cmp_end = jnp.arange(n_cmp, dtype=jnp.int32) * CMP_STRIDE + CMP_BLOCK - 1
    n_slc = S // SLC_BLOCK
    topk = min(SLC_TOPK, n_slc)
    cs = np.arange(n_cmp) * CMP_STRIDE
    ss = np.arange(n_slc) * SLC_BLOCK
    ov = np.clip(np.minimum(cs[:, None] + CMP_BLOCK, ss[None, :] + SLC_BLOCK)
                 - np.maximum(cs[:, None], ss[None, :]), 0, None) / CMP_BLOCK
    ov = jnp.asarray(ov, dtype=jnp.float32)
    ks_blk = k_s.reshape(B, n_slc, SLC_BLOCK, G, Dh).transpose(0, 3, 1, 2, 4)
    vs_blk = v_s.reshape(B, n_slc, SLC_BLOCK, G, Dh).transpose(0, 3, 1, 2, 4)
    gather_blocks = jax.vmap(jax.vmap(lambda kb, ix: kb[ix]))
    rb_sel = rel_bias.reshape(G, HPG, N_BUCKETS).transpose(0, 2, 1)
    g_index = jnp.arange(G)[None, None, :, None, None]
    kw_pad = jnp.pad(k_w, ((0, 0), (WINDOW, 0), (0, 0), (0, 0)))
    vw_pad = jnp.pad(v_w, ((0, 0), (WINDOW, 0), (0, 0), (0, 0)))
    kw_len = WINDOW + Q_BLOCK
    dist_w = jnp.arange(Q_BLOCK)[:, None] + WINDOW - jnp.arange(kw_len)[None, :]
    band = (dist_w >= 0) & (dist_w < WINDOW)
    bias_w = rel_bias[:, t5_bucket(dist_w)].reshape(G, HPG, Q_BLOCK, kw_len).transpose(2, 0, 1, 3)

    def chunk(args):
        c, q_c, g_c = args
        t = c * Q_BLOCK + jnp.arange(Q_BLOCK, dtype=jnp.int32)
        dist_c = t[:, None] - cmp_end[None, :]
        bias_c = rel_bias[:, t5_bucket(dist_c)].reshape(G, HPG, Q_BLOCK, n_cmp).transpose(2, 0, 1, 3)
        lg = jnp.einsum('bqghd,bngd->bqghn', q_c, kcmp).astype(jnp.float32) * scale + bias_c
        p_cmp = masked_softmax(lg, (dist_c >= 0)[:, None, None, :], -1)
        o_cmp = jnp.einsum('bqghn,bngd->bqghd', p_cmp, vcmp.astype(jnp.float32))
        imp = jnp.einsum('bqghn,nj->bqgj', p_cmp, ov)
        blk = jnp.arange(n_slc, dtype=jnp.int32)[None, :]
        cur = (t // SLC_BLOCK)[:, None]
        valid = blk <= cur
        forced = (blk == 0) | (blk == cur) | (blk == cur - 1)
        score = jnp.where(valid[:, None, :], imp + jnp.where(forced, FORCE_BONUS, 0.0)[:, None, :], NEG_INF)
        top_val, top_idx = lax.top_k(score, topk)
        sel_ok = top_val > 0.5 * NEG_INF
        idx_bg = top_idx.transpose(0, 2, 1, 3)
        k_sel = gather_blocks(ks_blk, idx_bg)
        v_sel = gather_blocks(vs_blk, idx_bg)
        pos = top_idx[..., None] * SLC_BLOCK + jnp.arange(SLC_BLOCK, dtype=jnp.int32)
        dist_s = t[None, :, None, None, None] - pos
        mask_s = sel_ok[..., None] & (dist_s >= 0)
        bias_s = jnp.moveaxis(rb_sel[g_index, t5_bucket(dist_s)], -1, 3)
        lg = jnp.einsum('bqghd,bgqkjd->bqghkj', q_c, k_sel).astype(jnp.float32) * scale + bias_s
        p_sel = masked_softmax(lg, mask_s[:, :, :, None], (-2, -1))
        o_sel = jnp.einsum('bqghkj,bgqkjd->bqghd', p_sel, v_sel.astype(jnp.float32))
        kw_c = lax.dynamic_slice_in_dim(kw_pad, c * Q_BLOCK, kw_len, axis=1)
        vw_c = lax.dynamic_slice_in_dim(vw_pad, c * Q_BLOCK, kw_len, axis=1)
        s_pos = c * Q_BLOCK - WINDOW + jnp.arange(kw_len, dtype=jnp.int32)
        mask_w = band & (s_pos >= 0)[None, :]
        lg = jnp.einsum('bqghd,bkgd->bqghk', q_c, kw_c).astype(jnp.float32) * scale + bias_w
        p_win = masked_softmax(lg, mask_w[:, None, None, :], -1)
        o_win = jnp.einsum('bqghk,bkgd->bqghd', p_win, vw_c.astype(jnp.float32))
        out = g_c[..., 0:1] * o_cmp + g_c[..., 1:2] * o_sel + g_c[..., 2:3] * o_win
        return out.astype(q.dtype)

    nc = S // Q_BLOCK
    q_chunks = jnp.moveaxis(q.reshape(B, nc, Q_BLOCK, G, HPG, Dh), 1, 0)
    g_chunks = jnp.moveaxis(gates.reshape(B, nc, Q_BLOCK, G, HPG, 3), 1, 0)
    out = lax.map(chunk, (jnp.arange(nc, dtype=jnp.int32), q_chunks, g_chunks))
    return jnp.moveaxis(out, 0, 1).reshape(B, S, G, HPG, Dh)

def hybrid_mixer(h, w_in, w_out, gn_nsa, gn_conv, conv_w, rel_bias, pe, ck1, ck2, cv1, cv2):
    B, S, _ = h.shape
    proj = h @ w_in
    q, kc, vc, ks, vs, kw, vw, gl, cb, cc, cx = jnp.split(proj, IN_SPLITS, axis=-1)
    G, HPG, Dh = NSA_KV_GROUPS, HEADS_PER_GROUP, HEAD_DIM
    kvr = lambda a: a.reshape(B, S, G, Dh)
    gates = jax.nn.sigmoid(gl.astype(jnp.float32)).reshape(B, S, G, HPG, 3)
    o_nsa = nsa_attention(q.reshape(B, S, G, HPG, Dh), kvr(kc), kvr(vc), kvr(ks), kvr(vs),
                          kvr(kw), kvr(vw), gates, rel_bias, pe, ck1, ck2, cv1, cv2)
    o_nsa = o_nsa.reshape(B, S, NSA_WIDTH)
    u = cc * cx
    u_pad = jnp.pad(u, ((0, 0), (CONV_K - 1, 0), (0, 0)))
    y = sum(conv_w[k] * u_pad[:, CONV_K - 1 - k: CONV_K - 1 - k + S] for k in range(CONV_K))
    o_conv = cb * y
    merged = jnp.concatenate([rmsnorm(o_nsa, gn_nsa), rmsnorm(o_conv, gn_conv)], axis=-1)
    return merged @ w_out

def memory_attention(h, mem_n, wq, wkv, wo):
    B, S, _ = h.shape
    M = mem_n.shape[1]
    q = (h @ wq).reshape(B, S, MEM_HEADS, MEM_HEAD_DIM)
    k, v = jnp.split(mem_n @ wkv, 2, axis=-1)
    k = k.reshape(B, M, MEM_HEADS, MEM_HEAD_DIM)
    v = v.reshape(B, M, MEM_HEADS, MEM_HEAD_DIM)
    lg = jnp.einsum('bshd,bmhd->bhsm', q, k).astype(jnp.float32) * (MEM_HEAD_DIM ** -0.5)
    p = jax.nn.softmax(lg, axis=-1)
    o = jnp.einsum('bhsm,bmhd->bshd', p, v.astype(jnp.float32)).reshape(B, S, MEM_WIDTH)
    return o.astype(h.dtype) @ wo

def swiglu(h, wg, wu, wd):
    return (jax.nn.silu(h @ wg) * (h @ wu)) @ wd

def first_inputs(seed: int = 0) -> dict:
    key = jax.random.key(seed)
    ks = jax.random.split(key, 24)
    f32 = jnp.float32
    nrm = lambda k, shape, fan_in: jax.random.normal(k, shape, f32) * fan_in ** -0.5
    gain = lambda k, shape: 1.0 + 0.05 * jax.random.normal(k, shape, f32)
    return {
        "x": jax.random.normal(ks[0], (BATCH, SEQ, D_MODEL), f32),
        "mem": jax.random.normal(ks[1], (BATCH, MEM_LEN, D_MODEL), f32),
        "rel_bias": 0.3 * jax.random.normal(ks[2], (NSA_HEADS, N_BUCKETS), f32),
        "norms": gain(ks[3], (DEPTH, 6, D_MODEL)),
        "mem_norm": gain(ks[4], (DEPTH, D_MODEL)),
        "gn_nsa": gain(ks[5], (DEPTH, NSA_WIDTH)),
        "gn_conv": gain(ks[6], (DEPTH, CONV_WIDTH)),
        "w_in": nrm(ks[7], (DEPTH, D_MODEL, IN_WIDTH), D_MODEL),
        "w_out": nrm(ks[8], (DEPTH, MIX_WIDTH, D_MODEL), MIX_WIDTH),
        "cmp_pe": 0.1 * jax.random.normal(ks[9], (DEPTH, CMP_BLOCK, HEAD_DIM), f32),
        "cmp_k_w1": nrm(ks[10], (DEPTH, CMP_BLOCK * HEAD_DIM, CMP_HIDDEN), CMP_BLOCK * HEAD_DIM),
        "cmp_k_w2": nrm(ks[11], (DEPTH, CMP_HIDDEN, HEAD_DIM), CMP_HIDDEN),
        "cmp_v_w1": nrm(ks[12], (DEPTH, CMP_BLOCK * HEAD_DIM, CMP_HIDDEN), CMP_BLOCK * HEAD_DIM),
        "cmp_v_w2": nrm(ks[13], (DEPTH, CMP_HIDDEN, HEAD_DIM), CMP_HIDDEN),
        "conv_w": nrm(ks[14], (DEPTH, CONV_K, CONV_WIDTH), CONV_K),
        "mem_wq": nrm(ks[15], (DEPTH, D_MODEL, MEM_WIDTH), D_MODEL),
        "mem_wkv": nrm(ks[16], (DEPTH, D_MODEL, 2 * MEM_WIDTH), D_MODEL),
        "mem_wo": nrm(ks[17], (DEPTH, MEM_WIDTH, D_MODEL), MEM_WIDTH),
        "ffn_wg": nrm(ks[18], (DEPTH, D_MODEL, FFN_HIDDEN), D_MODEL),
        "ffn_wu": nrm(ks[19], (DEPTH, D_MODEL, FFN_HIDDEN), D_MODEL),
        "ffn_wd": nrm(ks[20], (DEPTH, FFN_HIDDEN, D_MODEL), FFN_HIDDEN),
    }

def first_block(x, mem, rel_bias, norms, mem_norm, gn_nsa, gn_conv, w_in, w_out, cmp_pe,
              cmp_k_w1, cmp_k_w2, cmp_v_w1, cmp_v_w2, conv_w, mem_wq, mem_wkv, mem_wo,
              ffn_wg, ffn_wu, ffn_wd):
    for l in range(DEPTH):
        h = hybrid_mixer(rmsnorm(x, norms[l, 0]), w_in[l], w_out[l], gn_nsa[l], gn_conv[l], conv_w[l],
                         rel_bias, cmp_pe[l], cmp_k_w1[l], cmp_k_w2[l], cmp_v_w1[l], cmp_v_w2[l])
        x = x + rmsnorm(h, norms[l, 1])
        h = memory_attention(rmsnorm(x, norms[l, 2]), rmsnorm(mem, mem_norm[l]),
                             mem_wq[l], mem_wkv[l], mem_wo[l])
        x = x + rmsnorm(h, norms[l, 3])
        h = swiglu(rmsnorm(x, norms[l, 4]), ffn_wg[l], ffn_wu[l], ffn_wd[l])
        x = x + rmsnorm(h, norms[l, 5])
    return x


CHUNK = 64
LEFT_CHUNKS = 8
A_HEADS = 8
A_HEAD_DIM = 64
A_WIDTH = A_HEADS * A_HEAD_DIM
REL_CLIP = 128
B_HEADS = 4
B_HEAD_DIM = 128
B_WIDTH = B_HEADS * B_HEAD_DIM
CONV_K_2 = 4
PEER_HEADS = 8
N_KEYS = 128
N_EXPERTS = N_KEYS * N_KEYS
PEER_TOPK = 16
D_KEY = 256
PEER_BLOCK = 128
EPS = 1e-6
IN_SIZES_2 = [A_WIDTH, A_WIDTH, A_WIDTH, 2 * B_WIDTH, B_WIDTH, B_WIDTH, B_HEADS, B_HEADS, D_MODEL, D_MODEL]
IN_COLS = sum(IN_SIZES_2)


def rmsnorm_2(x, g):
    xf = x.astype(jnp.float32)
    y = xf * lax.rsqrt(jnp.mean(xf * xf, axis=-1, keepdims=True) + EPS)
    return (y * g.astype(jnp.float32)).astype(x.dtype)

def modulate(h, shift, scale):
    return h * (1.0 + scale[:, None, :]) + shift[:, None, :]

def causal_depthwise_conv(u, w, b):
    C = u.shape[-1]
    out = lax.conv_general_dilated(
        u, w[:, None, :].astype(u.dtype), window_strides=(1,), padding=[(CONV_K_2 - 1, 0)],
        dimension_numbers=("NWC", "WIO", "NWC"), feature_group_count=C)
    return out + b

def chunk_band_attention(q, k, v, rel_bias):
    B, S, H, dh = q.shape
    nc = S // CHUNK
    pad = LEFT_CHUNKS * CHUNK
    band = pad + CHUNK
    kp = jnp.pad(k, ((0, 0), (pad, 0), (0, 0), (0, 0)))
    vp = jnp.pad(v, ((0, 0), (pad, 0), (0, 0), (0, 0)))
    qc = q.reshape(B, nc, CHUNK, H, dh).transpose(1, 0, 2, 3, 4)
    k_idx = jnp.arange(band)
    rel = jnp.clip(jnp.arange(CHUNK)[:, None] + pad - k_idx[None, :], -REL_CLIP, REL_CLIP) + REL_CLIP
    bias = rel_bias[:, rel].astype(jnp.float32)
    scale = dh ** -0.5

    def one_chunk(args):
        j, qj = args
        kj = lax.dynamic_slice_in_dim(kp, j * CHUNK, band, axis=1)
        vj = lax.dynamic_slice_in_dim(vp, j * CHUNK, band, axis=1)
        s = jnp.einsum("blhd,bkhd->bhlk", qj, kj).astype(jnp.float32) * scale + bias
        valid = (j * CHUNK + k_idx - pad) >= 0
        s = jnp.where(valid[None, None, None, :], s, -jnp.inf)
        p = jax.nn.softmax(s, axis=-1).astype(vj.dtype)
        return jnp.einsum("bhlk,bkhd->blhd", p, vj)

    out = lax.map(one_chunk, (jnp.arange(nc), qc))
    return out.transpose(1, 0, 2, 3, 4).reshape(B, S, H * dh)

def mlstm_chunkwise(q, k, v, i_pre, f_pre):
    B, S, H, d = q.shape
    nc = S // CHUNK
    k = k * (d ** -0.5)
    to_c = lambda t: t.reshape(B, nc, CHUNK, H, d).transpose(1, 0, 3, 2, 4)
    qc, kc, vc = to_c(q), to_c(k), to_c(v)
    li = i_pre.astype(jnp.float32).reshape(B, nc, CHUNK, H).transpose(1, 0, 3, 2)
    lf = jax.nn.log_sigmoid(f_pre.astype(jnp.float32)).reshape(B, nc, CHUNK, H).transpose(1, 0, 3, 2)
    a = jnp.cumsum(lf, axis=-1)
    A = a[..., -1]
    causal = jnp.tril(jnp.ones((CHUNK, CHUNK), dtype=bool))

    def step(carry, inp):
        C, n, m = carry
        qj, kj, vj, aj, Aj, lij = inp
        D = aj[..., :, None] - aj[..., None, :] + lij[..., None, :]
        D = jnp.where(causal, D, -jnp.inf)
        inter = aj + m[..., None]
        m_row = jnp.maximum(inter, jnp.max(D, axis=-1))
        w_inter = jnp.exp(inter - m_row)
        Wd = jnp.exp(D - m_row[..., None])
        qk = jnp.einsum("bhld,bhsd->bhls", qj, kj).astype(jnp.float32) * Wd
        num = w_inter[..., None] * jnp.einsum("bhld,bhde->bhle", qj, C) + jnp.einsum("bhls,bhse->bhle", qk, vj)
        den = w_inter * jnp.einsum("bhld,bhd->bhl", qj, n) + jnp.sum(qk, axis=-1)
        h = num / jnp.maximum(jnp.abs(den), jnp.exp(-m_row))[..., None]
        g = Aj[..., None] - aj + lij
        m_new = jnp.maximum(Aj + m, jnp.max(g, axis=-1))
        decay = jnp.exp(Aj + m - m_new)
        wk = jnp.exp(g - m_new[..., None])
        C_new = decay[..., None, None] * C + jnp.einsum("bhl,bhld,bhle->bhde", wk, kj, vj)
        n_new = decay[..., None] * n + jnp.einsum("bhl,bhld->bhd", wk, kj)
        return (C_new, n_new, m_new), h

    init = (jnp.zeros((B, H, d, d), jnp.float32), jnp.zeros((B, H, d), jnp.float32), jnp.zeros((B, H), jnp.float32))
    _, hs = lax.scan(step, init, (qc, kc, vc, a, A, li))
    return hs.transpose(1, 0, 3, 2, 4).reshape(B, S, H, d).astype(v.dtype)

def peer_ffn(h, w_pq, sub_keys, u_exp, v_exp):
    B, S, D = h.shape
    T = B * S
    hb = h.reshape(T // PEER_BLOCK, PEER_BLOCK, D)

    def block(xb):
        q = (xb @ w_pq).reshape(PEER_BLOCK, PEER_HEADS, 2, D_KEY // 2)
        s = jnp.einsum("thpd,hpnd->thpn", q, sub_keys).astype(jnp.float32)
        s_top, i_top = lax.top_k(s, PEER_TOPK)
        cand = (s_top[:, :, 0, :, None] + s_top[:, :, 1, None, :]).reshape(PEER_BLOCK, PEER_HEADS, PEER_TOPK * PEER_TOPK)
        best, ci = lax.top_k(cand, PEER_TOPK)
        i1 = jnp.take_along_axis(i_top[:, :, 0, :], ci // PEER_TOPK, axis=-1)
        i2 = jnp.take_along_axis(i_top[:, :, 1, :], ci % PEER_TOPK, axis=-1)
        e = i1 * N_KEYS + i2
        gate = jax.nn.softmax(best, axis=-1)
        u = u_exp[e]
        v = v_exp[e]
        act = jax.nn.gelu(jnp.einsum("thkd,td->thk", u, xb))
        return jnp.einsum("thk,thkd->td", (gate * act).astype(xb.dtype), v)

    return lax.map(block, hb).reshape(B, S, D)

def second_inputs(seed: int = 0) -> dict:
    key = jax.random.key(seed)
    ks = jax.random.split(key, 24)
    nrm = lambda k, shape, s: jax.random.normal(k, shape, jnp.float32) * s
    L = DEPTH
    return {
        "x": nrm(ks[0], (BATCH, SEQ, D_MODEL), 1.0),
        "c": nrm(ks[1], (BATCH, D_MODEL), 1.0),
        "w_ada": nrm(ks[2], (L, D_MODEL, 6 * D_MODEL), 0.5 * D_MODEL ** -0.5),
        "b_ada": nrm(ks[3], (L, 6 * D_MODEL), 0.02),
        "norm1_g": 1.0 + nrm(ks[4], (L, D_MODEL), 0.02),
        "w_in": nrm(ks[5], (L, D_MODEL, IN_COLS), D_MODEL ** -0.5),
        "conv_w": nrm(ks[6], (L, CONV_K_2, 2 * B_WIDTH), CONV_K_2 ** -0.5),
        "conv_b": nrm(ks[7], (L, 2 * B_WIDTH), 0.02),
        "b_igate": nrm(ks[8], (L, B_HEADS), 0.1),
        "b_fgate": jnp.linspace(3.0, 6.0, B_HEADS)[None, :] + nrm(ks[9], (L, B_HEADS), 0.1),
        "rel_bias": nrm(ks[10], (L, A_HEADS, 2 * REL_CLIP + 1), 0.1),
        "mlstm_norm_g": 1.0 + nrm(ks[11], (L, B_WIDTH), 0.02),
        "w_branch_a": nrm(ks[12], (L, A_WIDTH, D_MODEL), A_WIDTH ** -0.5),
        "w_branch_b": nrm(ks[13], (L, B_WIDTH, D_MODEL), B_WIDTH ** -0.5),
        "w_out": nrm(ks[14], (L, D_MODEL, D_MODEL), D_MODEL ** -0.5),
        "norm2_g": 1.0 + nrm(ks[15], (L, D_MODEL), 0.02),
        "w_peer_q": nrm(ks[16], (L, D_MODEL, PEER_HEADS * D_KEY), D_MODEL ** -0.5),
        "peer_sub_keys": nrm(ks[17], (L, PEER_HEADS, 2, N_KEYS, D_KEY // 2), (D_KEY // 2) ** -0.5),
        "peer_u": nrm(ks[18], (L, N_EXPERTS, D_MODEL), D_MODEL ** -0.5),
        "peer_v": nrm(ks[19], (L, N_EXPERTS, D_MODEL), 0.5),
        "final_g": 1.0 + nrm(ks[20], (D_MODEL,), 0.02),
    }

def second_block(x, c, w_ada, b_ada, norm1_g, w_in, conv_w, conv_b, b_igate, b_fgate, rel_bias, mlstm_norm_g,
              w_branch_a, w_branch_b, w_out, norm2_g, w_peer_q, peer_sub_keys, peer_u, peer_v, final_g):
    B, S, _ = x.shape
    split_at = [int(s) for s in np.cumsum(IN_SIZES_2)[:-1]]
    for l in range(DEPTH):
        mod = jax.nn.silu(c) @ w_ada[l] + b_ada[l]
        sh1, sc1, gt1, sh2, sc2, gt2 = jnp.split(mod, 6, axis=-1)

        h = modulate(rmsnorm_2(x, norm1_g[l]), sh1, sc1)
        proj = h @ w_in[l]
        qa, ka, va, qkb, vb, ob, ib, fb, ga, gb = jnp.split(proj, split_at, axis=-1)
        qkb = jax.nn.silu(causal_depthwise_conv(qkb, conv_w[l], conv_b[l]))
        qb, kb = jnp.split(qkb, 2, axis=-1)
        heads_a = lambda t: t.reshape(B, S, A_HEADS, A_HEAD_DIM)
        heads_b = lambda t: t.reshape(B, S, B_HEADS, B_HEAD_DIM)
        y_a = chunk_band_attention(heads_a(qa), heads_a(ka), heads_a(va), rel_bias[l])
        hb = mlstm_chunkwise(heads_b(qb), heads_b(kb), heads_b(vb), ib + b_igate[l], fb + b_fgate[l])
        hb = rmsnorm_2(hb, mlstm_norm_g[l].reshape(B_HEADS, B_HEAD_DIM)).reshape(B, S, B_WIDTH)
        y_b = jax.nn.sigmoid(ob) * hb
        y = jax.nn.sigmoid(ga) * (y_a @ w_branch_a[l]) + jax.nn.sigmoid(gb) * (y_b @ w_branch_b[l])
        x = x + gt1[:, None, :] * (y @ w_out[l])

        h2 = modulate(rmsnorm_2(x, norm2_g[l]), sh2, sc2)
        x = x + gt2[:, None, :] * peer_ffn(h2, w_peer_q[l], peer_sub_keys[l], peer_u[l], peer_v[l])
    return rmsnorm_2(x, final_g)


def setup_inputs(seed=0):
    out = dict(first_inputs(seed))
    for name, value in second_inputs(seed + 1).items():
        if name != "x":
            out[name + "_2"] = value
    return out


def reference(
    x, mem, rel_bias, norms, mem_norm, gn_nsa, gn_conv, w_in, w_out, cmp_pe, cmp_k_w1, cmp_k_w2,
    cmp_v_w1, cmp_v_w2, conv_w, mem_wq, mem_wkv, mem_wo, ffn_wg, ffn_wu, ffn_wd, c_2, w_ada_2,
    b_ada_2, norm1_g_2, w_in_2, conv_w_2, conv_b_2, b_igate_2, b_fgate_2, rel_bias_2,
    mlstm_norm_g_2, w_branch_a_2, w_branch_b_2, w_out_2, norm2_g_2, w_peer_q_2, peer_sub_keys_2,
    peer_u_2, peer_v_2, final_g_2,
):
    x = first_block(
        x, mem, rel_bias, norms, mem_norm, gn_nsa, gn_conv, w_in, w_out, cmp_pe, cmp_k_w1,
        cmp_k_w2, cmp_v_w1, cmp_v_w2, conv_w, mem_wq, mem_wkv, mem_wo, ffn_wg, ffn_wu, ffn_wd,
    )
    return second_block(
        x, c_2, w_ada_2, b_ada_2, norm1_g_2, w_in_2, conv_w_2, conv_b_2, b_igate_2, b_fgate_2,
        rel_bias_2, mlstm_norm_g_2, w_branch_a_2, w_branch_b_2, w_out_2, norm2_g_2, w_peer_q_2,
        peer_sub_keys_2, peer_u_2, peer_v_2, final_g_2,
    )


_drawn_inputs = setup_inputs


def setup_inputs(seed=0):
    import zlib

    import numpy as np

    out = dict(_drawn_inputs(seed))
    spreads = {}
    factors = {'b_ada_2': 6.157,
     'norm1_g_2': 8.0,
     'conv_w_2': 4.907,
     'conv_b_2': 64.0,
     'b_igate_2': 64.0,
     'b_fgate_2': 5.329,
     'rel_bias_2': 8.0,
     'mlstm_norm_g_2': 22.005,
     'norm2_g_2': 8.0,
     'final_g_2': 7.875}
    for name, (base, spread) in spreads.items():
        noise = np.random.default_rng([zlib.crc32(name.encode()), seed]).standard_normal(out[name].shape)
        drawn = base * np.exp(spread * noise) if base else spread * noise
        out[name] = __import__('jax').numpy.asarray(drawn.astype(out[name].dtype))
    for name, factor in factors.items():
        out[name] = (out[name] * factor).astype(out[name].dtype)
    return out
```

```python
from contextlib import ExitStack
import math

import numpy as np

import concourse.bass as bass
from concourse import mybir

F32 = mybir.dt.float32
U32 = mybir.dt.uint32
ALU = mybir.AluOpType
ACT = mybir.ActivationFunctionType
AX = mybir.AxisListType

P = 128
T = 512
NT = T // P
D = 1024
KD = D // P
NH, HD = 8, 64
NCMP = 31
NM = 256
MH = 4
FH = 2816
KF = FH // P
BH = 4
RING = 8
PH = 8
TOPK = 16
JB = 8
NB = 128 // JB
GT = 16
EPS = 1e-6
BIG = 1e30
QS = -0.125


SMALL = {}


def small_columns():
    at = 0
    for name, n in [("norm0", 8), ("norm1", 8), ("norm2", 8), ("norm3", 8), ("norm4", 8), ("norm5", 8),
                    ("mem_norm", 8), ("gn_nsa", 4), ("gn_conv", 4), ("conv_w", 12), ("b_ada", 48),
                    ("norm1_2", 8), ("conv_w2", 32), ("conv_b2", 8), ("mlstm_g", 4), ("norm2_2", 8),
                    ("final_g", 8), ("cond", 8), ("pe", 32), ("b_if", 2),
                    ("w2k", 256), ("w2v", 64)]:
        SMALL[name] = (at, n)
        at += n
    return at


N_SMALL = small_columns()

C_ID, C_ONE, C_IOTA, C_SEL, C_TRI, C_ROW = 0, 128, 256, 384, 896, 1024
N_CONST = 1025


def constants():
    c = np.zeros((P, N_CONST), np.float32)
    c[:, C_ID:C_ID + P] = np.eye(P)
    c[:, C_ONE:C_ONE + P] = 1.0
    c[:, C_IOTA:C_IOTA + P] = np.arange(P)
    for h in range(BH):
        c[h, C_SEL + h * P:C_SEL + (h + 1) * P] = 1.0
    s, t = np.meshgrid(np.arange(P), np.arange(P), indexing="ij")
    c[:, C_TRI:C_TRI + P] = np.where(s > t, BIG, 0.0)
    c[:, C_ROW] = np.arange(P) >= 31
    return c


def cols(v):
    return np.reshape(v, (-1, P)).T


def tile_k(w):
    k, n = w.shape
    return w.reshape(k // P, P, n // P, P).transpose(2, 1, 0, 3).reshape(n // P, P, -1)


def padded(tiles):
    return np.pad(tiles, ((0, 0), (0, 0), (0, D - tiles.shape[2])))


def token_tiles(w):
    return w.reshape(4, 2, P, 512).transpose(0, 2, 1, 3).reshape(4, P, 1024)


def weight_stream(i):
    w_in = i["w_in"][0]
    heads = np.concatenate([np.r_[h * HD:(h + 1) * HD, (h + 4) * HD:(h + 5) * HD] for h in range(4)])
    out = [tile_k(w_in[:, heads])]
    for c in (512, 640, 768, 1024):
        out.append(tile_k(w_in[:, c:c + 128]))
    out.append(token_tiles(np.pad(w_in[:, 896:1304], ((0, 0), (0, 104)))))
    for j in range(4):
        for c in (1816, 2328, 1304):
            out.append(tile_k(w_in[:, c + j * P:c + (j + 1) * P]))
    for w in (i["cmp_k_w1"][0], i["cmp_v_w1"][0]):
        one = w.reshape(4, 8, HD, P).transpose(0, 2, 1, 3).reshape(4, HD, 1024)
        out.append(np.concatenate([one, one], axis=1))
    out.append(tile_k(i["w_out"][0]))
    out.append(tile_k(i["mem_wq"][0]))
    out.append(tile_k(i["mem_wkv"][0][:, :256]))
    out.append(i["mem_wkv"][0][:, 256:].reshape(2, 4, P, 256).transpose(0, 2, 1, 3).reshape(2, P, 1024))
    out.append(tile_k(i["mem_wo"][0]).reshape(2, 4, P, 256).transpose(0, 2, 1, 3).reshape(2, P, 1024))
    wg, wu, ada = tile_k(i["ffn_wg"][0]), tile_k(i["ffn_wu"][0]), tile_k(i["w_ada_2"][0])
    for m in range(KF):
        out += [wg[m:m + 1], wu[m:m + 1], ada[2 * m:2 * m + 2]]
    out.append(ada[2 * KF:])
    wd = tile_k(i["ffn_wd"][0])
    out.append(np.pad(wd, ((0, 0), (0, 0), (0, 256))).reshape(8, P, 3, 1024).transpose(0, 2, 1, 3).reshape(24, P, 1024))
    w2 = i["w_in_2"][0]
    out.append(tile_k(w2[:, 0:1024]))
    out.append(tile_k(w2[:, 1536:2560]))
    out.append(tile_k(np.pad(w2[:, 3584:3592], ((0, 0), (0, 120)))))
    out.append(tile_k(w2[:, 3072:3584]))
    out.append(token_tiles(w2[:, 1024:1536]))
    out.append(token_tiles(w2[:, 2560:3072]))
    ga, gb = tile_k(w2[:, 3592:4616]), tile_k(w2[:, 4616:5640])
    ab = np.concatenate([tile_k(i["w_branch_a_2"][0]), tile_k(i["w_branch_b_2"][0])], axis=2)
    for m in range(KD):
        out += [ga[m:m + 1], gb[m:m + 1], ab[m:m + 1]]
    out.append(tile_k(i["w_out_2"][0]))
    out.append(tile_k(i["w_peer_q_2"][0]))
    keys = i["peer_sub_keys_2"][0].reshape(2, 8, P, P)
    out.append(keys.transpose(0, 3, 1, 2).reshape(2, P, 1024))
    u = i["peer_u_2"][0].reshape(P, P, KD, P).transpose(1, 3, 2, 0).reshape(P, P, 1024)
    v = i["peer_v_2"][0].reshape(P, NB, JB, KD, P).transpose(1, 3, 0, 2, 4).reshape(NB, KD, P, 1024)
    out.append(u[:JB])
    for b in range(1, NB):
        both = np.stack([u[b * JB:(b + 1) * JB], v[b - 1]], axis=1)
        out.append(both.reshape(2 * JB, P, 1024))
    out.append(v[NB - 1])
    return np.concatenate(out, axis=0)


def buckets(n):
    large = 16 + np.floor(np.log(np.maximum(n, 1) / 16) / math.log(8) * 16 + 1e-9).astype(np.int64)
    return np.where(n < 16, n, np.minimum(large, 31))


def spread(table, index, keep):
    out = np.full((table.shape[0],) + index.shape, -BIG, np.float32)
    out[:, keep] = table[:, index[keep]]
    return np.moveaxis(out, 0, 1).reshape(P, -1)


def biases(i):
    r = np.arange(P)[:, None]
    dist = 384 + r - np.arange(T)[None, :]
    near = buckets(np.maximum(dist, 0))
    sel = spread(i["rel_bias"], near, dist >= 0)
    win = spread(i["rel_bias"], near[:, 128:], ((dist >= 0) & (dist < 256))[:, 128:])
    back = np.arange(T).reshape(NT, P).T[:, :, None] - (16 * np.arange(32) + 31)[None, None, :]
    cmp = spread(i["rel_bias"], buckets(np.maximum(back, 0)), back >= 0)
    rel = np.clip(dist, -128, 128) + 128
    band = spread(i["rel_bias_2"][0], rel, ~((r < 64) & (dist < r - 63)))
    return sel, win, cmp, band


def smalls(i):
    a = {"norm%d" % n: cols(i["norms"][0, n]) for n in range(6)}
    a |= {"mem_norm": cols(i["mem_norm"]), "gn_nsa": cols(i["gn_nsa"]), "gn_conv": cols(i["gn_conv"]),
          "conv_w": cols(i["conv_w"]), "b_ada": cols(i["b_ada_2"]), "norm1_2": cols(i["norm1_g_2"]),
          "conv_w2": cols(i["conv_w_2"]), "conv_b2": cols(i["conv_b_2"]), "mlstm_g": cols(i["mlstm_norm_g_2"]),
          "norm2_2": cols(i["norm2_g_2"]), "final_g": cols(i["final_g_2"]), "cond": cols(i["c_2"])}
    a["pe"] = np.concatenate([i["cmp_pe"][0].T] * 2, axis=0)
    a["b_if"] = np.pad(np.stack([i["b_igate_2"][0], i["b_fgate_2"][0]], 1), ((0, P - BH), (0, 0)))
    w2k, none = i["cmp_k_w2"][0], np.zeros((P, HD), np.float32)
    a["w2k"] = np.concatenate([w2k, none, none, w2k], axis=1)
    a["w2v"] = i["cmp_v_w2"][0]
    return np.concatenate([a[n] for n in SMALL], axis=1)




def build(nc, weights, x_in, mem_in, smalls_in, consts_in, sel_in, win_in, cmp_in, band_in, out):
    ctx = ExitStack()
    with ctx:
        def sb(name, shape, dt=F32):
            return ctx.enter_context(nc.sbuf_tensor(name, shape, dt))

        def sem(name):
            return ctx.enter_context(nc.semaphore(name))

        gates_dram = nc.dram_tensor("gates_spread", (NB, P, T, JB), F32, kind="Internal").ap()

        ring = sb("ring", [P, RING, D])
        xT = sb("xT", [P, KD, T])
        hT = sb("hT", [P, KD, T])
        small = sb("small", [P, N_SMALL])
        const = sb("const", [P, N_CONST])
        sq = sb("sq", [P, 2, T])
        rms = sb("rms", [P, T])
        rstd = sb("rstd", [P, T])
        mod = sb("mod", [P, 48])
        condT = sb("condT", [P, 8])
        gmod = sb("gmod", [P, 16])
        eps = sb("eps", [P, 2])
        pscr = sb("pool_scratch", [P, 2])
        arena = sb("arena", [P, 29700])

        def at(first, *dims):
            n = int(np.prod(dims))
            assert first + n <= 29700, (first, dims)
            v = arena[:, first:first + n]
            names = " ".join("abcd"[:len(dims)])
            return v if len(dims) == 1 else v.rearrange(
                f"p ({names}) -> p {names}", **{"abcd"[k]: dims[k] for k in range(len(dims))})

        logit = at(0, 2, T)
        prob = at(1024, 2, T)
        probT = at(2048, 2, T)
        least = at(3072, 96)
        total = at(3168, 96)
        rgate = at(3264, 96)
        rrec = at(3360, 96)
        qk = at(3500, 8, T)
        vtok = at(7596, NT, 408)
        conv = at(9228, 12, T)
        o_tok = at(15372, NT, T)
        bias_sel = at(17420, NH, T)
        bias_win = at(21516, NH, 384)
        bias_cmp = at(24588, NH, NT, 32)
        pe_col = at(25612, 2)
        hid = at(25614, 2, 2, 32)
        kcmp = at(25742, 32)
        vcmp = at(25774, P)
        gsig = at(25902, NT, 24)
        conv_y = at(26000, 2, T)
        nT = at(17420, 4, T)
        merged = at(19468, 8, T)
        yT = at(3500, 8, T)
        memT = at(7596, KD, NM)
        mT = at(9644, KD, NM)
        mq = at(11692, 2, T)
        mk = at(12716, 2, NM)
        mv = at(13228, 2, NM)
        om_tok = at(13740, NT, NM)
        omT = at(14764, 2, T)
        ff = at(7596, KF, T)
        ff_gate = at(0, 2, T)
        qk2 = at(3500, 8, T)
        cv2 = at(7596, 8, T)
        sig_o = at(11692, 4, T)
        va = at(13740, NT, T)
        vb = at(15788, NT, BH, P + 1)
        bias_band = at(17852, NH, T)
        oa_tok = at(21948, NT, T)
        hb_tok = at(23996, NT, T)
        conv_acc = at(26044, 2, T)
        yaT = at(17852, 4, T)
        ybT = at(19900, 4, T)
        y2T = at(3500, 8, T)
        gate_ab = at(0, 4, T)
        rows = at(27068, 4, T)
        row_f, row_i, row_a, row_b = (rows[0:BH, n, :] for n in range(4))
        tcol = at(29116, 64)
        wdec = at(0, 2, T)
        wdiag = at(1024, 2, P)
        mrow = at(1280, 2, T)
        wqk = at(17852, 2, NT, T)
        den = at(29200, 64)
        hsq = at(21948, NT, T)
        pq = at(0, 16, T)
        s_all = at(8192, 16, P)
        s_left = at(10240, 16, P)
        cand = at(12288, PH, TOPK, TOPK)
        cand_left = at(14336, PH, TOPK, TOPK)
        eqs = at(16384, PH, TOPK, TOPK)
        s_top = at(18432, 16, TOPK)
        i_topf = at(18688, 16, TOPK)
        best = at(18944, PH, TOPK)
        expd = at(19072, PH, TOPK)
        a_f = at(19200, PH, TOPK)
        b_f = at(19328, PH, TOPK)
        chosen = at(19456, 3, P)
        gsum = at(19840, 16)
        i_top = at(19856, 16, TOPK).bitcast(U32)
        c_top = at(20112, PH, TOPK).bitcast(U32)
        c_hi = at(20240, PH, TOPK).bitcast(U32)
        c_lo = at(20368, PH, TOPK).bitcast(U32)
        chosenT = at(20496, 3, T)
        cur = at(22032, 3, 2 * GT)
        hot1 = at(22128, 8, P)
        hot2 = at(23152, 8, P)
        stage = at(24176, 2, NB, GT * JB)
        gblk = at(0, 2, T, JB)
        pact = at(8192, 2, JB, T)
        act = at(16384, 2, T)
        acc = at(17408, KD, T)

        bank = [ctx.enter_context(nc.psum_tensor(f"bank{n}", [P, T], F32)) for n in range(8)]
        ident = const[:, C_ID:C_ID + P]
        ones = const[:, C_ONE:C_ONE + P]
        iota = const[:, C_IOTA:C_IOTA + P]
        rowmask = const[:, C_ROW:C_ROW + 1]

        def sm(name, k=0, n=1, rows=P):
            a = SMALL[name][0] + k
            return small[0:rows, a:a + n]

        consts_in_sem = sem("consts_loaded")
        x_loaded = sem("x_loaded")
        mem_loaded = sem("mem_loaded")
        bias_loaded = sem("bias_loaded")
        band_loaded = sem("band_loaded")
        tile_loaded = [sem(f"tile_loaded{n}") for n in range(RING)]
        tiles_used = sem("tiles_used")
        bias_negated = sem("bias_negated")
        sq_ready = sem("square_ready")
        sq_summed = sem("square_summed")
        rms_ready = sem("rms_ready")
        normed = sem("normed")
        proj_done = sem("proj_done")
        evac_act = sem("evacuated_by_act")
        evac_dve = sem("evacuated_by_dve")
        act_chain = sem("act_chain")
        dve_chain = sem("dve_chain")
        logits_ready = sem("logits_ready")
        qk_done = sem("qk_done")
        prob_ready = sem("prob_ready")
        prob_turned = sem("prob_turned")
        probT_ready = sem("probT_ready")
        pv_done = sem("pv_done")
        head_out = sem("head_out")
        gates_sig = sem("gates_sigmoid")
        conv_ready = sem("conv_ready")
        cmp_hidden = sem("cmp_hidden")
        cmp_pe_ready = sem("cmp_pe_ready")
        cmp_gelu = sem("cmp_gelu")
        cmp_kv = sem("cmp_kv")
        cmp_done = sem("cmp_done")
        turned = sem("turned")
        turned_out = sem("turned_out")
        yb_out = sem("yb_out")
        mrow_out = sem("mrow_out")
        eps_set = sem("eps_set")
        x3_ready = sem("x3_ready")
        cond_ready = sem("cond_ready")
        ada_done = sem("ada_done")
        conv2_acc = sem("conv2_acc")
        conv2_ready = sem("conv2_ready")
        ones_ready = sem("ones_ready")
        y2_ready = sem("y2_ready")
        rows_ln = sem("rows_ln")
        rows_m = sem("rows_m")
        rows_exp = sem("rows_exp")
        cols_done = sem("cols_done")
        cols_out = sem("cols_out")
        mrow_done = sem("mrow_done")
        diag_ready = sem("diag_ready")
        decay_ready = sem("decay_ready")
        lqk_done = sem("lqk_done")
        lqk_ready = sem("lqk_ready")
        lpv_done = sem("lpv_done")
        lnum_out = sem("lnum_out")
        hb_sq = sem("hb_square_mean")
        hb_rms = sem("hb_rms")
        hb_ready = sem("hb_ready")
        score_done = sem("score_done")
        score_out = sem("score_out")
        best_ready = sem("best_ready")
        best_exp = sem("best_exp")
        chosen_ready = sem("chosen_ready")
        chosen_turned = sem("chosen_turned")
        chosen_out = sem("chosen_out")
        cur_ready = sem("cur_ready")
        hot1_ready = sem("hot1_ready")
        hot2_ready = sem("hot2_ready")
        hot_used = sem("hot_used")
        staged = sem("staged")
        stored = [sem("gates_stored0"), sem("gates_stored1")]
        g_loaded = [sem("gates_loaded0"), sem("gates_loaded1")]
        up_done = sem("up_done")
        gelu_ready = sem("gelu_ready")
        pact_ready = sem("pact_ready")
        down_done = sem("down_done")
        down_out = sem("down_out")
        out_stored = sem("out_stored")

        PROJ = [("qk", "A" * 8), ("vtok", "A" * 4), ("conv", "A" * 12), ("w_out", "A" * 8),
                ("mq", "A" * 2), ("mk", "A" * 2), ("mv", "A" * 2), ("mo", "A" * 8),
                ("ffn", "AV" * KF), ("wd", "A" * 8),
                ("qk2", "A" * 8), ("cv2", "A" * 8), ("if", "AA"), ("og", "A" * 4),
                ("va", "A" * 4), ("vb", "A" * 4), ("branch", "AVAV" * KD), ("w_out2", "V" * 8),
                ("pq", "A" * 16)]
        first, takers = {}, ""
        for name, who in PROJ:
            first[name] = len(takers)
            takers += who

        def taken(j):
            who = takers[j]
            return (evac_act if who == "A" else evac_dve), takers[:j + 1].count(who)

        NORMS = [8, 4, 4, 8, 8, 8, 8, 8, 8, 8, 8, 8]
        norm_base = [sum(NORMS[:n]) for n in range(len(NORMS) + 1)]
        UNITS = 96 + 16 + 32

        def nsa_unit(i):
            return i // 32, (i % 32) // NH, i % NH

        def nsa_pieces(i):
            branch, t, _ = nsa_unit(i)
            return [NCMP] if branch == 2 else [P] * (t + 1 if branch == 0 else min(t + 1, 3))

        def nsa_width(i):
            return sum(nsa_pieces(i))

        def nsa_cols(i):
            return P * len(nsa_pieces(i))

        def wait(eng, semaphore, value):
            if not isinstance(value, int) or value > 0:
                eng.wait_ge(semaphore, value)

        block = ctx.enter_context(nc.Block())

        n_tiles = weights.shape[0]
        BEFORE = n_tiles - 2 * NB * JB

        @block.sync
        def _(sp):

            def load(n, slot):
                sp.dma_start(ring[:, slot, :], weights[n]).then_inc(tile_loaded[slot], 16)

            for n in range(RING):
                load(n, n)
            full = BEFORE // RING
            with sp.Fori(1, full) as g:
                for s in range(RING):
                    sp.wait_ge(tiles_used, (g - 1) * RING + s + 1)
                    load(g * RING + s, s)
            for n in range(full * RING, BEFORE):
                sp.wait_ge(tiles_used, n - RING + 1)
                load(n, n % RING)
            def tiles(base, many, i=0, step=0):
                for k in range(many):
                    n = base + k
                    sp.wait_ge(tiles_used, i * step + (n - RING + 1))
                    load(i * step + n, n % RING)

            def gates(b, i=0):
                half = b % 2
                wait(sp, pact_ready, i * (2 * JB) + (b - 1) * JB)
                sp.dma_start(gblk[:, half], gates_dram[i * 2 + b]).then_inc(g_loaded[half], 16)

            def block_tiles(b, i=0, more=True):
                base = BEFORE + JB + 2 * JB * (b - 1)
                tiles(base, 12, i, 4 * JB)
                if more:
                    gates(b + 1, i)
                tiles(base + 12, 4, i, 4 * JB)

            tiles(BEFORE, JB)
            for s in range(2):
                sp.wait_ge(stored[s], 16 * (T // GT // 2))
            gates(0)
            gates(1)
            block_tiles(1)
            with sp.Fori(0, NB // 2 - 2) as i:
                block_tiles(2, i)
                block_tiles(3, i)
            block_tiles(NB - 2)
            block_tiles(NB - 1, more=False)
            tiles(n_tiles - JB, JB)
            for k in range(KD):
                sp.wait_ge(normed, norm_base[11] + k + 1)
                sp.dma_start(out[k], hT[:, k, :]).then_inc(out_stored, 16)
            sp.wait_ge(out_stored, 16 * KD)

        @block.gpsimd
        def _(pool):
            pool.wait_ge(bias_loaded, 48)
            for b in (bias_sel, bias_win, bias_cmp):
                v = b.rearrange("p a b -> p (a b)") if len(b.shape) == 3 else b.rearrange("p a b c -> p (a b c)")
                nc.gpsimd.tensor_scalar(v, v, -1.0, None, ALU.mult).then_inc(bias_negated, 1)
            pool.wait_ge(band_loaded, 16)
            v = bias_band.rearrange("p a b -> p (a b)")
            nc.gpsimd.tensor_scalar(v, v, -1.0, None, ALU.mult).then_inc(bias_negated, 1)
            def one_hots(i):
                pool.wait_ge(cur_ready, i + 1)
                for t in range(2 * GT):
                    if t % 4 == 0:
                        wait(pool, hot_used, i * (2 * GT) + t - 4)
                        nc.gpsimd.tensor_tensor(pscr[:, t // 4 % 2:t // 4 % 2 + 1], iota[:, 0:1], iota[:, 0:1], ALU.add)
                    nc.gpsimd.tensor_scalar(hot1[:, t % 8, :], iota, cur[:, 0, t:t + 1], None,
                                            ALU.is_equal).then_inc(hot1_ready, 1)

            one_hots(0)
            with pool.Fori(1, T // (2 * GT)) as i:
                one_hots(i)

        @block.scalar
        def _(act_e):
            a = nc.scalar

            def link(ins, n=[0]):
                n[0] += 1
                ins.then_inc(act_chain, 1)
                act_e.wait_ge(act_chain, n[0])

            act_e.dma_start(const[:, :], consts_in).then_inc(consts_in_sem, 16)
            act_e.dma_start(small[:, :], smalls_in).then_inc(consts_in_sem, 16)
            for k in range(KD):
                act_e.dma_start(xT[:, k, :], x_in[k]).then_inc(x_loaded, 16)
            act_e.dma_start(bias_sel, sel_in.rearrange("p (a b) -> p a b", a=NH)).then_inc(bias_loaded, 16)
            act_e.dma_start(bias_win, win_in.rearrange("p (a b) -> p a b", a=NH)).then_inc(bias_loaded, 16)
            act_e.dma_start(bias_cmp, cmp_in.rearrange("p (a b c) -> p a b c", a=NH, b=NT)).then_inc(bias_loaded, 16)

            def norm(idx, src, width, free=T):
                for k in range(NORMS[idx]):
                    n = norm_base[idx] + k
                    if n >= 2:
                        act_e.wait_ge(sq_summed, n - 1)
                    a.activation(sq[:, n % 2, 0:free], src(k), ACT.Square).then_inc(sq_ready, 1)
                act_e.wait_ge(sq_summed, norm_base[idx + 1])
                if idx:
                    act_e.wait_ge(normed, norm_base[idx])
                a.activation(rms[:, 0:free], bank[7][:, 0:free], ACT.Sqrt, bias=eps[:, 0:1],
                             scale=1.0 / width).then_inc(rms_ready, 1)

            def take(j, dst, func=ACT.Copy, scale=1.0, m=P, n=T, bias=0.0):
                act_e.wait_ge(proj_done, j + 1)
                return a.activation(dst, bank[j % 2][0:m, 0:n], func, scale=scale, bias=bias).then_inc(evac_act, 1)

            def softmax(u0, units, width, scols):
                for i in range(units + 1):
                    if i < units:
                        u = u0 + i
                        w = width(i)
                        act_e.wait_ge(logits_ready, u + 1)
                        if u >= 2:
                            act_e.wait_ge(prob_turned, u - 1)
                        a.activation(prob[:, u % 2, 0:w], logit[:, u % 2, 0:w], ACT.Exp, scale=-1.0,
                                     bias=least[:, i:i + 1], accum_out=total[:, i:i + 1]).then_inc(prob_ready, 1)
                    if i >= 1:
                        u = u0 + i - 1
                        w = scols(i - 1)
                        rows_ = NCMP if width(i - 1) == NCMP else P
                        act_e.wait_ge(prob_turned, u + 1)
                        if u >= 2:
                            act_e.wait_ge(pv_done, u - 1)
                        a.activation(probT[0:rows_, u % 2, 0:w], bank[2 + u % 2][0:rows_, 0:w],
                                     ACT.Copy).then_inc(probT_ready, 1)

            act_e.wait_ge(eps_set, 1)
            act_e.wait_ge(consts_in_sem, 32)
            act_e.wait_ge(x_loaded, 16 * KD)
            norm(0, lambda k: xT[:, k, :], D)
            j = first["qk"]
            for k in range(8):
                take(j + k, qk[:, k, :], scale=QS if k < 4 else 1.0)
            j = first["vtok"]
            for t in range(NT):
                take(j + t, vtok[:, t, :], n=408)
            act_e.wait_ge(evac_act, 12)
            a.activation(gsig, vtok[:, :, 384:408], ACT.Sigmoid).then_inc(gates_sig, 1)
            j = first["conv"]
            for k in range(12):
                take(j + k, conv[:, k, :])
            for kv in range(2):
                act_e.wait_ge(cmp_pe_ready, kv + 1)
                for g in range(2):
                    a.activation(hid[:, kv, g, 0:NCMP], bank[6 - g][:, kv * 128 + g * 32:kv * 128 + g * 32 + NCMP],
                                 ACT.Gelu_apprx_tanh, bias=pe_col[:, kv:kv + 1]).then_inc(cmp_gelu, 1)
            act_e.wait_ge(cmp_kv, 1)
            a.activation(kcmp[:, 0:NCMP], bank[2][:, 0:NCMP], ACT.Copy).then_inc(cmp_done, 1)
            a.activation(vcmp[0:NCMP, :], bank[2][0:NCMP, 128:256], ACT.Copy).then_inc(cmp_done, 1)
            softmax(0, 96, nsa_width, nsa_cols)
            for c in range(4):
                act_e.wait_ge(turned, c + 1)
                a.activation(nT[:, c, :], bank[2 + c % 2][:, :], ACT.Copy).then_inc(turned_out, 1)
            act_e.wait_ge(turned_out, 4)
            norm(1, lambda k: nT[:, k, :], 512)
            act_e.wait_ge(conv_ready, 4)
            norm(2, lambda k: conv[:, 3 * k, :], 512)
            j = first["w_out"]
            for k in range(8):
                take(j + k, yT[:, k, :])
            act_e.wait_ge(evac_act, taken(j + 7)[1])
            act_e.dma_start(memT, mem_in.rearrange("k p m -> p k m")).then_inc(mem_loaded, 16)
            norm(3, lambda k: yT[:, k, :], D)
            act_e.wait_ge(normed, norm_base[4])
            norm(4, lambda k: xT[:, k, :], D)
            act_e.wait_ge(mem_loaded, 16)
            norm(5, lambda k: memT[:, k, :], D, NM)
            for k in range(2):
                take(first["mq"] + k, mq[:, k, :], scale=QS)
            for k in range(2):
                take(first["mk"] + k, mk[:, k, :], n=NM)
            for k in range(2):
                take(first["mv"] + k, mv[:, k, :], n=NM)
            softmax(96, 16, lambda i: NM, lambda i: NM)
            for c in range(2):
                act_e.wait_ge(turned, 4 + c + 1)
                a.activation(omT[:, c, :], bank[2 + c % 2][:, :], ACT.Copy).then_inc(turned_out, 1)
            for k in range(8):
                take(first["mo"] + k, yT[:, k, :])
            act_e.wait_ge(evac_act, taken(first["mo"] + 7)[1])
            norm(6, lambda k: yT[:, k, :], D)
            act_e.wait_ge(normed, norm_base[7])
            norm(7, lambda k: xT[:, k, :], D)
            a.activation(condT[:, :], sm("cond", 0, 8), ACT.Silu).then_inc(cond_ready, 1)
            for m in range(KF):
                j = first["ffn"] + 2 * m
                act_e.wait_ge(proj_done, j + 1)
                if m >= 2:
                    act_e.wait_ge(evac_dve, m - 1)
                a.activation(ff_gate[:, m % 2, :], bank[j % 2][:, :], ACT.Silu).then_inc(evac_act, 1)
            for k in range(8):
                take(first["wd"] + k, yT[:, k, :])
            act_e.wait_ge(evac_act, taken(first["wd"] + 7)[1])
            act_e.dma_start(bias_band, band_in.rearrange("p (a b) -> p a b", a=NH)).then_inc(band_loaded, 16)
            norm(8, lambda k: yT[:, k, :], D)
            act_e.wait_ge(normed, norm_base[9])
            norm(9, lambda k: xT[:, k, :], D)
            for k in range(8):
                take(first["qk2"] + k, qk2[:, k, :], scale=QS if k < 4 else 1.0)
            for k in range(8):
                take(first["cv2"] + k, cv2[:, k, :])
            take(first["if"], row_i, ACT.Identity, m=BH, bias=sm("b_if", 0, 1, BH))
            take(first["if"] + 1, row_f, ACT.Identity, m=BH, bias=sm("b_if", 1, 1, BH))
            for k in range(4):
                take(first["og"] + k, sig_o[:, k, :], ACT.Sigmoid)
            for t in range(NT):
                take(first["va"] + t, va[:, t, :])
            act_e.wait_ge(ones_ready, 1)
            for t in range(NT):
                j = first["vb"] + t
                act_e.wait_ge(proj_done, j + 1)
                a.activation(vb[:, t, :, 0:P], bank[j % 2][:, :].rearrange("p (h d) -> p h d", h=BH),
                             ACT.Copy).then_inc(evac_act, 1)
            act_e.wait_ge(evac_act, taken(first["if"] + 1)[1])
            link(a.activation(row_a, row_f, ACT.Abs))
            link(a.activation(row_a, row_a, ACT.Exp, scale=-1.0))
            a.activation(row_a, row_a, ACT.Ln, bias=eps[0:BH, 1:2]).then_inc(rows_ln, 1)
            for k in range(8):
                act_e.wait_ge(conv2_acc, k + 1)
                a.activation(cv2[:, k, :], conv_acc[:, k % 2, :], ACT.Silu,
                             bias=sm("conv_b2", k)).then_inc(conv2_ready, 1)
            act_e.wait_ge(rows_m, 1)
            a.activation(row_f, row_f, ACT.Exp, scale=-1.0).then_inc(rows_exp, 1)
            softmax(112, 32, lambda i: P * (i // NH + 1), lambda i: P * (i // NH + 1))
            act_e.wait_ge(cols_done, 1)
            a.activation(tcol[:, 0:32], bank[6][:, 0:32], ACT.Copy).then_inc(cols_out, 1)
            act_e.wait_ge(cols_out, 1)
            def take_mrow(h):
                act_e.wait_ge(mrow_done, h + 1)
                if h >= 2:
                    act_e.wait_ge(diag_ready, (h - 1) * NT)
                a.activation(mrow[:, h % 2, :], bank[4 + h % 2][:, :], ACT.Copy).then_inc(mrow_out, 1)

            take_mrow(0)
            for i in range(BH * NT):
                h, s = divmod(i, NT)
                w = T - s * P
                if s == 0:
                    if h + 1 < BH:
                        take_mrow(h + 1)
                    act_e.wait_ge(mrow_out, h + 1)
                act_e.wait_ge(diag_ready, i + 1)
                if i >= 2:
                    act_e.wait_ge(lqk_ready, i - 1)
                b_s = tcol[:, s * BH + h:s * BH + h + 1]
                last = a.activation(wdec[:, i % 2, 0:P], wdiag[:, i % 2, :], ACT.Exp, scale=-1.0, bias=b_s)
                if w > P:
                    last = a.activation(wdec[:, i % 2, P:w], mrow[:, h % 2, (s + 1) * P:T], ACT.Exp,
                                        scale=-1.0, bias=b_s)
                last.then_inc(decay_ready, 1)
            for c in range(4):
                act_e.wait_ge(turned, 6 + c + 1)
                a.activation(yaT[:, c, :], bank[2 + c % 2][:, :], ACT.Copy).then_inc(turned_out, 1)
            act_e.wait_ge(hb_sq, 1)
            a.activation(den[:, 16:32], den[:, 0:16], ACT.Sqrt, bias=eps[:, 0:1], scale=1.0 / P).then_inc(hb_rms, 1)
            for m in range(KD):
                j = first["branch"] + 4 * m
                for g in range(2):
                    n = 2 * m + g
                    act_e.wait_ge(proj_done, j + 2 * g + 1)
                    if m >= 1:
                        act_e.wait_ge(y2_ready, m)
                    a.activation(gate_ab[:, g, :], bank[(j + 2 * g) % 2][:, :], ACT.Sigmoid).then_inc(evac_act, 1)
            act_e.wait_ge(evac_dve, taken(first["w_out2"] + 7)[1])
            norm(10, lambda k: xT[:, k, :], D)
            for k in range(16):
                take(first["pq"] + k, pq[:, k, :])
            for t in range(NT):
                for q in range(4):
                    act_e.wait_ge(score_done, 4 * t + q + 1)
                    if t:
                        act_e.wait_ge(best_ready, t)
                    a.activation(s_all[:, 4 * q:4 * q + 4, :], bank[q].rearrange("p (a b) -> p a b", a=4),
                                 ACT.Copy).then_inc(score_out, 1)
                act_e.wait_ge(best_ready, t + 1)
                a.activation(expd, expd, ACT.Exp).then_inc(best_exp, 1)
            def spread(i):
                for half in range(2):
                    for q in range(GT // 4):
                        n = half * (GT // 4) + q
                        act_e.wait_ge(hot_used, i * (2 * GT) + 4 * n + 4)
                        if q == 0:
                            wait(act_e, stored[half], i * 16)
                        for tk in range(4):
                            last = a.activation(
                                stage[:, half].rearrange("p b (t j) -> p b t j", t=GT)[:, :, 4 * q + tk, :],
                                bank[n % 4][:, tk * P:(tk + 1) * P].rearrange("p (b j) -> p b j", j=JB),
                                ACT.Copy)
                        last.then_inc(staged, 1)
                    act_e.wait_ge(staged, i * (2 * GT // 4) + (half + 1) * (GT // 4))
                    act_e.dma_start(
                        gates_dram.rearrange("b p t j -> p b (t j)")[
                            :, :, bass.ds(i * (2 * GT * JB) + half * GT * JB, GT * JB)],
                        stage[:, half]).then_inc(stored[half], 16)

            spread(0)
            with act_e.Fori(1, T // (2 * GT)) as i:
                spread(i)

            def gelu(b, i=0):
                for j in range(JB):
                    n = b * JB + j
                    act_e.wait_ge(up_done, i * (2 * JB) + n + 1)
                    wait(act_e, pact_ready, i * (2 * JB) + n - 1)
                    a.activation(act[:, j % 2, :], bank[j % 2][:, :], ACT.Gelu_apprx_tanh).then_inc(gelu_ready, 1)

            gelu(0)
            gelu(1)
            with act_e.Fori(0, NB // 2 - 1) as i:
                gelu(2, i)
                gelu(3, i)
            act_e.wait_ge(x3_ready, KD)
            norm(11, lambda k: xT[:, k, :], D)

        @block.vector
        def _(dve):
            v = nc.vector
            chain = [0]

            def link(ins):
                chain[0] += 1
                ins.then_inc(dve_chain, 1)
                dve.wait_ge(dve_chain, chain[0])

            v.memset(eps[:, 0:1], EPS).then_inc(dve_chain, 1)
            chain[0] += 1
            dve.wait_ge(dve_chain, 1)
            v.memset(eps[:, 1:2], 1.0).then_inc(eps_set, 1)
            dve.wait_ge(consts_in_sem, 32)

            def norm(idx, src, dst, gain, free=T, shift=None, add=False):
                dve.wait_ge(rms_ready, idx + 1)
                link(v.reciprocal(rstd[:, 0:free], rms[:, 0:free]))
                for k in range(NORMS[idx]):
                    one = v.scalar_tensor_tensor(out=src(k) if add else dst(k), in0=src(k), scalar=gain(k),
                                                 in1=rstd[:, 0:free], op0=ALU.mult, op1=ALU.mult)
                    if add:
                        link(one)
                        v.tensor_tensor(dst(k), dst(k), src(k), ALU.add).then_inc(normed, 1)
                    elif shift is not None:
                        link(one)
                        v.tensor_scalar(dst(k), dst(k), shift(k), None, ALU.add).then_inc(normed, 1)
                    else:
                        one.then_inc(normed, 1)

            def attend(u0, units, width, bias, gate, where, adds):
                for i in range(units + 2):
                    if i < units:
                        u, w = u0 + i, width(i)
                        dve.wait_ge(qk_done, u + 1)
                        if u >= 2:
                            dve.wait_ge(prob_ready, u - 1)
                        if bias is None:
                            v.tensor_scalar(logit[:, u % 2, 0:w], bank[u % 2][:, 0:w], 0.0, 3.0e38, ALU.add, ALU.min,
                                            accum_out=least[:, i:i + 1]).then_inc(logits_ready, 1)
                        else:
                            v.tensor_tensor_reduce(logit[:, u % 2, 0:w], bank[u % 2][:, 0:w], bias(i), 1.0, 3.0e38,
                                                   ALU.add, ALU.min, least[:, i:i + 1]).then_inc(logits_ready, 1)
                    if i >= 2:
                        n = i - 2
                        u = u0 + n
                        dve.wait_ge(pv_done, u + 1)
                        link(v.reciprocal(rrec[:, n:n + 1], total[:, n:n + 1]))
                        o = bank[4 + u % 2][:, 0:HD]
                        if gate is None:
                            v.tensor_scalar(where(n), o, rrec[:, n:n + 1], None, ALU.mult).then_inc(head_out, 1)
                            continue
                        link(v.tensor_tensor(rgate[:, n:n + 1], rrec[:, n:n + 1], gate(n), ALU.mult))
                        if adds(n):
                            dve.wait_ge(head_out, u - 31)
                            v.scalar_tensor_tensor(out=where(n), in0=o, scalar=rgate[:, n:n + 1], in1=where(n),
                                                   op0=ALU.mult, op1=ALU.add).then_inc(head_out, 1)
                        else:
                            v.tensor_scalar(where(n), o, rgate[:, n:n + 1], None, ALU.mult).then_inc(head_out, 1)

            norm(0, lambda k: xT[:, k, :], lambda k: hT[:, k, :], lambda k: sm("norm0", k))
            for j in range(4):
                cc, cx, cb = (conv[:, 3 * j + n, :] for n in range(3))
                y = conv_y[:, j % 2, :]
                sem_, val = taken(first["conv"] + 3 * j + 2)
                dve.wait_ge(sem_, val)
                link(v.tensor_tensor(cx, cc, cx, ALU.mult))
                link(v.tensor_scalar(y, cx, sm("conv_w", j), None, ALU.mult))
                for k in range(1, 3):
                    link(v.scalar_tensor_tensor(out=y[:, k:T], in0=cx[:, 0:T - k], scalar=sm("conv_w", 4 * k + j),
                                                in1=y[:, k:T], op0=ALU.mult, op1=ALU.add))
                v.tensor_tensor(cc, cb, y, ALU.mult).then_inc(conv_ready, 1)
            dve.wait_ge(gates_sig, 1)
            link(v.tensor_scalar(gsig[:, 0, 0:24:3], gsig[:, 0, 0:24:3], rowmask, None, ALU.mult))
            for kv in range(2):
                dve.wait_ge(cmp_hidden, kv + 1)
                v.tensor_copy(pe_col[:, kv:kv + 1], bank[6][:, kv * 128 + 64:kv * 128 + 65]).then_inc(cmp_pe_ready, 1)
            dve.wait_ge(bias_negated, 3)

            def nsa_bias(i):
                br, t, h = nsa_unit(i)
                if br == 0:
                    return bias_sel[:, h, 384 - P * t:T]
                if br == 1:
                    return bias_win[:, h, max(256 - P * t, 0):384]
                return bias_cmp[:, h, t, 0:NCMP]

            def nsa_gate(i):
                br, t, h = nsa_unit(i)
                c = 3 * h + (1, 2, 0)[br]
                return gsig[:, t, c:c + 1]

            def nsa_where(i):
                br, t, h = nsa_unit(i)
                return o_tok[:, t, h * HD:(h + 1) * HD]

            attend(0, 96, nsa_width, nsa_bias, nsa_gate, nsa_where, lambda i: nsa_unit(i)[0] > 0)
            norm(1, lambda k: nT[:, k, :], lambda k: merged[:, k, :], lambda k: sm("gn_nsa", k))
            norm(2, lambda k: conv[:, 3 * k, :], lambda k: merged[:, 4 + k, :], lambda k: sm("gn_conv", k))
            norm(3, lambda k: yT[:, k, :], lambda k: xT[:, k, :], lambda k: sm("norm1", k), add=True)
            norm(4, lambda k: xT[:, k, :], lambda k: hT[:, k, :], lambda k: sm("norm2", k))
            norm(5, lambda k: memT[:, k, :], lambda k: mT[:, k, :], lambda k: sm("mem_norm", k), NM)
            attend(96, 16, lambda i: NM, None, None,
                   lambda i: om_tok[:, i // MH, (i % MH) * HD:(i % MH + 1) * HD], None)
            norm(6, lambda k: yT[:, k, :], lambda k: xT[:, k, :], lambda k: sm("norm3", k), add=True)
            norm(7, lambda k: xT[:, k, :], lambda k: hT[:, k, :], lambda k: sm("norm4", k))
            for m in range(KF):
                j = first["ffn"] + 2 * m + 1
                dve.wait_ge(evac_act, taken(j - 1)[1])
                dve.wait_ge(proj_done, j + 1)
                v.tensor_tensor(ff[:, m, :], bank[j % 2][:, :], ff_gate[:, m % 2, :], ALU.mult).then_inc(evac_dve, 1)
            dve.wait_ge(ada_done, 1)
            link(v.tensor_tensor(mod[:, :], bank[6][:, 0:48], sm("b_ada", 0, 48), ALU.add))
            link(v.scalar_tensor_tensor(out=gmod[:, 0:8], in0=mod[:, 8:16], scalar=1.0, in1=sm("norm1_2", 0, 8),
                                        op0=ALU.add, op1=ALU.mult))
            link(v.scalar_tensor_tensor(out=gmod[:, 8:16], in0=mod[:, 32:40], scalar=1.0, in1=sm("norm2_2", 0, 8),
                                        op0=ALU.add, op1=ALU.mult))
            norm(8, lambda k: yT[:, k, :], lambda k: xT[:, k, :], lambda k: sm("norm5", k), add=True)
            norm(9, lambda k: xT[:, k, :], lambda k: hT[:, k, :], lambda k: gmod[:, k:k + 1],
                 shift=lambda k: mod[:, k:k + 1])
            v.memset(vb[:, :, :, P:P + 1], 1.0).then_inc(ones_ready, 1)
            for k in range(8):
                sem_, val = taken(first["cv2"] + k)
                dve.wait_ge(sem_, val)
                if k >= 2:
                    dve.wait_ge(conv2_ready, k - 1)
                y, u = conv_acc[:, k % 2, :], cv2[:, k, :]
                link(v.tensor_scalar(y, u, sm("conv_w2", 24 + k), None, ALU.mult))
                for d in range(1, 4):
                    one = v.scalar_tensor_tensor(out=y[:, d:T], in0=u[:, 0:T - d],
                                                 scalar=sm("conv_w2", 8 * (3 - d) + k), in1=y[:, d:T],
                                                 op0=ALU.mult, op1=ALU.add)
                    if d < 3:
                        link(one)
                    else:
                        one.then_inc(conv2_acc, 1)
            dve.wait_ge(rows_ln, 1)
            link(v.scalar_tensor_tensor(out=row_b, in0=row_f, scalar=0.0, in1=row_a, op0=ALU.min, op1=ALU.subtract))
            link(v.memset(row_f, 0.0))
            link(v.tensor_tensor_scan(row_a, row_b, row_f, 0.0, ALU.add, ALU.add))
            link(v.tensor_tensor(row_b, row_i, row_a, ALU.subtract))
            link(v.tensor_tensor_scan(row_i, row_b, row_b, 0.0, ALU.max, ALU.max))
            v.tensor_tensor(row_f, row_a, row_i, ALU.add).then_inc(rows_m, 1)
            dve.wait_ge(bias_negated, 4)
            attend(112, 32, lambda i: P * (i // NH + 1), lambda i: bias_band[:, i % NH, 384 - P * (i // NH):T],
                   None, lambda i: oa_tok[:, i // NH, (i % NH) * HD:(i % NH + 1) * HD], None)
            dve.wait_ge(cols_out, 1)
            scale = P ** -0.5
            for i in range(BH * NT + 1):
                if i < BH * NT:
                    h, s = divmod(i, NT)
                    w = T - s * P
                    dve.wait_ge(mrow_out, h + 1)
                    if i >= 2:
                        dve.wait_ge(decay_ready, i - 1)
                    v.tensor_tensor(wdiag[:, i % 2, :], mrow[:, h % 2, s * P:(s + 1) * P],
                                    const[:, C_TRI:C_TRI + P], ALU.add).then_inc(diag_ready, 1)
                if i >= 1:
                    n = i - 1
                    h, s = divmod(n, NT)
                    w = T - s * P
                    dve.wait_ge(decay_ready, n + 1)
                    dve.wait_ge(lqk_done, n + 1)
                    if h >= 2:
                        dve.wait_ge(lpv_done, h - 1)
                    v.scalar_tensor_tensor(out=wqk[:, h % 2, s, 0:w], in0=bank[n % 2][:, 0:w], scalar=scale,
                                           in1=wdec[:, n % 2, 0:w], op0=ALU.mult, op1=ALU.mult).then_inc(lqk_ready, 1)
                if i >= 1 and (i - 1) % NT == NT - 1:
                    h = (i - 1) // NT
                    dve.wait_ge(lpv_done, h + 1)
                    for t in range(NT):
                        o = bank[2 + t // 2][:, (t % 2) * 256:(t % 2) * 256 + P + 1]
                        d = den[:, 32 + t * BH + h:33 + t * BH + h]
                        link(v.tensor_scalar(d, o[:, P:P + 1], -1.0, tcol[:, 16 + t * BH + h:17 + t * BH + h],
                                             ALU.mult, ALU.max))
                        link(v.tensor_tensor(d, o[:, P:P + 1], d, ALU.max))
                        link(v.reciprocal(d, d))
                        v.tensor_scalar(hb_tok[:, t, h * P:(h + 1) * P], o[:, 0:P], d, None,
                                        ALU.mult).then_inc(lnum_out, 1)
            dve.wait_ge(turned, 10)
            dve.wait_ge(lnum_out, BH * NT)
            link(v.tensor_tensor(hsq, hb_tok, hb_tok, ALU.mult))
            v.tensor_reduce(den[:, 0:16], hsq.rearrange("p t (h d) -> p (t h) d", h=BH), AX.X, ALU.add).then_inc(hb_sq, 1)
            dve.wait_ge(hb_rms, 1)
            link(v.reciprocal(den[:, 0:16], den[:, 16:32]))
            for n in range(16):
                t, h = divmod(n, BH)
                o = hb_tok[:, t, h * P:(h + 1) * P]
                v.tensor_scalar(o, o, den[:, n:n + 1], None, ALU.mult).then_inc(hb_ready, 1)
            for c in range(4):
                dve.wait_ge(turned, 10 + c + 1)
                v.scalar_tensor_tensor(out=ybT[:, c, :], in0=bank[2 + c % 2][:, :], scalar=sm("mlstm_g", c),
                                       in1=sig_o[:, c, :], op0=ALU.mult, op1=ALU.mult).then_inc(yb_out, 1)
            for m in range(KD):
                j = first["branch"] + 4 * m
                for g in range(2):
                    dve.wait_ge(evac_act, taken(j + 2 * g)[1])
                    dve.wait_ge(proj_done, j + 2 * g + 2)
                    v.tensor_tensor(gate_ab[:, 2 + g, :], bank[(j + 2 * g + 1) % 2][:, :], gate_ab[:, g, :],
                                    ALU.mult).then_inc(evac_dve, 1)
                dve.wait_ge(evac_dve, taken(j + 3)[1])
                v.tensor_tensor(y2T[:, m, :], gate_ab[:, 2, :], gate_ab[:, 3, :], ALU.add).then_inc(y2_ready, 1)
            for k in range(8):
                j = first["w_out2"] + k
                dve.wait_ge(proj_done, j + 1)
                v.scalar_tensor_tensor(out=xT[:, k, :], in0=bank[j % 2][:, :], scalar=mod[:, 16 + k:17 + k],
                                       in1=xT[:, k, :], op0=ALU.mult, op1=ALU.add).then_inc(evac_dve, 1)
            dve.wait_ge(evac_dve, taken(first["w_out2"] + 7)[1])
            norm(10, lambda k: xT[:, k, :], lambda k: hT[:, k, :], lambda k: gmod[:, 8 + k:9 + k],
                 shift=lambda k: mod[:, 24 + k:25 + k])

            def each(n, op):
                for g in range(n):
                    one = op(g)
                link(one)

            for t in range(NT):
                dve.wait_ge(score_out, 4 * t + 4)
                each(16, lambda g: v.max(s_top[:, g, 0:8], s_all[:, g, :]))
                each(16, lambda g: v.max_index(i_top[:, g, 0:8], s_top[:, g, 0:8], s_all[:, g, :]))
                each(16, lambda g: v.match_replace(s_left[:, g, :], s_top[:, g, 0:8], s_all[:, g, :], -3.0e38))
                each(16, lambda g: v.max(s_top[:, g, 8:16], s_left[:, g, :]))
                each(16, lambda g: v.max_index(i_top[:, g, 8:16], s_top[:, g, 8:16], s_left[:, g, :]))
                tops = s_top.rearrange("p (h b) k -> p h b k", b=2)
                shape = [P, PH, TOPK, TOPK]
                for h in range(PH):
                    one = v.tensor_tensor(cand[:, h], tops[:, h, 0, :].unsqueeze(2).to_broadcast([P, TOPK, TOPK]),
                                          tops[:, h, 1, :].unsqueeze(1).to_broadcast([P, TOPK, TOPK]), ALU.add)
                link(one)
                flat = lambda c, h: c[:, h].rearrange("p a b -> p (a b)")
                each(PH, lambda h: v.max(best[:, h, 0:8], flat(cand, h)))
                each(PH, lambda h: v.max_index(c_top[:, h, 0:8], best[:, h, 0:8], flat(cand, h)))
                each(PH, lambda h: v.match_replace(flat(cand_left, h), best[:, h, 0:8], flat(cand, h), -3.0e38))
                each(PH, lambda h: v.max(best[:, h, 8:16], flat(cand_left, h)))
                each(PH, lambda h: v.max_index(c_top[:, h, 8:16], best[:, h, 8:16], flat(cand_left, h)))
                if t:
                    dve.wait_ge(best_exp, t)
                v.tensor_tensor(expd, best, best[:, :, 0:1].to_broadcast([P, PH, TOPK]), ALU.subtract).then_inc(best_ready, 1)
                v.tensor_scalar(c_hi, c_top, 4, None, ALU.logical_shift_right)
                link(v.tensor_scalar(c_lo, c_top, 15, None, ALU.bitwise_and))
                v.tensor_copy(a_f, c_hi)
                v.tensor_copy(b_f, c_lo)
                link(v.tensor_copy(i_topf, i_top))
                if t:
                    dve.wait_ge(chosen_turned, t)
                for half, rank in ((0, a_f), (1, b_f)):
                    for h in range(PH):
                        one = v.tensor_tensor(eqs[:, h], rank[:, h, :].unsqueeze(2).to_broadcast([P, TOPK, TOPK]),
                                              iota[:, 0:TOPK].unsqueeze(1).to_broadcast([P, TOPK, TOPK]), ALU.is_equal)
                    link(one)
                    for h in range(PH):
                        one = v.tensor_tensor(eqs[:, h], eqs[:, h],
                                              i_topf[:, 2 * h + half, :].unsqueeze(1).to_broadcast([P, TOPK, TOPK]),
                                              ALU.mult)
                    link(one)
                    link(v.tensor_reduce(chosen[:, half, :], eqs.rearrange("p h k a -> p (h k) a"), AX.X, ALU.add))
                dve.wait_ge(best_exp, t + 1)
                link(v.tensor_reduce(gsum[:, 0:8], expd, AX.X, ALU.add))
                link(v.reciprocal(gsum[:, 8:16], gsum[:, 0:8]))
                v.tensor_tensor(chosen[:, 2, :].rearrange("p (h k) -> p h k", h=PH), expd,
                                gsum[:, 8:16].unsqueeze(2).to_broadcast([P, PH, TOPK]), ALU.mult).then_inc(chosen_ready, 1)
                dve.wait_ge(chosen_turned, t + 1)
                v.tensor_copy(chosenT[:, :, t * P:(t + 1) * P],
                              bank[4 + t % 2][:, 0:3 * P].rearrange("p (a b) -> p a b", a=3)).then_inc(chosen_out, 1)
            dve.wait_ge(chosen_out, NT)
            def one_hots(i):
                wait(dve, hot1_ready, i * (2 * GT))
                wait(dve, hot2_ready, i * (2 * GT))
                v.tensor_copy(cur, chosenT[:, :, bass.ds(i * (2 * GT), 2 * GT)]).then_inc(cur_ready, 1)
                dve.wait_ge(cur_ready, i + 1)
                for t in range(2 * GT):
                    wait(dve, hot_used, i * (2 * GT) + t - 7)
                    v.tensor_scalar(hot2[:, t % 8, :], iota, cur[:, 1, t:t + 1], cur[:, 2, t:t + 1],
                                    ALU.is_equal, ALU.mult).then_inc(hot2_ready, 1)

            one_hots(0)
            with dve.Fori(1, T // (2 * GT)) as i:
                one_hots(i)

            def weigh(b, j, i=0):
                if j == 0:
                    dve.wait_ge(g_loaded[b % 2], i * 16 + 16 * (b // 2 + 1))
                    wait(dve, down_done, i * (2 * KD) + (b - 1) * KD)
                dve.wait_ge(gelu_ready, i * (2 * JB) + b * JB + j + 1)
                v.tensor_tensor(pact[:, b % 2, j, :], act[:, j % 2, :], gblk[:, b % 2, :, j],
                                ALU.mult).then_inc(pact_ready, 1)

            def gather(b, k, i=0):
                dve.wait_ge(down_done, i * (2 * KD) + b * KD + k + 1)
                v.tensor_tensor(acc[:, k, :], acc[:, k, :], bank[2 + k % 2][:, :], ALU.add).then_inc(down_out, 1)

            dve.wait_ge(hot_used, T)
            dve.wait_ge(staged, T // 4)
            for s in range(2):
                dve.wait_ge(stored[s], 16 * (T // GT // 2))
            link(v.memset(acc, 0.0))
            for j in range(JB):
                weigh(0, j)
            for j in range(JB):
                weigh(1, j)
                gather(0, j)
            with dve.Fori(0, NB // 2 - 1) as i:
                for b in (2, 3):
                    for j in range(JB):
                        weigh(b, j, i)
                        gather(b - 1, j, i)
            for j in range(JB):
                gather(NB - 1, j)
            dve.wait_ge(down_out, NB * KD)
            for k in range(KD):
                v.scalar_tensor_tensor(out=xT[:, k, :], in0=acc[:, k, :], scalar=mod[:, 40 + k:41 + k],
                                       in1=xT[:, k, :], op0=ALU.mult, op1=ALU.add).then_inc(x3_ready, 1)
            dve.wait_ge(x3_ready, KD)
            norm(11, lambda k: xT[:, k, :], lambda k: hT[:, k, :], lambda k: sm("final_g", k))

        @block.tensor
        def _(pe):
            mm = nc.tensor.matmul
            tile = [0]
            job = [0]
            held = [0]

            def weight():
                n = tile[0]
                tile[0] += 1
                pe.wait_ge(tile_loaded[n % RING], 16 * (n // RING + 1))
                return ring[:, n % RING, :]

            def norm(idx, free=T):
                for k in range(NORMS[idx]):
                    n = norm_base[idx] + k
                    pe.wait_ge(sq_ready, n + 1)
                    if k == 0 and idx:
                        pe.wait_ge(rms_ready, idx)
                    mm(bank[7][:, 0:free], ones, sq[:, n % 2, 0:free], start=(k == 0),
                       stop=(k == NORMS[idx] - 1)).then_inc(sq_summed, 1)

            def project(chunks, m=P, n=T, used=1, ready=None):
                j = job[0]
                job[0] += 1
                if j >= 2:
                    s, value = taken(j - 2)
                    pe.wait_ge(s, value)
                for k, (lhsT, rhs) in enumerate(chunks):
                    if ready:
                        ready(k)
                    last = mm(bank[j % 2][0:m, 0:n], lhsT, rhs, start=(k == 0), stop=(k == len(chunks) - 1))
                    if k == 0:
                        release_held(last)
                last.then_inc(proj_done, 1)
                if used:
                    release(used)

            def release(n):
                held[0] += n

            def release_held(ins):
                if held[0]:
                    ins.then_inc(tiles_used, held[0])
                held[0] = 0

            def after_norm(idx):
                return lambda k: pe.wait_ge(normed, norm_base[idx] + k + 1)

            def dense(count, src, kd=KD, ready=None, n=T):
                for m in range(count):
                    w = weight()
                    project([(w[:, k * P:(k + 1) * P], src[:, k, :]) for k in range(kd)], n=n,
                            ready=ready if m == 0 else None)

            def token_major(src, n, tiles=NT, per=2):
                width = D // per
                w = [weight() for _ in range(KD // per)]
                for t in range(tiles):
                    project([(src[:, k, t * P:(t + 1) * P], w[k // per][:, (k % per) * width:(k % per) * width + n])
                             for k in range(KD)], n=n, used=0 if t < tiles - 1 else KD // per)

            def attend(u0, units, q, k, width, pieces, vals):
                for i in range(units + 2):
                    if i < units:
                        u = u0 + i
                        if u >= 2:
                            pe.wait_ge(logits_ready, u - 1)
                        mm(bank[u % 2][:, 0:width(i)], q(i), k(i), start=True, stop=True).then_inc(qk_done, 1)
                    if 1 <= i <= units:
                        n, u = i - 1, u0 + i - 1
                        pe.wait_ge(prob_ready, u + 1)
                        if u >= 2:
                            pe.wait_ge(probT_ready, u - 1)
                        for c, w in enumerate(pieces(n)):
                            last = nc.tensor.transpose(bank[2 + u % 2][0:w, c * P:(c + 1) * P],
                                                       prob[:, u % 2, c * P:c * P + w], ident)
                        last.then_inc(prob_turned, 1)
                    if i >= 2:
                        n, u = i - 2, u0 + i - 2
                        pe.wait_ge(probT_ready, u + 1)
                        if u >= 2:
                            pe.wait_ge(head_out, u - 1)
                        parts = pieces(n)
                        for c, w in enumerate(parts):
                            last = mm(bank[4 + u % 2][:, 0:HD], probT[0:w, u % 2, c * P:(c + 1) * P], vals(n, c),
                                      start=(c == 0), stop=(c == len(parts) - 1))
                        last.then_inc(pv_done, 1)

            def turn_chosen(t):
                pe.wait_ge(chosen_ready, t + 1)
                wait(pe, chosen_out, t - 1)
                for n in range(3):
                    last = nc.tensor.transpose(bank[4 + t % 2][:, n * P:(n + 1) * P], chosen[:, n, :], ident)
                last.then_inc(chosen_turned, 1)

            def turn(n0, count, src, out_sem=None):
                for c in range(count):
                    if out_sem is not None:
                        wait(pe, out_sem, c - 1)
                    elif n0 + c >= 2:
                        pe.wait_ge(turned_out, n0 + c - 1)
                    for t in range(NT):
                        last = nc.tensor.transpose(bank[2 + c % 2][:, t * P:(t + 1) * P],
                                                   src[:, t, c * P:(c + 1) * P], ident)
                    last.then_inc(turned, 1)

            pe.wait_ge(consts_in_sem, 32)
            norm(0)
            dense(8, hT, ready=after_norm(0))
            token_major(hT, 408)
            dense(12, hT)
            s_, val = taken(first["qk"] + 5)
            pe.wait_ge(s_, val)
            for kv in range(2):
                w = [weight() for _ in range(4)]
                for g in range(2):
                    rows_ = slice(g * HD, (g + 1) * HD)
                    for j in range(32):
                        w1 = w[j // 8][rows_, (j % 8) * P:(j % 8 + 1) * P]
                        one = mm(bank[6 - g][:, kv * 128 + g * 32:kv * 128 + g * 32 + NCMP], w1,
                                 qk[rows_, 4 + kv, j:j + 16 * (NCMP - 1) + 1:16], start=(j == 0), stop=(j == 31))
                        release_held(one)
                for j in range(32):
                    w1 = w[j // 8][0:HD, (j % 8) * P:(j % 8 + 1) * P]
                    last = mm(bank[6][:, kv * 128 + 64:kv * 128 + 65], w1, small[0:HD, SMALL["pe"][0] + j:SMALL["pe"][0] + j + 1],
                              start=(j == 0), stop=(j == 31))
                last.then_inc(cmp_hidden, 1)
                release(4)
                pe.wait_ge(cmp_gelu, 2 * kv + 2)
            for g in range(2):
                mm(bank[2][:, 0:NCMP], sm("w2k", g * P, P), hid[:, 0, g, 0:NCMP], start=(g == 0), stop=(g == 1))
            for g in range(2):
                last = mm(bank[2][0:NCMP, 128 + g * HD:128 + (g + 1) * HD], hid[:, 1, g, 0:NCMP], sm("w2v", 0, HD),
                          start=True, stop=True)
            last.then_inc(cmp_kv, 1)

            def nsa_q(i):
                br, t, h = nsa_unit(i)
                g = h // 4
                return qk[g * HD:(g + 1) * HD, h % 4, t * P:(t + 1) * P]

            def nsa_k(i):
                br, t, h = nsa_unit(i)
                g = h // 4
                if br == 2:
                    return kcmp[g * HD:(g + 1) * HD, 0:NCMP]
                lo = 0 if br == 0 else max(t - 2, 0)
                return qk[g * HD:(g + 1) * HD, 6 + br, lo * P:(t + 1) * P]

            def nsa_v(i, c):
                br, t, h = nsa_unit(i)
                g = h // 4
                if br == 2:
                    return vcmp[0:NCMP, g * HD:(g + 1) * HD]
                lo = 0 if br == 0 else max(t - 2, 0)
                a0 = (0, 256)[br] + g * HD
                return vtok[:, lo + c, a0:a0 + HD]

            for s_, val in (taken(first["conv"] - 1), taken(first["conv"] + 11)):
                pe.wait_ge(s_, val)
            pe.wait_ge(cmp_done, 2)
            attend(0, 96, nsa_q, nsa_k, nsa_width, nsa_pieces, nsa_v)
            pe.wait_ge(head_out, 96)
            turn(0, 4, o_tok)
            norm(1)
            norm(2)
            for m in range(8):
                w = weight()
                project([(w[:, k * P:(k + 1) * P], merged[:, k, :]) for k in range(8)],
                        ready=(lambda k: pe.wait_ge(normed, norm_base[1] + k + 1)) if m == 0 else None)
            norm(3)
            norm(4)
            norm(5, NM)
            dense(2, hT, ready=after_norm(4))
            dense(2, mT, ready=after_norm(5), n=NM)
            token_major(mT, NM, tiles=2, per=4)
            s_, val = taken(first["mv"] + 1)
            pe.wait_ge(s_, val)
            attend(96, 16, lambda i: mq[(i % 2) * HD:(i % 2 + 1) * HD, (i % MH) // 2, (i // MH) * P:(i // MH + 1) * P],
                   lambda i: mk[(i % 2) * HD:(i % 2 + 1) * HD, (i % MH) // 2, :], lambda i: NM,
                   lambda i: [P, P], lambda i, c: mv[:, c, (i % MH) * HD:(i % MH + 1) * HD])
            pe.wait_ge(head_out, 96 + 16)
            turn(4, 2, om_tok)
            pe.wait_ge(turned_out, 6)
            for half in range(2):
                w = weight()
                for m in range(4):
                    project([(w[:, m * 256 + k * P:m * 256 + (k + 1) * P], omT[:, k, :]) for k in range(2)],
                            used=1 if m == 3 else 0)
            norm(6)
            norm(7)
            pe.wait_ge(cond_ready, 1)

            def ada(m):
                w = weight()
                for k in range(KD):
                    last = mm(bank[6][:, m:m + 1], w[:, k * P:(k + 1) * P], condT[:, k:k + 1],
                              start=(k == 0), stop=(k == KD - 1))
                    if k == 0:
                        release_held(last)
                release(1)
                return last

            for m in range(KF):
                for _ in range(2):
                    w = weight()
                    project([(w[:, k * P:(k + 1) * P], hT[:, k, :]) for k in range(KD)],
                            ready=after_norm(7) if m == 0 and _ == 0 else None)
                ada(2 * m)
                ada(2 * m + 1)
            for m in range(2 * KF, 48):
                last = ada(m)
            last.then_inc(ada_done, 1)
            s_, val = taken(first["ffn"] + 2 * KF - 1)
            pe.wait_ge(s_, val)
            for m in range(8):
                w = [weight() for _ in range(3)]
                project([(w[k // 8][:, (k % 8) * P:(k % 8 + 1) * P], ff[:, k, :]) for k in range(KF)], used=3)
            norm(8)
            norm(9)
            dense(8, hT, ready=after_norm(9))
            dense(8, hT)
            w = weight()
            for n in range(2):
                project([(w[:, k * P + BH * n:k * P + BH * (n + 1)], hT[:, k, :]) for k in range(KD)], m=BH, used=n)
            dense(4, hT)
            token_major(hT, T)
            token_major(hT, T)
            pe.wait_ge(rows_m, 1)
            pe.wait_ge(rows_exp, 1)
            for src, c0 in ((row_b, 0), (row_f, 16)):
                for t in range(NT):
                    last = nc.tensor.transpose(bank[6][:, c0 + t * BH:c0 + (t + 1) * BH],
                                               src[:, t * P:(t + 1) * P], const[0:BH, C_ID:C_ID + BH])
            last.then_inc(cols_done, 1)
            s_, val = taken(first["vb"] + 3)
            pe.wait_ge(s_, val)
            attend(112, 32, lambda i: qk2[(i % 2) * HD:(i % 2 + 1) * HD, (i % NH) // 2, (i // NH) * P:(i // NH + 1) * P],
                   lambda i: qk2[(i % 2) * HD:(i % 2 + 1) * HD, 4 + (i % NH) // 2, 0:(i // NH + 1) * P],
                   lambda i: P * (i // NH + 1), lambda i: [P] * (i // NH + 1),
                   lambda i, c: va[:, c, (i % NH) * HD:(i % NH + 1) * HD])
            pe.wait_ge(head_out, UNITS)
            pe.wait_ge(conv2_ready, 8)
            def m_row(h):
                wait(pe, mrow_out, h - 1)
                mm(bank[4 + h % 2][:, :], const[0:BH, C_SEL + h * P:C_SEL + (h + 1) * P], row_i,
                   start=True, stop=True).then_inc(mrow_done, 1)

            m_row(0)
            for h in range(BH):
                if h + 1 < BH:
                    m_row(h + 1)
                for s in range(NT):
                    n = h * NT + s
                    if n >= 2:
                        pe.wait_ge(lqk_ready, n - 1)
                    mm(bank[n % 2][:, 0:T - s * P], cv2[:, 4 + h, s * P:(s + 1) * P], cv2[:, h, s * P:T],
                       start=True, stop=True).then_inc(lqk_done, 1)
                pe.wait_ge(lqk_ready, (h + 1) * NT)
                if h:
                    pe.wait_ge(lnum_out, h * NT)
                for t in range(NT):
                    for s in range(t + 1):
                        last = mm(bank[2 + t // 2][:, (t % 2) * 256:(t % 2) * 256 + P + 1],
                                  wqk[:, h % 2, s, (t - s) * P:(t - s + 1) * P], vb[:, s, h, :],
                                  start=(s == 0), stop=(s == t))
                last.then_inc(lpv_done, 1)
            pe.wait_ge(lnum_out, BH * NT)
            turn(6, 4, oa_tok)
            pe.wait_ge(hb_ready, 16)
            pe.wait_ge(turned_out, 10)
            turn(10, 4, hb_tok, yb_out)
            pe.wait_ge(yb_out, 4)
            for m in range(KD):
                wa, wb, wab = weight(), weight(), weight()
                project([(wa[:, k * P:(k + 1) * P], hT[:, k, :]) for k in range(KD)], used=0)
                project([(wab[:, k * P:(k + 1) * P], yaT[:, k, :]) for k in range(4)], used=0)
                project([(wb[:, k * P:(k + 1) * P], hT[:, k, :]) for k in range(KD)], used=0)
                project([(wab[:, (4 + k) * P:(5 + k) * P], ybT[:, k, :]) for k in range(4)], used=3)
            pe.wait_ge(y2_ready, KD)
            dense(8, y2T)
            norm(10)
            dense(16, hT, ready=after_norm(10))
            keys = [weight(), weight()]
            s_, val = taken(first["pq"] + 15)
            pe.wait_ge(s_, val)
            for t in range(NT):
                for q in range(4):
                    if t:
                        pe.wait_ge(score_out, 4 * (t - 1) + q + 1)
                    for j in range(4 * q, 4 * q + 4):
                        last = mm(bank[q][:, (j % 4) * P:(j % 4 + 1) * P], pq[:, j, t * P:(t + 1) * P],
                                  keys[j // 8][:, (j % 8) * P:(j % 8 + 1) * P], start=True, stop=True)
                    last.then_inc(score_done, 1)
                if t == NT - 1:
                    release(2)
                if t:
                    turn_chosen(t - 1)
            turn_chosen(NT - 1)
            pe.wait_ge(score_out, 4 * NT)

            def spread(i):
                for t in range(2 * GT):
                    n = t // 4
                    pe.wait_ge(hot1_ready, i * (2 * GT) + t + 1)
                    pe.wait_ge(hot2_ready, i * (2 * GT) + t + 1)
                    if t % 4 == 0:
                        wait(pe, staged, i * (2 * GT // 4) + n - 3)
                    mm(bank[n % 4][:, (t % 4) * P:(t % 4 + 1) * P], hot1[:, t % 8, :], hot2[:, t % 8, :],
                       start=True, stop=True).then_inc(hot_used, 1)

            spread(0)
            with pe.Fori(1, T // (2 * GT)) as i:
                spread(i)
            pe.wait_ge(staged, T // 4)

            def stream_tile(n, i):
                pe.wait_ge(tile_loaded[n % RING], i * (16 * 4 * JB // RING) + 16 * (n // RING + 1))
                return ring[:, n % RING, :]

            def up(b, j, i=0):
                w = stream_tile(BEFORE + j if b == 0 else BEFORE + JB + 2 * JB * (b - 1) + 2 * j, i)
                wait(pe, gelu_ready, i * (2 * JB) + b * JB + j - 1)
                for k in range(KD):
                    last = mm(bank[j % 2][:, :], w[:, k * P:(k + 1) * P], hT[:, k, :], start=(k == 0),
                              stop=(k == KD - 1))
                    if k == 0:
                        release_held(last)
                last.then_inc(up_done, 1)
                release(1)

            def down(b, k, i=0, last_block=False):
                first_ = n_tiles - JB if last_block else BEFORE + 2 * JB + 2 * JB * b - JB + 1
                w = stream_tile(first_ + (k if last_block else 2 * k), i)
                if k == 0:
                    pe.wait_ge(pact_ready, i * (2 * JB) + (b + 1) * JB)
                wait(pe, down_out, i * (2 * KD) + b * KD + k - 1)
                for j in range(JB):
                    last = mm(bank[2 + k % 2][:, :], w[:, j * P:(j + 1) * P], pact[:, b % 2, j, :],
                              start=(j == 0), stop=(j == JB - 1))
                    if j == 0:
                        release_held(last)
                last.then_inc(down_done, 1)
                release(1)

            for j in range(JB):
                up(0, j)
            for j in range(JB):
                up(1, j)
                down(0, j)
            with pe.Fori(0, NB // 2 - 1) as i:
                for b in (2, 3):
                    for j in range(JB):
                        up(b, j, i)
                        down(b - 1, j, i)
            for k in range(KD):
                down(NB - 1, k, last_block=True)
            norm(11)


def kernel(**inputs):
    import numpy as _np
    import concourse.bacc as _bacc
    from concourse import mybir as _mybir
    from concourse.bass_utils import run_bass_kernel_spmd as _run

    i = {k: _np.asarray(v) for k, v in inputs.items()}
    sel, win, cmp, band = biases(i)
    arrays = {
        "weights": weight_stream(i),
        "x_t": i["x"][0].T.reshape(KD, P, T),
        "mem_t": i["mem"][0].T.reshape(KD, P, NM),
        "smalls": smalls(i), "consts": constants(),
        "bias_sel": sel, "bias_win": win, "bias_cmp": cmp, "bias_band": band,
    }
    arrays = {k: _np.ascontiguousarray(v) for k, v in arrays.items()}
    nc = _bacc.Bacc("TRN2", target_bir_lowering=False, num_devices=1)
    args = [nc.dram_tensor(k, v.shape, _mybir.dt.from_np(v.dtype), kind="ExternalInput").ap()
            for k, v in arrays.items()]
    result = nc.dram_tensor("out_t", (KD, P, T), _mybir.dt.float32, kind="ExternalOutput").ap()
    build(nc, *args, result)
    r = _run(nc, [arrays], core_ids=[0])
    got = r.results[0]["out_t"]
    return _np.ascontiguousarray(_np.asarray(got).reshape(D, T).T).reshape(1, T, D)
```

```python
from contextlib import ExitStack
import math

import numpy as np

import concourse.bass as bass
from concourse import mybir

F32 = mybir.dt.float32
F32R = mybir.dt.float32r
U32 = mybir.dt.uint32
ALU = mybir.AluOpType
ACT = mybir.ActivationFunctionType
AX = mybir.AxisListType

P = 128
T = 512
NT = T // P
D = 1024
KD = D // P
NH, HD = 8, 64
NCMP = 31
NM = 256
MH = 4
FH = 2816
KF = FH // P
BH = 4
RING = 8
PH = 8
TOPK = 16
NE = 128
JB = 8
NB = NE // JB
CHOICE = 7
SPREAD = 8
TT = T // (SPREAD * JB)
GT = 16
HOT = 16
AS = 4
PS = 4
EPS = 1e-6
BIG = 1e30
QS = -0.125


SMALL = {}


def small_columns():
    at = 0
    for name, n in [("norm0", 8), ("norm1", 8), ("norm2", 8), ("norm3", 8), ("norm4", 8), ("norm5", 8),
                    ("mem_norm", 8), ("gn_nsa", 4), ("gn_conv", 4), ("conv_w", 12), ("b_ada", 48),
                    ("norm1_2", 8), ("conv_w2", 32), ("conv_b2", 8), ("mlstm_g", 4), ("norm2_2", 8),
                    ("final_g", 8), ("cond", 8), ("pe", 32), ("b_if", 2),
                    ("w2k", 256), ("w2v", 64)]:
        SMALL[name] = (at, n)
        at += n
    return at


N_SMALL = small_columns()

C_ID, C_ONE, C_IOTA, C_SEL, C_TRI, C_ROW = 0, 128, 256, 384, 896, 1024
N_CONST = 1025


def constants():
    c = np.zeros((P, N_CONST), np.float32)
    c[:, C_ID:C_ID + P] = np.eye(P)
    c[:, C_ONE:C_ONE + P] = 1.0
    c[:, C_IOTA:C_IOTA + P] = np.arange(P)
    for h in range(BH):
        c[h, C_SEL + h * P:C_SEL + (h + 1) * P] = 1.0
    s, t = np.meshgrid(np.arange(P), np.arange(P), indexing="ij")
    c[:, C_TRI:C_TRI + P] = np.where(s > t, BIG, 0.0)
    c[:, C_ROW] = np.arange(P) >= 31
    return c


def cols(v):
    return np.reshape(v, (-1, P)).T


def tile_k(w):
    k, n = w.shape
    return w.reshape(k // P, P, n // P, P).transpose(2, 1, 0, 3).reshape(n // P, P, -1)


def padded(tiles):
    return np.pad(tiles, ((0, 0), (0, 0), (0, D - tiles.shape[2])))


def token_tiles(w):
    return w.reshape(4, 2, P, 512).transpose(0, 2, 1, 3).reshape(4, P, 1024)


def weight_stream(i):
    w_in = i["w_in"][0]
    heads = np.concatenate([np.r_[h * HD:(h + 1) * HD, (h + 4) * HD:(h + 5) * HD] for h in range(4)])
    out = [tile_k(w_in[:, heads])]
    for c in (512, 640, 768, 1024):
        out.append(tile_k(w_in[:, c:c + 128]))
    out.append(token_tiles(np.pad(w_in[:, 896:1304], ((0, 0), (0, 104)))))
    for j in range(4):
        for c in (1816, 2328, 1304):
            out.append(tile_k(w_in[:, c + j * P:c + (j + 1) * P]))
    for w in (i["cmp_k_w1"][0], i["cmp_v_w1"][0]):
        one = w.reshape(4, 8, HD, P).transpose(0, 2, 1, 3).reshape(4, HD, 1024)
        out.append(np.concatenate([one, one], axis=1))
    out.append(tile_k(i["w_out"][0]))
    out.append(tile_k(i["mem_wq"][0]))
    out.append(tile_k(i["mem_wkv"][0][:, :256]))
    out.append(i["mem_wkv"][0][:, 256:].reshape(2, 4, P, 256).transpose(0, 2, 1, 3).reshape(2, P, 1024))
    out.append(tile_k(i["mem_wo"][0]).reshape(2, 4, P, 256).transpose(0, 2, 1, 3).reshape(2, P, 1024))
    wg, wu, ada = tile_k(i["ffn_wg"][0]), tile_k(i["ffn_wu"][0]), tile_k(i["w_ada_2"][0])
    for m in range(KF):
        out += [wg[m:m + 1], wu[m:m + 1], ada[2 * m:2 * m + 2]]
    out.append(ada[2 * KF:])
    wd = tile_k(i["ffn_wd"][0])
    out.append(np.pad(wd, ((0, 0), (0, 0), (0, 256))).reshape(8, P, 3, 1024).transpose(0, 2, 1, 3).reshape(24, P, 1024))
    w2 = i["w_in_2"][0]
    out.append(tile_k(w2[:, 0:1024]))
    out.append(tile_k(w2[:, 1536:2560]))
    out.append(tile_k(np.pad(w2[:, 3584:3592], ((0, 0), (0, 120)))))
    out.append(tile_k(w2[:, 3072:3584]))
    out.append(token_tiles(w2[:, 1024:1536]))
    out.append(token_tiles(w2[:, 2560:3072]))
    ga, gb = tile_k(w2[:, 3592:4616]), tile_k(w2[:, 4616:5640])
    ab = np.concatenate([tile_k(i["w_branch_a_2"][0]), tile_k(i["w_branch_b_2"][0])], axis=2)
    for m in range(KD):
        out += [ga[m:m + 1], gb[m:m + 1], ab[m:m + 1]]
    out.append(tile_k(i["w_out_2"][0]))
    out.append(tile_k(i["w_peer_q_2"][0]))
    keys = i["peer_sub_keys_2"][0].reshape(2, 8, P, P)
    out.append(keys.transpose(0, 3, 1, 2).reshape(2, P, 1024))
    u = i["peer_u_2"][0].reshape(P, P, KD, P).transpose(1, 3, 2, 0).reshape(P, P, 1024)
    v = i["peer_v_2"][0].reshape(P, P, D).transpose(1, 0, 2)
    out += [u, v]
    return np.concatenate(out, axis=0)


def buckets(n):
    large = 16 + np.floor(np.log(np.maximum(n, 1) / 16) / math.log(8) * 16 + 1e-9).astype(np.int64)
    return np.where(n < 16, n, np.minimum(large, 31))


def spread(table, index, keep):
    out = np.full((table.shape[0],) + index.shape, -BIG, np.float32)
    out[:, keep] = table[:, index[keep]]
    return np.moveaxis(out, 0, 1).reshape(P, -1)


def biases(i):
    r = np.arange(P)[:, None]
    dist = 384 + r - np.arange(T)[None, :]
    near = buckets(np.maximum(dist, 0))
    sel = spread(i["rel_bias"], near, dist >= 0)
    win = spread(i["rel_bias"], near[:, 128:], ((dist >= 0) & (dist < 256))[:, 128:])
    back = np.arange(T).reshape(NT, P).T[:, :, None] - (16 * np.arange(32) + 31)[None, None, :]
    cmp = spread(i["rel_bias"], buckets(np.maximum(back, 0)), back >= 0)
    rel = np.clip(dist, -128, 128) + 128
    band = spread(i["rel_bias_2"][0], rel, ~((r < 64) & (dist < r - 63)))
    return sel, win, cmp, band


def smalls(i):
    a = {"norm%d" % n: cols(i["norms"][0, n]) for n in range(6)}
    a |= {"mem_norm": cols(i["mem_norm"]), "gn_nsa": cols(i["gn_nsa"]), "gn_conv": cols(i["gn_conv"]),
          "conv_w": cols(i["conv_w"]), "b_ada": cols(i["b_ada_2"]), "norm1_2": cols(i["norm1_g_2"]),
          "conv_w2": cols(i["conv_w_2"]), "conv_b2": cols(i["conv_b_2"]), "mlstm_g": cols(i["mlstm_norm_g_2"]),
          "norm2_2": cols(i["norm2_g_2"]), "final_g": cols(i["final_g_2"]), "cond": cols(i["c_2"])}
    a["pe"] = np.concatenate([i["cmp_pe"][0].T] * 2, axis=0)
    a["b_if"] = np.pad(np.stack([i["b_igate_2"][0], i["b_fgate_2"][0]], 1), ((0, P - BH), (0, 0)))
    w2k, none = i["cmp_k_w2"][0], np.zeros((P, HD), np.float32)
    a["w2k"] = np.concatenate([w2k, none, none, w2k], axis=1)
    a["w2v"] = i["cmp_v_w2"][0]
    return np.concatenate([a[n] for n in SMALL], axis=1)




def build(nc, weights, x_in, mem_in, smalls_in, consts_in, sel_in, win_in, cmp_in, band_in, out):
    ctx = ExitStack()
    with ctx:
        def sb(name, shape, dt=F32):
            return ctx.enter_context(nc.sbuf_tensor(name, shape, dt))

        def sem(name):
            return ctx.enter_context(nc.semaphore(name))

        gates_dram = nc.dram_tensor("gates_spread", (NB, P, T, JB), F32, kind="Internal").ap()
        acts_dram = nc.dram_tensor("expert_acts", (NE, P, T), F32, kind="Internal").ap()

        ring = sb("ring", [P, RING, D])
        xT = sb("xT", [P, KD, T])
        hT_base = nc.sbuf_base + -nc.sbuf_base % 32
        hT = sb("hT", [P, KD, T])
        small = sb("small", [P, N_SMALL])
        const = sb("const", [P, N_CONST])
        sq = sb("sq", [P, 2, T])
        rms = sb("rms", [P, T])
        rstd = sb("rstd", [P, T])
        mod = sb("mod", [P, 48])
        condT = sb("condT", [P, 8])
        gmod = sb("gmod", [P, 16])
        eps = sb("eps", [P, 2])
        pscr = sb("pool_scratch", [P, 2])
        arena_base = nc.sbuf_base + -nc.sbuf_base % 32
        arena = sb("arena", [P, 29700])

        def at(first, *dims):
            n = int(np.prod(dims))
            assert first + n <= 29700, (first, dims)
            v = arena[:, first:first + n]
            names = " ".join("abcd"[:len(dims)])
            return v if len(dims) == 1 else v.rearrange(
                f"p ({names}) -> p {names}", **{"abcd"[k]: dims[k] for k in range(len(dims))})

        logit = at(0, 2, T)
        prob = at(1024, 2, T)
        probT = at(2048, 2, T)
        least = at(3072, 96)
        total = at(3168, 96)
        rgate = at(3264, 96)
        rrec = at(3360, 96)
        qk = at(3500, 8, T)
        vtok = at(7596, NT, 408)
        conv = at(9228, 12, T)
        o_tok = at(15372, NT, T)
        bias_sel = at(17420, NH, T)
        bias_win = at(21516, NH, 384)
        bias_cmp = at(24588, NH, NT, 32)
        pe_col = at(25612, 2)
        hid = at(25614, 2, 2, 32)
        kcmp = at(25742, 32)
        vcmp = at(25774, P)
        gsig = at(25902, NT, 24)
        conv_y = at(26000, 2, T)
        nT = at(17420, 4, T)
        merged = at(19468, 8, T)
        yT = at(3500, 8, T)
        memT = at(7596, KD, NM)
        mT = at(9644, KD, NM)
        mq = at(11692, 2, T)
        mk = at(12716, 2, NM)
        mv = at(13228, 2, NM)
        om_tok = at(13740, NT, NM)
        omT = at(14764, 2, T)
        ff = at(7596, KF, T)
        ff_gate = at(0, 2, T)
        qk2 = at(3500, 8, T)
        cv2 = at(7596, 8, T)
        sig_o = at(11692, 4, T)
        va = at(13740, NT, T)
        vb = at(15788, NT, BH, P + 1)
        bias_band = at(17852, NH, T)
        oa_tok = at(21948, NT, T)
        hb_tok = at(23996, NT, T)
        conv_acc = at(26044, 2, T)
        yaT = at(17852, 4, T)
        ybT = at(19900, 4, T)
        y2T = at(3500, 8, T)
        gate_ab = at(0, 4, T)
        rows = at(27068, 4, T)
        row_f, row_i, row_a, row_b = (rows[0:BH, n, :] for n in range(4))
        tcol = at(29116, 64)
        wdec = at(0, 2, T)
        wdiag = at(1024, 2, P)
        mrow = at(1280, 2, T)
        wqk = at(17852, 2, NT, T)
        den = at(29200, 64)
        hsq = at(21948, NT, T)
        pq = at(0, 16, T)
        s_left = at(0, 16, P)
        cand = at(2048, PH, TOPK, TOPK)
        cand_left = at(4096, PH, TOPK, TOPK)
        eqs = at(6144, PH, TOPK, TOPK)
        s_all = at(8192, NT, 16, P)
        kept = at(8192, NT, 16 * P)
        chosen = kept[:, :, 0:3 * P]
        expd = kept[:, :, 3 * P:4 * P]
        s_top = at(16384, 16, TOPK)
        i_topf = at(16640, 16, TOPK)
        best = at(16896, PH, TOPK)
        a_f = at(17024, PH, TOPK)
        b_f = at(17152, PH, TOPK)
        gsum = at(17280, 2, NT, PH)
        i_top = at(17344, 16, TOPK).bitcast(U32)
        c_top = at(17600, PH, TOPK).bitcast(U32)
        c_hi = at(17728, PH, TOPK).bitcast(U32)
        c_lo = at(17856, PH, TOPK).bitcast(U32)
        chosenT = at(17984, 3, T)
        cur = at(19520, 3, JB * TT)
        hot1 = at(0, HOT, P)
        hot2 = at(2048, HOT, P)
        stage = at(4096, 2, NB, GT * JB)
        act = at(19800, 2, T)
        gblk = at(0, 2, T, JB)
        act_in = at(8192, AS, T)
        weighed = at(10240, 2, T)

        def split(name, base, first, *dims):
            return nc.alloc_sbuf_tensor_at(name, [P] + list(dims), F32R, offset=base + 4 * first)

        p_split = split("weighted_split", arena_base, 11264, PS, 2, T)
        h_split = split("hidden_split", arena_base, 21400, 2, KD, T)
        w_split = split("weight_split", hT_base, 0, 2, 2, D)

        bank = [ctx.enter_context(nc.psum_tensor(f"bank{n}", [P, T], F32)) for n in range(8)]
        ident = const[:, C_ID:C_ID + P]
        ones = const[:, C_ONE:C_ONE + P]
        iota = const[:, C_IOTA:C_IOTA + P]
        rowmask = const[:, C_ROW:C_ROW + 1]

        def sm(name, k=0, n=1, rows=P):
            a = SMALL[name][0] + k
            return small[0:rows, a:a + n]

        consts_in_sem = sem("consts_loaded")
        x_loaded = sem("x_loaded")
        mem_loaded = sem("mem_loaded")
        bias_loaded = sem("bias_loaded")
        band_loaded = sem("band_loaded")
        tile_loaded = [sem(f"tile_loaded{n}") for n in range(RING)]
        tiles_used = sem("tiles_used")
        bias_negated = sem("bias_negated")
        sq_ready = sem("square_ready")
        sq_summed = sem("square_summed")
        rms_ready = sem("rms_ready")
        normed = sem("normed")
        proj_done = sem("proj_done")
        evac_act = sem("evacuated_by_act")
        evac_dve = sem("evacuated_by_dve")
        act_chain = sem("act_chain")
        dve_chain = sem("dve_chain")
        logits_ready = sem("logits_ready")
        qk_done = sem("qk_done")
        prob_ready = sem("prob_ready")
        prob_turned = sem("prob_turned")
        probT_ready = sem("probT_ready")
        pv_done = sem("pv_done")
        head_out = sem("head_out")
        gates_sig = sem("gates_sigmoid")
        conv_ready = sem("conv_ready")
        cmp_hidden = sem("cmp_hidden")
        cmp_pe_ready = sem("cmp_pe_ready")
        cmp_gelu = sem("cmp_gelu")
        cmp_kv = sem("cmp_kv")
        cmp_done = sem("cmp_done")
        turned = sem("turned")
        turned_out = sem("turned_out")
        yb_out = sem("yb_out")
        mrow_out = sem("mrow_out")
        eps_set = sem("eps_set")
        x3_ready = sem("x3_ready")
        cond_ready = sem("cond_ready")
        ada_done = sem("ada_done")
        conv2_acc = sem("conv2_acc")
        conv2_ready = sem("conv2_ready")
        ones_ready = sem("ones_ready")
        y2_ready = sem("y2_ready")
        rows_ln = sem("rows_ln")
        rows_m = sem("rows_m")
        rows_exp = sem("rows_exp")
        cols_done = sem("cols_done")
        cols_out = sem("cols_out")
        mrow_done = sem("mrow_done")
        diag_ready = sem("diag_ready")
        decay_ready = sem("decay_ready")
        lqk_done = sem("lqk_done")
        lqk_ready = sem("lqk_ready")
        lpv_done = sem("lpv_done")
        lnum_out = sem("lnum_out")
        hb_sq = sem("hb_square_mean")
        hb_rms = sem("hb_rms")
        hb_ready = sem("hb_ready")
        score_done = sem("score_done")
        score_out = sem("score_out")
        best_ready = sem("best_ready")
        best_exp = sem("best_exp")
        chosen_ready = sem("chosen_ready")
        chosen_turned = sem("chosen_turned")
        chosen_out = sem("chosen_out")
        cur_ready = sem("cur_ready")
        hot_ready = sem("hot_ready")
        hot_used = sem("hot_used")
        staged = sem("staged")
        stored = [sem("gates_stored0"), sem("gates_stored1")]
        g_loaded = [sem("gates_loaded0"), sem("gates_loaded1")]
        h_hi_ready = sem("h_hi_ready")
        h_lo_ready = sem("h_lo_ready")
        w_hi_ready = sem("w_hi_ready")
        w_lo_ready = sem("w_lo_ready")
        expert_done = sem("expert_tile_done")
        gelu_ready = sem("gelu_ready")
        act_stored = [sem(f"act_stored{n}") for n in range(2)]
        act_loaded = [sem(f"act_loaded{n}") for n in range(AS)]
        weighed_ready = sem("weighed_ready")
        p_hi_ready = sem("p_hi_ready")
        p_lo_ready = sem("p_lo_ready")
        out_stored = sem("out_stored")

        PROJ = [("qk", "A" * 8), ("vtok", "A" * 4), ("conv", "A" * 12), ("w_out", "A" * 8),
                ("mq", "A" * 2), ("mk", "A" * 2), ("mv", "A" * 2), ("mo", "A" * 8),
                ("ffn", "AV" * KF), ("wd", "A" * 8),
                ("qk2", "A" * 8), ("cv2", "A" * 8), ("if", "AA"), ("og", "A" * 4),
                ("va", "A" * 4), ("vb", "A" * 4), ("branch", "AVAV" * KD), ("w_out2", "V" * 8),
                ("pq", "A" * 16)]
        first, takers = {}, ""
        for name, who in PROJ:
            first[name] = len(takers)
            takers += who

        def taken(j):
            who = takers[j]
            return (evac_act if who == "A" else evac_dve), takers[:j + 1].count(who)

        NORMS = [8, 4, 4, 8, 8, 8, 8, 8, 8, 8, 8, 8]
        norm_base = [sum(NORMS[:n]) for n in range(len(NORMS) + 1)]
        UNITS = 96 + 16 + 32

        def nsa_unit(i):
            return i // 32, (i % 32) // NH, i % NH

        def nsa_pieces(i):
            branch, t, _ = nsa_unit(i)
            return [NCMP] if branch == 2 else [P] * (t + 1 if branch == 0 else min(t + 1, 3))

        def nsa_width(i):
            return sum(nsa_pieces(i))

        def nsa_cols(i):
            return P * len(nsa_pieces(i))

        def wait(eng, semaphore, value):
            if not isinstance(value, int) or value > 0:
                eng.wait_ge(semaphore, value)

        block = ctx.enter_context(nc.Block())

        n_tiles = weights.shape[0]
        BEFORE = n_tiles - 2 * NE

        @block.sync
        def _(sp):

            def load(n, slot):
                sp.dma_start(ring[:, slot, :], weights[n]).then_inc(tile_loaded[slot], 16)

            for n in range(RING):
                load(n, n)
            full = BEFORE // RING
            with sp.Fori(1, full) as g:
                for s in range(RING):
                    sp.wait_ge(tiles_used, (g - 1) * RING + s + 1)
                    load(g * RING + s, s)
            for n in range(full * RING, BEFORE):
                sp.wait_ge(tiles_used, n - RING + 1)
                load(n, n % RING)
            def tile(e, i=0, used=None):
                sp.wait_ge(*(used or (w_lo_ready, i * JB + (e - RING + 1))))
                load(i * JB + (BEFORE + e), (BEFORE + e) % RING)

            def hidden(e, i=0):
                sp.wait_ge(gelu_ready, i * JB + (e + 1))
                sp.dma_start(acts_dram[i * JB + e], act[:, e % 2, :]).then_inc(act_stored[e % 2], 16)

            def act_back(e, i=0):
                wait(sp, weighed_ready, i * (2 * JB) + (e - AS + 1))
                sp.dma_start(act_in[:, e % AS, :], acts_dram[i * (2 * JB) + e]).then_inc(act_loaded[e % AS], 16)

            def gates(b, i=0):
                wait(sp, weighed_ready, i * (2 * JB) + (b - 1) * JB)
                sp.dma_start(gblk[:, b % 2], gates_dram[i * 2 + b]).then_inc(g_loaded[b % 2], 16)

            for e in range(RING):
                tile(e, used=(tiles_used, BEFORE + e - RING + 1))
            with sp.Fori(0, NB - 1) as i:
                for e in range(JB):
                    hidden(e, i)
                    tile(e + RING, i)
            for e in range(JB):
                hidden(NE - JB + e)
                tile(NE - JB + e + RING)
            for n in range(2):
                sp.wait_ge(act_stored[n], 16 * (NE // 2))
            for e in range(AS - 1):
                act_back(e)
            for n in range(2):
                sp.wait_ge(stored[n], 16 * (T // GT // 2))
            sp.wait_ge(hot_used, T)
            gates(0)

            def second(b, i=0, last=False):
                if not last:
                    gates(b + 1, i)
                for j in range(JB):
                    e = b * JB + j
                    if not last or j < JB - AS + 1:
                        act_back(e + AS - 1, i)
                    if not last:
                        sp.wait_ge(w_lo_ready, i * (2 * JB) + (NE + e + 1))
                        load(i * (2 * JB) + (BEFORE + NE + RING + e), (BEFORE + e) % RING)

            second(0)
            second(1)
            with sp.Fori(0, NB // 2 - 2) as i:
                second(2, i)
                second(3, i)
            second(NB - 2)
            second(NB - 1, last=True)
            for k in range(KD):
                sp.wait_ge(normed, norm_base[11] + k + 1)
                sp.dma_start(out[k], hT[:, k, :]).then_inc(out_stored, 16)
            sp.wait_ge(out_stored, 16 * KD)

        @block.gpsimd
        def _(pool):
            pool.wait_ge(bias_loaded, 48)
            for b in (bias_sel, bias_win, bias_cmp):
                v = b.rearrange("p a b -> p (a b)") if len(b.shape) == 3 else b.rearrange("p a b c -> p (a b c)")
                nc.gpsimd.tensor_scalar(v, v, -1.0, None, ALU.mult).then_inc(bias_negated, 1)
            pool.wait_ge(band_loaded, 16)
            v = bias_band.rearrange("p a b -> p (a b)")
            nc.gpsimd.tensor_scalar(v, v, -1.0, None, ALU.mult).then_inc(bias_negated, 1)
            def split_low(e, i=0):
                pool.wait_ge(w_hi_ready, i * JB + (e + 1))
                nc.gpsimd.tensor_tensor(w_split[:, e % 2, 1, :], ring[:, (BEFORE + e) % RING, :],
                                        w_split[:, e % 2, 0, :], ALU.subtract).then_inc(w_lo_ready, 1)

            with pool.Fori(0, 2 * NE // JB) as i:
                for e in range(JB):
                    split_low(e, i)

        @block.scalar
        def _(act_e):
            a = nc.scalar

            def link(ins, n=[0]):
                n[0] += 1
                ins.then_inc(act_chain, 1)
                act_e.wait_ge(act_chain, n[0])

            act_e.dma_start(const[:, :], consts_in).then_inc(consts_in_sem, 16)
            act_e.dma_start(small[:, :], smalls_in).then_inc(consts_in_sem, 16)
            for k in range(KD):
                act_e.dma_start(xT[:, k, :], x_in[k]).then_inc(x_loaded, 16)
            act_e.dma_start(bias_sel, sel_in.rearrange("p (a b) -> p a b", a=NH)).then_inc(bias_loaded, 16)
            act_e.dma_start(bias_win, win_in.rearrange("p (a b) -> p a b", a=NH)).then_inc(bias_loaded, 16)
            act_e.dma_start(bias_cmp, cmp_in.rearrange("p (a b c) -> p a b c", a=NH, b=NT)).then_inc(bias_loaded, 16)

            def norm(idx, src, width, free=T):
                for k in range(NORMS[idx]):
                    n = norm_base[idx] + k
                    if n >= 2:
                        act_e.wait_ge(sq_summed, n - 1)
                    a.activation(sq[:, n % 2, 0:free], src(k), ACT.Square).then_inc(sq_ready, 1)
                act_e.wait_ge(sq_summed, norm_base[idx + 1])
                if idx:
                    act_e.wait_ge(normed, norm_base[idx])
                a.activation(rms[:, 0:free], bank[7][:, 0:free], ACT.Sqrt, bias=eps[:, 0:1],
                             scale=1.0 / width).then_inc(rms_ready, 1)

            def take(j, dst, func=ACT.Copy, scale=1.0, m=P, n=T, bias=0.0):
                act_e.wait_ge(proj_done, j + 1)
                return a.activation(dst, bank[j % 2][0:m, 0:n], func, scale=scale, bias=bias).then_inc(evac_act, 1)

            def softmax(u0, units, width, scols):
                for i in range(units + 1):
                    if i < units:
                        u = u0 + i
                        w = width(i)
                        act_e.wait_ge(logits_ready, u + 1)
                        if u >= 2:
                            act_e.wait_ge(prob_turned, u - 1)
                        a.activation(prob[:, u % 2, 0:w], logit[:, u % 2, 0:w], ACT.Exp, scale=-1.0,
                                     bias=least[:, i:i + 1], accum_out=total[:, i:i + 1]).then_inc(prob_ready, 1)
                    if i >= 1:
                        u = u0 + i - 1
                        w = scols(i - 1)
                        rows_ = NCMP if width(i - 1) == NCMP else P
                        act_e.wait_ge(prob_turned, u + 1)
                        if u >= 2:
                            act_e.wait_ge(pv_done, u - 1)
                        a.activation(probT[0:rows_, u % 2, 0:w], bank[2 + u % 2][0:rows_, 0:w],
                                     ACT.Copy).then_inc(probT_ready, 1)

            act_e.wait_ge(eps_set, 1)
            act_e.wait_ge(consts_in_sem, 32)
            act_e.wait_ge(x_loaded, 16 * KD)
            norm(0, lambda k: xT[:, k, :], D)
            j = first["qk"]
            for k in range(8):
                take(j + k, qk[:, k, :], scale=QS if k < 4 else 1.0)
            j = first["vtok"]
            for t in range(NT):
                take(j + t, vtok[:, t, :], n=408)
            act_e.wait_ge(evac_act, 12)
            a.activation(gsig, vtok[:, :, 384:408], ACT.Sigmoid).then_inc(gates_sig, 1)
            j = first["conv"]
            for k in range(12):
                take(j + k, conv[:, k, :])
            for kv in range(2):
                act_e.wait_ge(cmp_pe_ready, kv + 1)
                for g in range(2):
                    a.activation(hid[:, kv, g, 0:NCMP], bank[6 - g][:, kv * 128 + g * 32:kv * 128 + g * 32 + NCMP],
                                 ACT.Gelu_apprx_tanh, bias=pe_col[:, kv:kv + 1]).then_inc(cmp_gelu, 1)
            act_e.wait_ge(cmp_kv, 1)
            a.activation(kcmp[:, 0:NCMP], bank[2][:, 0:NCMP], ACT.Copy).then_inc(cmp_done, 1)
            a.activation(vcmp[0:NCMP, :], bank[2][0:NCMP, 128:256], ACT.Copy).then_inc(cmp_done, 1)
            softmax(0, 96, nsa_width, nsa_cols)
            for c in range(4):
                act_e.wait_ge(turned, c + 1)
                a.activation(nT[:, c, :], bank[2 + c % 2][:, :], ACT.Copy).then_inc(turned_out, 1)
            act_e.wait_ge(turned_out, 4)
            norm(1, lambda k: nT[:, k, :], 512)
            act_e.wait_ge(conv_ready, 4)
            norm(2, lambda k: conv[:, 3 * k, :], 512)
            j = first["w_out"]
            for k in range(8):
                take(j + k, yT[:, k, :])
            act_e.wait_ge(evac_act, taken(j + 7)[1])
            act_e.dma_start(memT, mem_in.rearrange("k p m -> p k m")).then_inc(mem_loaded, 16)
            norm(3, lambda k: yT[:, k, :], D)
            act_e.wait_ge(normed, norm_base[4])
            norm(4, lambda k: xT[:, k, :], D)
            act_e.wait_ge(mem_loaded, 16)
            norm(5, lambda k: memT[:, k, :], D, NM)
            for k in range(2):
                take(first["mq"] + k, mq[:, k, :], scale=QS)
            for k in range(2):
                take(first["mk"] + k, mk[:, k, :], n=NM)
            for k in range(2):
                take(first["mv"] + k, mv[:, k, :], n=NM)
            softmax(96, 16, lambda i: NM, lambda i: NM)
            for c in range(2):
                act_e.wait_ge(turned, 4 + c + 1)
                a.activation(omT[:, c, :], bank[2 + c % 2][:, :], ACT.Copy).then_inc(turned_out, 1)
            for k in range(8):
                take(first["mo"] + k, yT[:, k, :])
            act_e.wait_ge(evac_act, taken(first["mo"] + 7)[1])
            norm(6, lambda k: yT[:, k, :], D)
            act_e.wait_ge(normed, norm_base[7])
            norm(7, lambda k: xT[:, k, :], D)
            a.activation(condT[:, :], sm("cond", 0, 8), ACT.Silu).then_inc(cond_ready, 1)
            for m in range(KF):
                j = first["ffn"] + 2 * m
                act_e.wait_ge(proj_done, j + 1)
                if m >= 2:
                    act_e.wait_ge(evac_dve, m - 1)
                a.activation(ff_gate[:, m % 2, :], bank[j % 2][:, :], ACT.Silu).then_inc(evac_act, 1)
            for k in range(8):
                take(first["wd"] + k, yT[:, k, :])
            act_e.wait_ge(evac_act, taken(first["wd"] + 7)[1])
            act_e.dma_start(bias_band, band_in.rearrange("p (a b) -> p a b", a=NH)).then_inc(band_loaded, 16)
            norm(8, lambda k: yT[:, k, :], D)
            act_e.wait_ge(normed, norm_base[9])
            norm(9, lambda k: xT[:, k, :], D)
            for k in range(8):
                take(first["qk2"] + k, qk2[:, k, :], scale=QS if k < 4 else 1.0)
            for k in range(8):
                take(first["cv2"] + k, cv2[:, k, :])
            take(first["if"], row_i, ACT.Identity, m=BH, bias=sm("b_if", 0, 1, BH))
            take(first["if"] + 1, row_f, ACT.Identity, m=BH, bias=sm("b_if", 1, 1, BH))
            for k in range(4):
                take(first["og"] + k, sig_o[:, k, :], ACT.Sigmoid)
            for t in range(NT):
                take(first["va"] + t, va[:, t, :])
            act_e.wait_ge(ones_ready, 1)
            for t in range(NT):
                j = first["vb"] + t
                act_e.wait_ge(proj_done, j + 1)
                a.activation(vb[:, t, :, 0:P], bank[j % 2][:, :].rearrange("p (h d) -> p h d", h=BH),
                             ACT.Copy).then_inc(evac_act, 1)
            act_e.wait_ge(evac_act, taken(first["if"] + 1)[1])
            link(a.activation(row_a, row_f, ACT.Abs))
            link(a.activation(row_a, row_a, ACT.Exp, scale=-1.0))
            a.activation(row_a, row_a, ACT.Ln, bias=eps[0:BH, 1:2]).then_inc(rows_ln, 1)
            for k in range(8):
                act_e.wait_ge(conv2_acc, k + 1)
                a.activation(cv2[:, k, :], conv_acc[:, k % 2, :], ACT.Silu,
                             bias=sm("conv_b2", k)).then_inc(conv2_ready, 1)
            act_e.wait_ge(rows_m, 1)
            a.activation(row_f, row_f, ACT.Exp, scale=-1.0).then_inc(rows_exp, 1)
            softmax(112, 32, lambda i: P * (i // NH + 1), lambda i: P * (i // NH + 1))
            act_e.wait_ge(cols_done, 1)
            a.activation(tcol[:, 0:32], bank[6][:, 0:32], ACT.Copy).then_inc(cols_out, 1)
            act_e.wait_ge(cols_out, 1)
            def take_mrow(h):
                act_e.wait_ge(mrow_done, h + 1)
                if h >= 2:
                    act_e.wait_ge(diag_ready, (h - 1) * NT)
                a.activation(mrow[:, h % 2, :], bank[4 + h % 2][:, :], ACT.Copy).then_inc(mrow_out, 1)

            take_mrow(0)
            for i in range(BH * NT):
                h, s = divmod(i, NT)
                w = T - s * P
                if s == 0:
                    if h + 1 < BH:
                        take_mrow(h + 1)
                    act_e.wait_ge(mrow_out, h + 1)
                act_e.wait_ge(diag_ready, i + 1)
                if i >= 2:
                    act_e.wait_ge(lqk_ready, i - 1)
                b_s = tcol[:, s * BH + h:s * BH + h + 1]
                last = a.activation(wdec[:, i % 2, 0:P], wdiag[:, i % 2, :], ACT.Exp, scale=-1.0, bias=b_s)
                if w > P:
                    last = a.activation(wdec[:, i % 2, P:w], mrow[:, h % 2, (s + 1) * P:T], ACT.Exp,
                                        scale=-1.0, bias=b_s)
                last.then_inc(decay_ready, 1)
            for c in range(4):
                act_e.wait_ge(turned, 6 + c + 1)
                a.activation(yaT[:, c, :], bank[2 + c % 2][:, :], ACT.Copy).then_inc(turned_out, 1)
            act_e.wait_ge(hb_sq, 1)
            a.activation(den[:, 16:32], den[:, 0:16], ACT.Sqrt, bias=eps[:, 0:1], scale=1.0 / P).then_inc(hb_rms, 1)
            for m in range(KD):
                j = first["branch"] + 4 * m
                for g in range(2):
                    n = 2 * m + g
                    act_e.wait_ge(proj_done, j + 2 * g + 1)
                    if m >= 1:
                        act_e.wait_ge(y2_ready, m)
                    a.activation(gate_ab[:, g, :], bank[(j + 2 * g) % 2][:, :], ACT.Sigmoid).then_inc(evac_act, 1)
            act_e.wait_ge(evac_dve, taken(first["w_out2"] + 7)[1])
            norm(10, lambda k: xT[:, k, :], D)
            for k in range(KD):
                act_e.wait_ge(normed, norm_base[10] + k + 1)
                a.activation(h_split[:, 0, k, :], hT[:, k, :], ACT.Copy).then_inc(h_hi_ready, 1)
            for k in range(16):
                take(first["pq"] + k, pq[:, k, :])
            for n in range(4 * NT):
                t, q = divmod(n, 4)
                act_e.wait_ge(score_done, n + 1)
                a.activation(s_all[:, t, 4 * q:4 * q + 4, :], bank[2 + q].rearrange("p (a b) -> p a b", a=4),
                             ACT.Copy).then_inc(score_out, 1)

            def split_high(e, i=0, step=JB):
                n = BEFORE + e
                act_e.wait_ge(tile_loaded[n % RING], i * (16 * step // RING) + 16 * (n // RING + 1))
                wait(act_e, expert_done, i * step + (e - 1))
                a.activation(w_split[:, e % 2, 0, :], ring[:, n % RING, :], ACT.Copy).then_inc(w_hi_ready, 1)

            def gelu(e, i=0):
                act_e.wait_ge(expert_done, i * JB + (e + 1))
                wait(act_e, act_stored[e % 2], i * (16 * JB // 2) + 16 * (e // 2))
                a.activation(act[:, e % 2, :], bank[e % 2][:, :], ACT.Gelu_apprx_tanh).then_inc(gelu_ready, 1)

            act_e.wait_ge(h_hi_ready, KD)
            act_e.wait_ge(h_lo_ready, KD)
            act_e.wait_ge(evac_act, taken(first["pq"] + 15)[1])
            split_high(0)
            split_high(1)
            for e in range(JB):
                split_high(e + 2)
                gelu(e)
            with act_e.Fori(0, CHOICE - 1) as i:
                for e in range(JB, 2 * JB):
                    split_high(e + 2, i)
                    gelu(e, i)
            for e in range(CHOICE * JB, (CHOICE + 1) * JB):
                split_high(e + 2)
                gelu(e)
                if e == CHOICE * JB:
                    act_e.wait_ge(best_ready, 1)
                    a.activation(expd, expd, ACT.Exp).then_inc(best_exp, 1)

            def stage_gates(n, i=0):
                half, q = n // 4 % 2, n % 4
                act_e.wait_ge(hot_used, i * (JB * TT) + 4 * n + 4)
                if q == 0:
                    wait(act_e, stored[half], i * (16 * JB * TT // GT // 2) + 16 * (n // 8))
                a.activation(
                    stage[:, half].rearrange("p b (t j) -> p b t j", t=GT)[:, :, 4 * q:4 * q + 4, :].rearrange(
                        "p b t j -> p t b j"),
                    bank[2 + n % 4][:, :].rearrange("p (t b j) -> p t b j", t=4, j=JB), ACT.Copy).then_inc(staged, 1)
                if q == 3:
                    act_e.wait_ge(staged, i * (JB * TT // 4) + n + 1)
                    act_e.dma_start(
                        gates_dram.rearrange("b p t j -> p b (t j)")[
                            :, :, bass.ds(i * (JB * TT * JB) + n // 4 * GT * JB, GT * JB)],
                        stage[:, half]).then_inc(stored[half], 16)

            def spread_block(i):
                for j in range(JB):
                    e = (CHOICE + 1) * JB + j
                    split_high(e + 2, i)
                    gelu(e, i)
                    for n in range(j * TT // 4, (j + 1) * TT // 4):
                        stage_gates(n, i)

            spread_block(0)
            with act_e.Fori(1, SPREAD) as i:
                spread_block(i)

            def weighted_high(e, i=0):
                act_e.wait_ge(weighed_ready, i * (2 * JB) + e + 1)
                if e >= PS:
                    act_e.wait_ge(expert_done, i * (2 * JB) + NE + e - PS + 1)
                a.activation(p_split[:, e % PS, 0, :], weighed[:, e % 2, :], ACT.Copy).then_inc(p_hi_ready, 1)

            def second(b, i=0):
                for e in range(b * JB, (b + 1) * JB):
                    if e >= 2:
                        split_high(NE + e, i, 2 * JB)
                    if e + 1 < NE:
                        weighted_high(e + 1, i)

            weighted_high(0)
            for b in range(2):
                second(b)
            with act_e.Fori(0, NB // 2 - 2) as i:
                second(2, i)
                second(3, i)
            for b in range(NB - 2, NB):
                second(b)
            act_e.wait_ge(x3_ready, KD)
            norm(11, lambda k: xT[:, k, :], D)

        @block.vector
        def _(dve):
            v = nc.vector
            chain = [0]

            def link(ins):
                chain[0] += 1
                ins.then_inc(dve_chain, 1)
                dve.wait_ge(dve_chain, chain[0])

            v.memset(eps[:, 0:1], EPS).then_inc(dve_chain, 1)
            chain[0] += 1
            dve.wait_ge(dve_chain, 1)
            v.memset(eps[:, 1:2], 1.0).then_inc(eps_set, 1)
            dve.wait_ge(consts_in_sem, 32)

            def norm(idx, src, dst, gain, free=T, shift=None, add=False):
                dve.wait_ge(rms_ready, idx + 1)
                link(v.reciprocal(rstd[:, 0:free], rms[:, 0:free]))
                for k in range(NORMS[idx]):
                    one = v.scalar_tensor_tensor(out=src(k) if add else dst(k), in0=src(k), scalar=gain(k),
                                                 in1=rstd[:, 0:free], op0=ALU.mult, op1=ALU.mult)
                    if add:
                        link(one)
                        v.tensor_tensor(dst(k), dst(k), src(k), ALU.add).then_inc(normed, 1)
                    elif shift is not None:
                        link(one)
                        v.tensor_scalar(dst(k), dst(k), shift(k), None, ALU.add).then_inc(normed, 1)
                    else:
                        one.then_inc(normed, 1)

            def attend(u0, units, width, bias, gate, where, adds):
                for i in range(units + 2):
                    if i < units:
                        u, w = u0 + i, width(i)
                        dve.wait_ge(qk_done, u + 1)
                        if u >= 2:
                            dve.wait_ge(prob_ready, u - 1)
                        if bias is None:
                            v.tensor_scalar(logit[:, u % 2, 0:w], bank[u % 2][:, 0:w], 0.0, 3.0e38, ALU.add, ALU.min,
                                            accum_out=least[:, i:i + 1]).then_inc(logits_ready, 1)
                        else:
                            v.tensor_tensor_reduce(logit[:, u % 2, 0:w], bank[u % 2][:, 0:w], bias(i), 1.0, 3.0e38,
                                                   ALU.add, ALU.min, least[:, i:i + 1]).then_inc(logits_ready, 1)
                    if i >= 2:
                        n = i - 2
                        u = u0 + n
                        dve.wait_ge(pv_done, u + 1)
                        link(v.reciprocal(rrec[:, n:n + 1], total[:, n:n + 1]))
                        o = bank[4 + u % 2][:, 0:HD]
                        if gate is None:
                            v.tensor_scalar(where(n), o, rrec[:, n:n + 1], None, ALU.mult).then_inc(head_out, 1)
                            continue
                        link(v.tensor_tensor(rgate[:, n:n + 1], rrec[:, n:n + 1], gate(n), ALU.mult))
                        if adds(n):
                            dve.wait_ge(head_out, u - 31)
                            v.scalar_tensor_tensor(out=where(n), in0=o, scalar=rgate[:, n:n + 1], in1=where(n),
                                                   op0=ALU.mult, op1=ALU.add).then_inc(head_out, 1)
                        else:
                            v.tensor_scalar(where(n), o, rgate[:, n:n + 1], None, ALU.mult).then_inc(head_out, 1)

            norm(0, lambda k: xT[:, k, :], lambda k: hT[:, k, :], lambda k: sm("norm0", k))
            for j in range(4):
                cc, cx, cb = (conv[:, 3 * j + n, :] for n in range(3))
                y = conv_y[:, j % 2, :]
                sem_, val = taken(first["conv"] + 3 * j + 2)
                dve.wait_ge(sem_, val)
                link(v.tensor_tensor(cx, cc, cx, ALU.mult))
                link(v.tensor_scalar(y, cx, sm("conv_w", j), None, ALU.mult))
                for k in range(1, 3):
                    link(v.scalar_tensor_tensor(out=y[:, k:T], in0=cx[:, 0:T - k], scalar=sm("conv_w", 4 * k + j),
                                                in1=y[:, k:T], op0=ALU.mult, op1=ALU.add))
                v.tensor_tensor(cc, cb, y, ALU.mult).then_inc(conv_ready, 1)
            dve.wait_ge(gates_sig, 1)
            link(v.tensor_scalar(gsig[:, 0, 0:24:3], gsig[:, 0, 0:24:3], rowmask, None, ALU.mult))
            for kv in range(2):
                dve.wait_ge(cmp_hidden, kv + 1)
                v.tensor_copy(pe_col[:, kv:kv + 1], bank[6][:, kv * 128 + 64:kv * 128 + 65]).then_inc(cmp_pe_ready, 1)
            dve.wait_ge(bias_negated, 3)

            def nsa_bias(i):
                br, t, h = nsa_unit(i)
                if br == 0:
                    return bias_sel[:, h, 384 - P * t:T]
                if br == 1:
                    return bias_win[:, h, max(256 - P * t, 0):384]
                return bias_cmp[:, h, t, 0:NCMP]

            def nsa_gate(i):
                br, t, h = nsa_unit(i)
                c = 3 * h + (1, 2, 0)[br]
                return gsig[:, t, c:c + 1]

            def nsa_where(i):
                br, t, h = nsa_unit(i)
                return o_tok[:, t, h * HD:(h + 1) * HD]

            attend(0, 96, nsa_width, nsa_bias, nsa_gate, nsa_where, lambda i: nsa_unit(i)[0] > 0)
            norm(1, lambda k: nT[:, k, :], lambda k: merged[:, k, :], lambda k: sm("gn_nsa", k))
            norm(2, lambda k: conv[:, 3 * k, :], lambda k: merged[:, 4 + k, :], lambda k: sm("gn_conv", k))
            norm(3, lambda k: yT[:, k, :], lambda k: xT[:, k, :], lambda k: sm("norm1", k), add=True)
            norm(4, lambda k: xT[:, k, :], lambda k: hT[:, k, :], lambda k: sm("norm2", k))
            norm(5, lambda k: memT[:, k, :], lambda k: mT[:, k, :], lambda k: sm("mem_norm", k), NM)
            attend(96, 16, lambda i: NM, None, None,
                   lambda i: om_tok[:, i // MH, (i % MH) * HD:(i % MH + 1) * HD], None)
            norm(6, lambda k: yT[:, k, :], lambda k: xT[:, k, :], lambda k: sm("norm3", k), add=True)
            norm(7, lambda k: xT[:, k, :], lambda k: hT[:, k, :], lambda k: sm("norm4", k))
            for m in range(KF):
                j = first["ffn"] + 2 * m + 1
                dve.wait_ge(evac_act, taken(j - 1)[1])
                dve.wait_ge(proj_done, j + 1)
                v.tensor_tensor(ff[:, m, :], bank[j % 2][:, :], ff_gate[:, m % 2, :], ALU.mult).then_inc(evac_dve, 1)
            dve.wait_ge(ada_done, 1)
            link(v.tensor_tensor(mod[:, :], bank[6][:, 0:48], sm("b_ada", 0, 48), ALU.add))
            link(v.scalar_tensor_tensor(out=gmod[:, 0:8], in0=mod[:, 8:16], scalar=1.0, in1=sm("norm1_2", 0, 8),
                                        op0=ALU.add, op1=ALU.mult))
            link(v.scalar_tensor_tensor(out=gmod[:, 8:16], in0=mod[:, 32:40], scalar=1.0, in1=sm("norm2_2", 0, 8),
                                        op0=ALU.add, op1=ALU.mult))
            norm(8, lambda k: yT[:, k, :], lambda k: xT[:, k, :], lambda k: sm("norm5", k), add=True)
            norm(9, lambda k: xT[:, k, :], lambda k: hT[:, k, :], lambda k: gmod[:, k:k + 1],
                 shift=lambda k: mod[:, k:k + 1])
            v.memset(vb[:, :, :, P:P + 1], 1.0).then_inc(ones_ready, 1)
            for k in range(8):
                sem_, val = taken(first["cv2"] + k)
                dve.wait_ge(sem_, val)
                if k >= 2:
                    dve.wait_ge(conv2_ready, k - 1)
                y, u = conv_acc[:, k % 2, :], cv2[:, k, :]
                link(v.tensor_scalar(y, u, sm("conv_w2", 24 + k), None, ALU.mult))
                for d in range(1, 4):
                    one = v.scalar_tensor_tensor(out=y[:, d:T], in0=u[:, 0:T - d],
                                                 scalar=sm("conv_w2", 8 * (3 - d) + k), in1=y[:, d:T],
                                                 op0=ALU.mult, op1=ALU.add)
                    if d < 3:
                        link(one)
                    else:
                        one.then_inc(conv2_acc, 1)
            dve.wait_ge(rows_ln, 1)
            link(v.scalar_tensor_tensor(out=row_b, in0=row_f, scalar=0.0, in1=row_a, op0=ALU.min, op1=ALU.subtract))
            link(v.memset(row_f, 0.0))
            link(v.tensor_tensor_scan(row_a, row_b, row_f, 0.0, ALU.add, ALU.add))
            link(v.tensor_tensor(row_b, row_i, row_a, ALU.subtract))
            link(v.tensor_tensor_scan(row_i, row_b, row_b, 0.0, ALU.max, ALU.max))
            v.tensor_tensor(row_f, row_a, row_i, ALU.add).then_inc(rows_m, 1)
            dve.wait_ge(bias_negated, 4)
            attend(112, 32, lambda i: P * (i // NH + 1), lambda i: bias_band[:, i % NH, 384 - P * (i // NH):T],
                   None, lambda i: oa_tok[:, i // NH, (i % NH) * HD:(i % NH + 1) * HD], None)
            dve.wait_ge(cols_out, 1)
            scale = P ** -0.5
            for i in range(BH * NT + 1):
                if i < BH * NT:
                    h, s = divmod(i, NT)
                    w = T - s * P
                    dve.wait_ge(mrow_out, h + 1)
                    if i >= 2:
                        dve.wait_ge(decay_ready, i - 1)
                    v.tensor_tensor(wdiag[:, i % 2, :], mrow[:, h % 2, s * P:(s + 1) * P],
                                    const[:, C_TRI:C_TRI + P], ALU.add).then_inc(diag_ready, 1)
                if i >= 1:
                    n = i - 1
                    h, s = divmod(n, NT)
                    w = T - s * P
                    dve.wait_ge(decay_ready, n + 1)
                    dve.wait_ge(lqk_done, n + 1)
                    if h >= 2:
                        dve.wait_ge(lpv_done, h - 1)
                    v.scalar_tensor_tensor(out=wqk[:, h % 2, s, 0:w], in0=bank[n % 2][:, 0:w], scalar=scale,
                                           in1=wdec[:, n % 2, 0:w], op0=ALU.mult, op1=ALU.mult).then_inc(lqk_ready, 1)
                if i >= 1 and (i - 1) % NT == NT - 1:
                    h = (i - 1) // NT
                    dve.wait_ge(lpv_done, h + 1)
                    for t in range(NT):
                        o = bank[2 + t // 2][:, (t % 2) * 256:(t % 2) * 256 + P + 1]
                        d = den[:, 32 + t * BH + h:33 + t * BH + h]
                        link(v.tensor_scalar(d, o[:, P:P + 1], -1.0, tcol[:, 16 + t * BH + h:17 + t * BH + h],
                                             ALU.mult, ALU.max))
                        link(v.tensor_tensor(d, o[:, P:P + 1], d, ALU.max))
                        link(v.reciprocal(d, d))
                        v.tensor_scalar(hb_tok[:, t, h * P:(h + 1) * P], o[:, 0:P], d, None,
                                        ALU.mult).then_inc(lnum_out, 1)
            dve.wait_ge(turned, 10)
            dve.wait_ge(lnum_out, BH * NT)
            link(v.tensor_tensor(hsq, hb_tok, hb_tok, ALU.mult))
            v.tensor_reduce(den[:, 0:16], hsq.rearrange("p t (h d) -> p (t h) d", h=BH), AX.X, ALU.add).then_inc(hb_sq, 1)
            dve.wait_ge(hb_rms, 1)
            link(v.reciprocal(den[:, 0:16], den[:, 16:32]))
            for n in range(16):
                t, h = divmod(n, BH)
                o = hb_tok[:, t, h * P:(h + 1) * P]
                v.tensor_scalar(o, o, den[:, n:n + 1], None, ALU.mult).then_inc(hb_ready, 1)
            for c in range(4):
                dve.wait_ge(turned, 10 + c + 1)
                v.scalar_tensor_tensor(out=ybT[:, c, :], in0=bank[2 + c % 2][:, :], scalar=sm("mlstm_g", c),
                                       in1=sig_o[:, c, :], op0=ALU.mult, op1=ALU.mult).then_inc(yb_out, 1)
            for m in range(KD):
                j = first["branch"] + 4 * m
                for g in range(2):
                    dve.wait_ge(evac_act, taken(j + 2 * g)[1])
                    dve.wait_ge(proj_done, j + 2 * g + 2)
                    v.tensor_tensor(gate_ab[:, 2 + g, :], bank[(j + 2 * g + 1) % 2][:, :], gate_ab[:, g, :],
                                    ALU.mult).then_inc(evac_dve, 1)
                dve.wait_ge(evac_dve, taken(j + 3)[1])
                v.tensor_tensor(y2T[:, m, :], gate_ab[:, 2, :], gate_ab[:, 3, :], ALU.add).then_inc(y2_ready, 1)
            for k in range(8):
                j = first["w_out2"] + k
                dve.wait_ge(proj_done, j + 1)
                v.scalar_tensor_tensor(out=xT[:, k, :], in0=bank[j % 2][:, :], scalar=mod[:, 16 + k:17 + k],
                                       in1=xT[:, k, :], op0=ALU.mult, op1=ALU.add).then_inc(evac_dve, 1)
            dve.wait_ge(evac_dve, taken(first["w_out2"] + 7)[1])
            norm(10, lambda k: xT[:, k, :], lambda k: hT[:, k, :], lambda k: gmod[:, 8 + k:9 + k],
                 shift=lambda k: mod[:, 24 + k:25 + k])
            for k in range(KD):
                dve.wait_ge(h_hi_ready, k + 1)
                v.tensor_tensor(h_split[:, 1, k, :], hT[:, k, :], h_split[:, 0, k, :],
                                ALU.subtract).then_inc(h_lo_ready, 1)

            def each(n, op):
                for g in range(n):
                    one = op(g)
                link(one)

            dve.wait_ge(score_out, 4 * NT)
            for t in range(NT):
                each(16, lambda g: v.max(s_top[:, g, 0:8], s_all[:, t, g, :]))
                each(16, lambda g: v.max_index(i_top[:, g, 0:8], s_top[:, g, 0:8], s_all[:, t, g, :]))
                each(16, lambda g: v.match_replace(s_left[:, g, :], s_top[:, g, 0:8], s_all[:, t, g, :], -3.0e38))
                each(16, lambda g: v.max(s_top[:, g, 8:16], s_left[:, g, :]))
                each(16, lambda g: v.max_index(i_top[:, g, 8:16], s_top[:, g, 8:16], s_left[:, g, :]))
                tops = s_top.rearrange("p (h b) k -> p h b k", b=2)
                shape = [P, PH, TOPK, TOPK]
                for h in range(PH):
                    one = v.tensor_tensor(cand[:, h], tops[:, h, 0, :].unsqueeze(2).to_broadcast([P, TOPK, TOPK]),
                                          tops[:, h, 1, :].unsqueeze(1).to_broadcast([P, TOPK, TOPK]), ALU.add)
                link(one)
                flat = lambda c, h: c[:, h].rearrange("p a b -> p (a b)")
                each(PH, lambda h: v.max(best[:, h, 0:8], flat(cand, h)))
                each(PH, lambda h: v.max_index(c_top[:, h, 0:8], best[:, h, 0:8], flat(cand, h)))
                each(PH, lambda h: v.match_replace(flat(cand_left, h), best[:, h, 0:8], flat(cand, h), -3.0e38))
                each(PH, lambda h: v.max(best[:, h, 8:16], flat(cand_left, h)))
                each(PH, lambda h: v.max_index(c_top[:, h, 8:16], best[:, h, 8:16], flat(cand_left, h)))
                link(v.tensor_tensor(expd[:, t].rearrange("p (h k) -> p h k", h=PH), best,
                                     best[:, :, 0:1].to_broadcast([P, PH, TOPK]), ALU.subtract))
                v.tensor_scalar(c_hi, c_top, 4, None, ALU.logical_shift_right)
                link(v.tensor_scalar(c_lo, c_top, 15, None, ALU.bitwise_and))
                v.tensor_copy(a_f, c_hi)
                v.tensor_copy(b_f, c_lo)
                link(v.tensor_copy(i_topf, i_top))
                for half, rank in ((0, a_f), (1, b_f)):
                    for h in range(PH):
                        one = v.tensor_tensor(eqs[:, h], rank[:, h, :].unsqueeze(2).to_broadcast([P, TOPK, TOPK]),
                                              iota[:, 0:TOPK].unsqueeze(1).to_broadcast([P, TOPK, TOPK]), ALU.is_equal)
                    link(one)
                    for h in range(PH):
                        one = v.tensor_tensor(eqs[:, h], eqs[:, h],
                                              i_topf[:, 2 * h + half, :].unsqueeze(1).to_broadcast([P, TOPK, TOPK]),
                                              ALU.mult)
                    link(one)
                    one = v.tensor_reduce(chosen[:, t, half * P:(half + 1) * P],
                                          eqs.rearrange("p h k a -> p (h k) a"), AX.X, ALU.add)
                    if t == NT - 1 and half:
                        one.then_inc(best_ready, 1)
                    else:
                        link(one)
            dve.wait_ge(best_exp, 1)
            by_head = lambda a: a.rearrange("p (h k) -> p h k", h=PH)
            for t in range(NT):
                one = v.tensor_reduce(gsum[:, 0, t, :], by_head(expd[:, t]), AX.X, ALU.add)
            link(one)
            link(v.reciprocal(gsum[:, 1], gsum[:, 0]))
            for t in range(NT):
                v.tensor_tensor(by_head(chosen[:, t, 2 * P:3 * P]), by_head(expd[:, t]),
                                gsum[:, 1, t, :].unsqueeze(2).to_broadcast([P, PH, TOPK]),
                                ALU.mult).then_inc(chosen_ready, 1)
            for t in range(NT):
                dve.wait_ge(chosen_turned, t + 1)
                v.tensor_copy(chosenT[:, :, t * P:(t + 1) * P],
                              bank[4 + t % 2][:, 0:3 * P].rearrange("p (a b) -> p a b", a=3)).then_inc(chosen_out, 1)
            dve.wait_ge(chosen_out, NT)

            def one_hots(i):
                many = JB * TT
                wait(dve, hot_ready, i * (2 * many))
                v.tensor_copy(cur, chosenT[:, :, bass.ds(i * many, many)]).then_inc(cur_ready, 1)
                dve.wait_ge(cur_ready, i + 1)
                for t in range(many):
                    wait(dve, hot_used, i * many + t - HOT + 1)
                    v.tensor_scalar(hot1[:, t % HOT, :], iota, cur[:, 0, t:t + 1], None,
                                    ALU.is_equal).then_inc(hot_ready, 1)
                    v.tensor_scalar(hot2[:, t % HOT, :], iota, cur[:, 1, t:t + 1], cur[:, 2, t:t + 1],
                                    ALU.is_equal, ALU.mult).then_inc(hot_ready, 1)

            one_hots(0)
            with dve.Fori(1, SPREAD) as i:
                one_hots(i)

            def weigh(e, i=0):
                b, j = divmod(e, JB)
                if j == 0:
                    dve.wait_ge(g_loaded[b % 2], i * 16 + 16 * (b // 2 + 1))
                dve.wait_ge(act_loaded[e % AS], i * (16 * 2 * JB // AS) + 16 * (e // AS + 1))
                wait(dve, p_lo_ready, i * (2 * JB) + e - 1)
                v.tensor_tensor(weighed[:, e % 2, :], act_in[:, e % AS, :], gblk[:, b % 2, :, j],
                                ALU.mult).then_inc(weighed_ready, 1)

            def weighted_low(e, i=0):
                dve.wait_ge(p_hi_ready, i * (2 * JB) + e + 1)
                v.tensor_tensor(p_split[:, e % PS, 1, :], weighed[:, e % 2, :], p_split[:, e % PS, 0, :],
                                ALU.subtract).then_inc(p_lo_ready, 1)

            def second(b, i=0):
                for e in range(b * JB, (b + 1) * JB):
                    if e + 1 < NE:
                        weigh(e + 1, i)
                    weighted_low(e, i)

            weigh(0)
            for b in range(2):
                second(b)
            with dve.Fori(0, NB // 2 - 2) as i:
                second(2, i)
                second(3, i)
            for b in range(NB - 2, NB):
                second(b)
            dve.wait_ge(expert_done, 2 * NE)
            for k in (7, 0, 1, 2, 3, 4, 5, 6):
                v.scalar_tensor_tensor(out=xT[:, k, :], in0=bank[k][:, :], scalar=mod[:, 40 + k:41 + k],
                                       in1=xT[:, k, :], op0=ALU.mult, op1=ALU.add).then_inc(x3_ready, 1)
            dve.wait_ge(x3_ready, KD)
            norm(11, lambda k: xT[:, k, :], lambda k: hT[:, k, :], lambda k: sm("final_g", k))

        @block.tensor
        def _(pe):
            mm = nc.tensor.matmul
            tile = [0]
            job = [0]
            held = [0]

            def weight():
                n = tile[0]
                tile[0] += 1
                pe.wait_ge(tile_loaded[n % RING], 16 * (n // RING + 1))
                return ring[:, n % RING, :]

            def norm(idx, free=T):
                for k in range(NORMS[idx]):
                    n = norm_base[idx] + k
                    pe.wait_ge(sq_ready, n + 1)
                    if k == 0 and idx:
                        pe.wait_ge(rms_ready, idx)
                    mm(bank[7][:, 0:free], ones, sq[:, n % 2, 0:free], start=(k == 0),
                       stop=(k == NORMS[idx] - 1)).then_inc(sq_summed, 1)

            def project(chunks, m=P, n=T, used=1, ready=None):
                j = job[0]
                job[0] += 1
                if j >= 2:
                    s, value = taken(j - 2)
                    pe.wait_ge(s, value)
                for k, (lhsT, rhs) in enumerate(chunks):
                    if ready:
                        ready(k)
                    last = mm(bank[j % 2][0:m, 0:n], lhsT, rhs, start=(k == 0), stop=(k == len(chunks) - 1))
                    if k == 0:
                        release_held(last)
                last.then_inc(proj_done, 1)
                if used:
                    release(used)

            def release(n):
                held[0] += n

            def release_held(ins):
                if held[0]:
                    ins.then_inc(tiles_used, held[0])
                held[0] = 0

            def after_norm(idx):
                return lambda k: pe.wait_ge(normed, norm_base[idx] + k + 1)

            def dense(count, src, kd=KD, ready=None, n=T):
                for m in range(count):
                    w = weight()
                    project([(w[:, k * P:(k + 1) * P], src[:, k, :]) for k in range(kd)], n=n,
                            ready=ready if m == 0 else None)

            def token_major(src, n, tiles=NT, per=2):
                width = D // per
                w = [weight() for _ in range(KD // per)]
                for t in range(tiles):
                    project([(src[:, k, t * P:(t + 1) * P], w[k // per][:, (k % per) * width:(k % per) * width + n])
                             for k in range(KD)], n=n, used=0 if t < tiles - 1 else KD // per)

            def attend(u0, units, q, k, width, pieces, vals):
                for i in range(units + 2):
                    if i < units:
                        u = u0 + i
                        if u >= 2:
                            pe.wait_ge(logits_ready, u - 1)
                        mm(bank[u % 2][:, 0:width(i)], q(i), k(i), start=True, stop=True).then_inc(qk_done, 1)
                    if 1 <= i <= units:
                        n, u = i - 1, u0 + i - 1
                        pe.wait_ge(prob_ready, u + 1)
                        if u >= 2:
                            pe.wait_ge(probT_ready, u - 1)
                        for c, w in enumerate(pieces(n)):
                            last = nc.tensor.transpose(bank[2 + u % 2][0:w, c * P:(c + 1) * P],
                                                       prob[:, u % 2, c * P:c * P + w], ident)
                        last.then_inc(prob_turned, 1)
                    if i >= 2:
                        n, u = i - 2, u0 + i - 2
                        pe.wait_ge(probT_ready, u + 1)
                        if u >= 2:
                            pe.wait_ge(head_out, u - 1)
                        parts = pieces(n)
                        for c, w in enumerate(parts):
                            last = mm(bank[4 + u % 2][:, 0:HD], probT[0:w, u % 2, c * P:(c + 1) * P], vals(n, c),
                                      start=(c == 0), stop=(c == len(parts) - 1))
                        last.then_inc(pv_done, 1)

            def turn_chosen(t):
                pe.wait_ge(chosen_ready, t + 1)
                wait(pe, chosen_out, t - 1)
                for n in range(3):
                    last = nc.tensor.transpose(bank[4 + t % 2][:, n * P:(n + 1) * P], chosen[:, t, n * P:(n + 1) * P], ident)
                last.then_inc(chosen_turned, 1)

            def turn(n0, count, src, out_sem=None):
                for c in range(count):
                    if out_sem is not None:
                        wait(pe, out_sem, c - 1)
                    elif n0 + c >= 2:
                        pe.wait_ge(turned_out, n0 + c - 1)
                    for t in range(NT):
                        last = nc.tensor.transpose(bank[2 + c % 2][:, t * P:(t + 1) * P],
                                                   src[:, t, c * P:(c + 1) * P], ident)
                    last.then_inc(turned, 1)

            pe.wait_ge(consts_in_sem, 32)
            norm(0)
            dense(8, hT, ready=after_norm(0))
            token_major(hT, 408)
            dense(12, hT)
            s_, val = taken(first["qk"] + 5)
            pe.wait_ge(s_, val)
            for kv in range(2):
                w = [weight() for _ in range(4)]
                for g in range(2):
                    rows_ = slice(g * HD, (g + 1) * HD)
                    for j in range(32):
                        w1 = w[j // 8][rows_, (j % 8) * P:(j % 8 + 1) * P]
                        one = mm(bank[6 - g][:, kv * 128 + g * 32:kv * 128 + g * 32 + NCMP], w1,
                                 qk[rows_, 4 + kv, j:j + 16 * (NCMP - 1) + 1:16], start=(j == 0), stop=(j == 31))
                        release_held(one)
                for j in range(32):
                    w1 = w[j // 8][0:HD, (j % 8) * P:(j % 8 + 1) * P]
                    last = mm(bank[6][:, kv * 128 + 64:kv * 128 + 65], w1, small[0:HD, SMALL["pe"][0] + j:SMALL["pe"][0] + j + 1],
                              start=(j == 0), stop=(j == 31))
                last.then_inc(cmp_hidden, 1)
                release(4)
                pe.wait_ge(cmp_gelu, 2 * kv + 2)
            for g in range(2):
                mm(bank[2][:, 0:NCMP], sm("w2k", g * P, P), hid[:, 0, g, 0:NCMP], start=(g == 0), stop=(g == 1))
            for g in range(2):
                last = mm(bank[2][0:NCMP, 128 + g * HD:128 + (g + 1) * HD], hid[:, 1, g, 0:NCMP], sm("w2v", 0, HD),
                          start=True, stop=True)
            last.then_inc(cmp_kv, 1)

            def nsa_q(i):
                br, t, h = nsa_unit(i)
                g = h // 4
                return qk[g * HD:(g + 1) * HD, h % 4, t * P:(t + 1) * P]

            def nsa_k(i):
                br, t, h = nsa_unit(i)
                g = h // 4
                if br == 2:
                    return kcmp[g * HD:(g + 1) * HD, 0:NCMP]
                lo = 0 if br == 0 else max(t - 2, 0)
                return qk[g * HD:(g + 1) * HD, 6 + br, lo * P:(t + 1) * P]

            def nsa_v(i, c):
                br, t, h = nsa_unit(i)
                g = h // 4
                if br == 2:
                    return vcmp[0:NCMP, g * HD:(g + 1) * HD]
                lo = 0 if br == 0 else max(t - 2, 0)
                a0 = (0, 256)[br] + g * HD
                return vtok[:, lo + c, a0:a0 + HD]

            for s_, val in (taken(first["conv"] - 1), taken(first["conv"] + 11)):
                pe.wait_ge(s_, val)
            pe.wait_ge(cmp_done, 2)
            attend(0, 96, nsa_q, nsa_k, nsa_width, nsa_pieces, nsa_v)
            pe.wait_ge(head_out, 96)
            turn(0, 4, o_tok)
            norm(1)
            norm(2)
            for m in range(8):
                w = weight()
                project([(w[:, k * P:(k + 1) * P], merged[:, k, :]) for k in range(8)],
                        ready=(lambda k: pe.wait_ge(normed, norm_base[1] + k + 1)) if m == 0 else None)
            norm(3)
            norm(4)
            norm(5, NM)
            dense(2, hT, ready=after_norm(4))
            dense(2, mT, ready=after_norm(5), n=NM)
            token_major(mT, NM, tiles=2, per=4)
            s_, val = taken(first["mv"] + 1)
            pe.wait_ge(s_, val)
            attend(96, 16, lambda i: mq[(i % 2) * HD:(i % 2 + 1) * HD, (i % MH) // 2, (i // MH) * P:(i // MH + 1) * P],
                   lambda i: mk[(i % 2) * HD:(i % 2 + 1) * HD, (i % MH) // 2, :], lambda i: NM,
                   lambda i: [P, P], lambda i, c: mv[:, c, (i % MH) * HD:(i % MH + 1) * HD])
            pe.wait_ge(head_out, 96 + 16)
            turn(4, 2, om_tok)
            pe.wait_ge(turned_out, 6)
            for half in range(2):
                w = weight()
                for m in range(4):
                    project([(w[:, m * 256 + k * P:m * 256 + (k + 1) * P], omT[:, k, :]) for k in range(2)],
                            used=1 if m == 3 else 0)
            norm(6)
            norm(7)
            pe.wait_ge(cond_ready, 1)

            def ada(m):
                w = weight()
                for k in range(KD):
                    last = mm(bank[6][:, m:m + 1], w[:, k * P:(k + 1) * P], condT[:, k:k + 1],
                              start=(k == 0), stop=(k == KD - 1))
                    if k == 0:
                        release_held(last)
                release(1)
                return last

            for m in range(KF):
                for _ in range(2):
                    w = weight()
                    project([(w[:, k * P:(k + 1) * P], hT[:, k, :]) for k in range(KD)],
                            ready=after_norm(7) if m == 0 and _ == 0 else None)
                ada(2 * m)
                ada(2 * m + 1)
            for m in range(2 * KF, 48):
                last = ada(m)
            last.then_inc(ada_done, 1)
            s_, val = taken(first["ffn"] + 2 * KF - 1)
            pe.wait_ge(s_, val)
            for m in range(8):
                w = [weight() for _ in range(3)]
                project([(w[k // 8][:, (k % 8) * P:(k % 8 + 1) * P], ff[:, k, :]) for k in range(KF)], used=3)
            norm(8)
            norm(9)
            dense(8, hT, ready=after_norm(9))
            dense(8, hT)
            w = weight()
            for n in range(2):
                project([(w[:, k * P + BH * n:k * P + BH * (n + 1)], hT[:, k, :]) for k in range(KD)], m=BH, used=n)
            dense(4, hT)
            token_major(hT, T)
            token_major(hT, T)
            pe.wait_ge(rows_m, 1)
            pe.wait_ge(rows_exp, 1)
            for src, c0 in ((row_b, 0), (row_f, 16)):
                for t in range(NT):
                    last = nc.tensor.transpose(bank[6][:, c0 + t * BH:c0 + (t + 1) * BH],
                                               src[:, t * P:(t + 1) * P], const[0:BH, C_ID:C_ID + BH])
            last.then_inc(cols_done, 1)
            s_, val = taken(first["vb"] + 3)
            pe.wait_ge(s_, val)
            attend(112, 32, lambda i: qk2[(i % 2) * HD:(i % 2 + 1) * HD, (i % NH) // 2, (i // NH) * P:(i // NH + 1) * P],
                   lambda i: qk2[(i % 2) * HD:(i % 2 + 1) * HD, 4 + (i % NH) // 2, 0:(i // NH + 1) * P],
                   lambda i: P * (i // NH + 1), lambda i: [P] * (i // NH + 1),
                   lambda i, c: va[:, c, (i % NH) * HD:(i % NH + 1) * HD])
            pe.wait_ge(head_out, UNITS)
            pe.wait_ge(conv2_ready, 8)
            def m_row(h):
                wait(pe, mrow_out, h - 1)
                mm(bank[4 + h % 2][:, :], const[0:BH, C_SEL + h * P:C_SEL + (h + 1) * P], row_i,
                   start=True, stop=True).then_inc(mrow_done, 1)

            m_row(0)
            for h in range(BH):
                if h + 1 < BH:
                    m_row(h + 1)
                for s in range(NT):
                    n = h * NT + s
                    if n >= 2:
                        pe.wait_ge(lqk_ready, n - 1)
                    mm(bank[n % 2][:, 0:T - s * P], cv2[:, 4 + h, s * P:(s + 1) * P], cv2[:, h, s * P:T],
                       start=True, stop=True).then_inc(lqk_done, 1)
                pe.wait_ge(lqk_ready, (h + 1) * NT)
                if h:
                    pe.wait_ge(lnum_out, h * NT)
                for t in range(NT):
                    for s in range(t + 1):
                        last = mm(bank[2 + t // 2][:, (t % 2) * 256:(t % 2) * 256 + P + 1],
                                  wqk[:, h % 2, s, (t - s) * P:(t - s + 1) * P], vb[:, s, h, :],
                                  start=(s == 0), stop=(s == t))
                last.then_inc(lpv_done, 1)
            pe.wait_ge(lnum_out, BH * NT)
            turn(6, 4, oa_tok)
            pe.wait_ge(hb_ready, 16)
            pe.wait_ge(turned_out, 10)
            turn(10, 4, hb_tok, yb_out)
            pe.wait_ge(yb_out, 4)
            for m in range(KD):
                wa, wb, wab = weight(), weight(), weight()
                project([(wa[:, k * P:(k + 1) * P], hT[:, k, :]) for k in range(KD)], used=0)
                project([(wab[:, k * P:(k + 1) * P], yaT[:, k, :]) for k in range(4)], used=0)
                project([(wb[:, k * P:(k + 1) * P], hT[:, k, :]) for k in range(KD)], used=0)
                project([(wab[:, (4 + k) * P:(5 + k) * P], ybT[:, k, :]) for k in range(4)], used=3)
            pe.wait_ge(y2_ready, KD)
            dense(8, y2T)
            norm(10)
            dense(16, hT, ready=after_norm(10))
            keys = [weight(), weight()]
            s_, val = taken(first["pq"] + 15)
            pe.wait_ge(s_, val)
            for t in range(NT):
                for q in range(4):
                    if t:
                        pe.wait_ge(score_out, 4 * (t - 1) + q + 1)
                    for j in range(4 * q, 4 * q + 4):
                        last = mm(bank[2 + q][:, (j % 4) * P:(j % 4 + 1) * P], pq[:, j, t * P:(t + 1) * P],
                                  keys[j // 8][:, (j % 8) * P:(j % 8 + 1) * P], start=True, stop=True)
                    last.then_inc(score_done, 1)
            release(2)

            def products(out_bank, w, x, start=True, stop_=True):
                mm(out_bank, w[0], x[0], start=start, stop=False)
                mm(out_bank, w[0], x[1], start=False, stop=False)
                return mm(out_bank, w[1], x[0], start=False, stop=stop_)

            def up(e, i=0):
                wait(pe, gelu_ready, i * JB + e - 1)
                pe.wait_ge(w_lo_ready, i * JB + e + 1)
                for k in range(KD):
                    w = [w_split[:, e % 2, part, k * P:(k + 1) * P] for part in range(2)]
                    x = [h_split[:, part, k, :] for part in range(2)]
                    if e == 0 and k == 0:
                        release_held(mm(bank[0][:, :], w[0], x[0], start=True, stop=False))
                        mm(bank[0][:, :], w[0], x[1], start=False, stop=False)
                        mm(bank[0][:, :], w[1], x[0], start=False, stop=False)
                        continue
                    last = products(bank[e % 2][:, :], w, x, k == 0, k == KD - 1)
                last.then_inc(expert_done, 1)

            pe.wait_ge(h_lo_ready, KD)
            for e in range(JB):
                up(e)
            with pe.Fori(0, CHOICE - 1) as i:
                for e in range(JB, 2 * JB):
                    up(e, i)
            for e in range(CHOICE * JB, (CHOICE + 1) * JB):
                up(e)
            for t in range(NT):
                turn_chosen(t)

            def spread(n, i):
                wait(pe, staged, i * (JB * TT // 4) + n - 3)
                for t in range(4 * n, 4 * n + 4):
                    pe.wait_ge(hot_ready, i * (2 * JB * TT) + 2 * (t + 1))
                    mm(bank[2 + n % 4][:, (t % 4) * P:(t % 4 + 1) * P], hot1[:, t % HOT, :], hot2[:, t % HOT, :],
                       start=True, stop=True).then_inc(hot_used, 1)

            def spread_block(i):
                for j in range(JB):
                    up((CHOICE + 1) * JB + j, i)
                    for n in range(j * TT // 4, (j + 1) * TT // 4):
                        spread(n, i)

            spread_block(0)
            with pe.Fori(1, SPREAD) as i:
                spread_block(i)

            def down(e, i=0):
                pe.wait_ge(w_lo_ready, i * (2 * JB) + NE + e + 1)
                pe.wait_ge(p_lo_ready, i * (2 * JB) + e + 1)
                for k in (2, 3, 4, 5, 6, 7, 0, 1):
                    if e == 0 and k == 0:
                        pe.wait_ge(gelu_ready, NE)
                    last = products(bank[k][:, :], [w_split[:, e % 2, part, k * P:(k + 1) * P] for part in range(2)],
                                    [p_split[:, e % PS, part, :] for part in range(2)], e == 0, e == NE - 1)
                last.then_inc(expert_done, 1)

            pe.wait_ge(staged, T // 4)
            for e in range(2 * JB):
                down(e)
            with pe.Fori(0, NB // 2 - 2) as i:
                for e in range(2 * JB, 4 * JB):
                    down(e, i)
            for e in range(NE - 2 * JB, NE):
                down(e)
            norm(11)


def kernel(**inputs):
    import numpy as _np
    import concourse.bacc as _bacc
    from concourse import mybir as _mybir
    from concourse.bass_utils import run_bass_kernel_spmd as _run

    i = {k: _np.asarray(v) for k, v in inputs.items()}
    sel, win, cmp, band = biases(i)
    arrays = {
        "weights": weight_stream(i),
        "x_t": i["x"][0].T.reshape(KD, P, T),
        "mem_t": i["mem"][0].T.reshape(KD, P, NM),
        "smalls": smalls(i), "consts": constants(),
        "bias_sel": sel, "bias_win": win, "bias_cmp": cmp, "bias_band": band,
    }
    arrays = {k: _np.ascontiguousarray(v) for k, v in arrays.items()}
    nc = _bacc.Bacc("TRN2", target_bir_lowering=False, num_devices=1)
    args = [nc.dram_tensor(k, v.shape, _mybir.dt.from_np(v.dtype), kind="ExternalInput").ap()
            for k, v in arrays.items()]
    result = nc.dram_tensor("out_t", (KD, P, T), _mybir.dt.float32, kind="ExternalOutput").ap()
    build(nc, *args, result)
    r = _run(nc, [arrays], core_ids=[0])
    got = r.results[0]["out_t"]
    return _np.ascontiguousarray(_np.asarray(got).reshape(D, T).T).reshape(1, T, D)
```

```python
from contextlib import ExitStack
import math

import numpy as np

import concourse.bass as bass
from concourse import mybir

F32 = mybir.dt.float32
F32R = mybir.dt.float32r
U32 = mybir.dt.uint32
ALU = mybir.AluOpType
ACT = mybir.ActivationFunctionType
AX = mybir.AxisListType

P = 128
T = 512
NT = T // P
D = 1024
KD = D // P
NH, HD = 8, 64
NCMP = 31
NM = 256
MH = 4
FH = 2816
KF = FH // P
BH = 4
RING = 4
ARENA = 28400
PH = 8
TOPK = 16
NE = 128
JB = 8
NB = NE // JB
CHOICE = 7
SPREAD = 8
QUADS = (4, 3, 3, 3, 3, 0, 0, 0)
TB = T // SPREAD
GT = 16
HOT = 16
AS = 4
PS = 4
EPS = 1e-6
BIG = 1e30
QS = -0.125


SMALL = {}


def small_columns():
    at = 0
    for name, n in [("norm0", 8), ("norm1", 8), ("norm2", 8), ("norm3", 8), ("norm4", 8), ("norm5", 8),
                    ("mem_norm", 8), ("gn_nsa", 4), ("gn_conv", 4), ("conv_w", 12), ("b_ada", 48),
                    ("norm1_2", 8), ("conv_w2", 32), ("conv_b2", 8), ("mlstm_g", 4), ("norm2_2", 8),
                    ("final_g", 8), ("cond", 8), ("pe", 32), ("b_if", 2),
                    ("w2k", 256), ("w2v", 64)]:
        SMALL[name] = (at, n)
        at += n
    return at


N_SMALL = small_columns()

C_ID, C_ONE, C_IOTA, C_SEL, C_TRI, C_ROW = 0, 128, 256, 384, 896, 1024
N_CONST = 1025


def constants():
    c = np.zeros((P, N_CONST), np.float32)
    c[:, C_ID:C_ID + P] = np.eye(P)
    c[:, C_ONE:C_ONE + P] = 1.0
    c[:, C_IOTA:C_IOTA + P] = np.arange(P)
    for h in range(BH):
        c[h, C_SEL + h * P:C_SEL + (h + 1) * P] = 1.0
    s, t = np.meshgrid(np.arange(P), np.arange(P), indexing="ij")
    c[:, C_TRI:C_TRI + P] = np.where(s > t, BIG, 0.0)
    c[:, C_ROW] = np.arange(P) >= 31
    return c


def cols(v):
    return np.reshape(v, (-1, P)).T


def tile_k(w):
    k, n = w.shape
    return w.reshape(k // P, P, n // P, P).transpose(2, 1, 0, 3).reshape(n // P, P, -1)


def padded(tiles):
    return np.pad(tiles, ((0, 0), (0, 0), (0, D - tiles.shape[2])))


def token_tiles(w):
    return w.reshape(4, 2, P, 512).transpose(0, 2, 1, 3).reshape(4, P, 1024)


def weight_stream(i):
    w_in = i["w_in"][0]
    heads = np.concatenate([np.r_[h * HD:(h + 1) * HD, (h + 4) * HD:(h + 5) * HD] for h in range(4)])
    out = [tile_k(w_in[:, heads])]
    for c in (512, 640, 768, 1024):
        out.append(tile_k(w_in[:, c:c + 128]))
    out.append(token_tiles(np.pad(w_in[:, 896:1304], ((0, 0), (0, 104)))))
    for j in range(4):
        for c in (1816, 2328, 1304):
            out.append(tile_k(w_in[:, c + j * P:c + (j + 1) * P]))
    for w in (i["cmp_k_w1"][0], i["cmp_v_w1"][0]):
        one = w.reshape(4, 8, HD, P).transpose(0, 2, 1, 3).reshape(4, HD, 1024)
        out.append(np.concatenate([one, one], axis=1))
    out.append(tile_k(i["w_out"][0]))
    out.append(tile_k(i["mem_wkv"][0][:, :256]))
    out.append(i["mem_wkv"][0][:, 256:].reshape(2, 4, P, 256).transpose(0, 2, 1, 3).reshape(2, P, 1024))
    out.append(tile_k(i["mem_wq"][0]))
    out.append(tile_k(i["mem_wo"][0]).reshape(2, 4, P, 256).transpose(0, 2, 1, 3).reshape(2, P, 1024))
    wg, wu = tile_k(i["ffn_wg"][0]), tile_k(i["ffn_wu"][0])
    ada = i["w_ada_2"][0].reshape(KD, P, 6, D).transpose(2, 0, 1, 3).reshape(6 * KD, P, D)
    for m in range(KF):
        out += [wg[m:m + 1], wu[m:m + 1], ada[ADA_AT[m]:ADA_AT[m + 1]]]
    wd = tile_k(i["ffn_wd"][0])
    out.append(np.pad(wd, ((0, 0), (0, 0), (0, 256))).reshape(8, P, 3, 1024).transpose(0, 2, 1, 3).reshape(24, P, 1024))
    w2 = i["w_in_2"][0]
    out.append(tile_k(w2[:, 0:1024]))
    out.append(tile_k(w2[:, 1536:2560]))
    for c in (3584, 3588):
        out.append(tile_k(np.pad(w2[:, c:c + BH], ((0, 0), (0, P - BH)))))
    out.append(tile_k(w2[:, 3072:3584]))
    out.append(token_tiles(w2[:, 1024:1536]))
    out.append(token_tiles(w2[:, 2560:3072]))
    ga, gb = tile_k(w2[:, 3592:4616]), tile_k(w2[:, 4616:5640])
    ab = np.concatenate([tile_k(i["w_branch_a_2"][0]), tile_k(i["w_branch_b_2"][0])], axis=2)
    for m in range(KD):
        out += [ga[m:m + 1], ab[m:m + 1], gb[m:m + 1]]
    out.append(tile_k(i["w_out_2"][0]))
    out.append(tile_k(i["w_peer_q_2"][0]))
    keys = i["peer_sub_keys_2"][0].reshape(2, 8, P, P)
    out.append(keys.transpose(0, 3, 1, 2).reshape(2, P, 1024))
    u = i["peer_u_2"][0].reshape(P, P, KD, P).transpose(1, 3, 2, 0).reshape(P, P, 1024)
    v = i["peer_v_2"][0].reshape(P, P, D).transpose(1, 0, 2)
    out += [u, v]
    return np.concatenate(out, axis=0)


ADA = [3] * 4 + [2] * (KF - 4)
ADA_AT = [sum(ADA[:m]) for m in range(KF + 1)]
KINDS = ("S" * 24 + "R" * 8 + "S" * (8 + 8) + "SSAAA" * 4 + "SSAA" * (KF - 4) + "S" * 24
         + "S" * (8 + 8 + 2 + 4 + 4 + 4) + "SSS" * KD + "S" * (8 + 16) + "RR")


def buckets(n):
    large = 16 + np.floor(np.log(np.maximum(n, 1) / 16) / math.log(8) * 16 + 1e-9).astype(np.int64)
    return np.where(n < 16, n, np.minimum(large, 31))


def spread(table, index, keep):
    out = np.full((table.shape[0],) + index.shape, -BIG, np.float32)
    out[:, keep] = table[:, index[keep]]
    return np.moveaxis(out, 0, 1).reshape(P, -1)


def biases(i):
    r = np.arange(P)[:, None]
    dist = 384 + r - np.arange(T)[None, :]
    near = buckets(np.maximum(dist, 0))
    sel = spread(i["rel_bias"], near, dist >= 0)
    win = spread(i["rel_bias"], near[:, 128:], ((dist >= 0) & (dist < 256))[:, 128:])
    back = np.arange(T).reshape(NT, P).T[:, :, None] - (16 * np.arange(32) + 31)[None, None, :]
    cmp = spread(i["rel_bias"], buckets(np.maximum(back, 0)), back >= 0)
    rel = np.clip(dist, -128, 128) + 128
    band = spread(i["rel_bias_2"][0], rel, ~((r < 64) & (dist < r - 63)))
    return sel, win, cmp, band


def smalls(i):
    a = {"norm%d" % n: cols(i["norms"][0, n]) for n in range(6)}
    a |= {"mem_norm": cols(i["mem_norm"]), "gn_nsa": cols(i["gn_nsa"]), "gn_conv": cols(i["gn_conv"]),
          "conv_w": cols(i["conv_w"]), "b_ada": cols(i["b_ada_2"]), "norm1_2": cols(i["norm1_g_2"]),
          "conv_w2": cols(i["conv_w_2"]), "conv_b2": cols(i["conv_b_2"]), "mlstm_g": cols(i["mlstm_norm_g_2"]),
          "norm2_2": cols(i["norm2_g_2"]), "final_g": cols(i["final_g_2"]), "cond": cols(i["c_2"])}
    a["pe"] = np.concatenate([i["cmp_pe"][0].T] * 2, axis=0)
    a["b_if"] = np.pad(np.stack([i["b_igate_2"][0], i["b_fgate_2"][0]], 1), ((0, P - BH), (0, 0)))
    w2k, none = i["cmp_k_w2"][0], np.zeros((P, HD), np.float32)
    a["w2k"] = np.concatenate([w2k, none, none, w2k], axis=1)
    a["w2v"] = i["cmp_v_w2"][0]
    return np.concatenate([a[n] for n in SMALL], axis=1)




def build(nc, weights, x_in, mem_in, smalls_in, consts_in, sel_in, win_in, cmp_in, band_in, out):
    ctx = ExitStack()
    with ctx:
        def sb(name, shape, dt=F32):
            return ctx.enter_context(nc.sbuf_tensor(name, shape, dt))

        def sem(name):
            return ctx.enter_context(nc.semaphore(name))

        gates_dram = nc.dram_tensor("gates_spread", (NB, P, T, JB), F32, kind="Internal").ap()
        acts_dram = nc.dram_tensor("expert_acts", (NE, P, T), F32, kind="Internal").ap()

        ring = sb("ring", [P, RING, D])
        xT = sb("xT", [P, KD, T])
        w_split = sb("weight_split", [P, 2, 2, D], F32R)
        h_base = nc.sbuf_base + -nc.sbuf_base % 32
        hT = sb("hT", [P, 2 * KD, T])
        small = sb("small", [P, N_SMALL])
        const = sb("const", [P, N_CONST])
        sq = sb("sq", [P, 2, T])
        rms = sb("rms", [P, T])
        full = sb("full", [P, T])
        rstd = sb("rstd", [P, T])
        mod = sb("mod", [P, 48])
        condT = sb("condT", [P, 8])
        gmod = sb("gmod", [P, 16])
        eps = sb("eps", [P, 2])
        arena_base = nc.sbuf_base + -nc.sbuf_base % 32
        arena = sb("arena", [P, ARENA])

        def at(first, *dims):
            n = int(np.prod(dims))
            assert first + n <= ARENA, (first, dims)
            v = arena[:, first:first + n]
            names = " ".join("abcd"[:len(dims)])
            return v if len(dims) == 1 else v.rearrange(
                f"p ({names}) -> p {names}", **{"abcd"[k]: dims[k] for k in range(len(dims))})

        logit = at(0, 2, T)
        prob = at(1024, 2, T)
        probT = at(2048, 2, T)
        least = at(3072, 96)
        total = at(3168, 96)
        rgate = at(3264, 96)
        rrec = at(3360, 96)
        qk = at(3500, 8, T)
        vtok = at(7596, NT, 408)
        conv = at(9232, 12, T)
        o_tok = at(15376, NT, T)
        bias_sel = at(17424, NH, T)
        bias_win = at(21520, NH, 384)
        bias_cmp = at(24592, NH, NT, 32)
        hid = at(25616, 2, 2, 32)
        kcmp = at(25744, 32)
        vcmp = at(25776, P)
        gsig = at(25904, NT, 24)
        conv_y = at(26004, 2, T)
        placed = at(0, 4, T)
        hid_rows = at(2048, 4, P)
        def split(name, base, first, *dims):
            return nc.alloc_sbuf_tensor_at(name, [P] + list(dims), F32R, offset=base + 4 * first)

        h_split = split("h_split", h_base, 0, 2, KD, T)
        nT = at(17424, 4, T)
        conv_split = split("conv_split", arena_base, 9232, 4, 3, T)
        merged = split("merged_split", arena_base, 19472, 2, 8, T)
        yT = at(3500, 8, T)
        memT = at(0, KD, NM)
        m_split = split("mem_split", arena_base, 15376, 2, KD, NM)
        mq = at(13744, 2, T)
        mk = at(14768, 2, NM)
        mv = at(9232, 2, NM)
        om_tok = at(9744, NT, NM)
        om_split = split("memory_out_split", arena_base, 16816, 2, 2, T)
        ff_gate = at(0, 2, T)
        yF = at(1024, 8, T)
        ff_split = split("hidden_layer_split", arena_base, 5120, 2, KF, T)
        qk2 = at(3500, 8, T)
        cv2 = at(7596, 8, T)
        sig_o = at(11692, 4, T)
        va = at(13740, NT, T)
        vb = at(15788, NT, BH, P + 1)
        bias_band = at(17856, NH, T)
        oa_tok = at(21952, NT, T)
        hb_tok = at(24000, NT, T)
        conv_acc = at(24000, 2, T)
        ya_split = split("ya_split", arena_base, 17856, 2, 4, T)
        yb_split = split("yb_split", arena_base, 13744, 2, 4, T)
        y2_split = split("y2_split", arena_base, 3504, 2, 8, T)
        gate_ab = at(0, 4, T)
        rows = at(26048, 4, T)
        row_f, row_i, row_a, row_b = (rows[0:BH, n, :] for n in range(4))
        tcol = at(28096, 64)
        wdec = at(0, 2, T)
        wdiag = at(1024, 2, P)
        mrow = at(1280, 2, T)
        wqk = at(17856, 2, NT, T)
        den = at(28160, 64)
        hsq = at(21952, NT, T)
        pq = at(0, 16, T)
        s_left = at(0, 16, P)
        cand = at(2048, PH, TOPK, TOPK)
        cand_left = at(4096, PH, TOPK, TOPK)
        eqs = at(6144, PH, TOPK, TOPK)
        s_all = at(8192, NT, 16, P)
        kept = at(8192, NT, 16 * P)
        chosen = kept[:, :, 0:3 * P]
        expd = kept[:, :, 3 * P:4 * P]
        s_top = at(16384, 16, TOPK)
        i_topf = at(16640, 16, TOPK)
        best = at(16896, PH, TOPK)
        a_f = at(17024, PH, TOPK)
        b_f = at(17152, PH, TOPK)
        gsum = at(17280, 2, NT, PH)
        i_top = at(17344, 16, TOPK).bitcast(U32)
        c_top = at(17600, PH, TOPK).bitcast(U32)
        c_hi = at(17728, PH, TOPK).bitcast(U32)
        c_lo = at(17856, PH, TOPK).bitcast(U32)
        chosenT = at(17984, 3, T)
        cur = at(19520, 3, TB)
        hot1 = at(0, HOT, P)
        hot2 = at(2048, HOT, P)
        stage = at(4096, 2, NB, GT * JB)
        act = at(19800, 2, T)
        gblk = at(0, 2, T, JB)
        act_in = at(8192, AS, T)
        weighed = at(10240, 2, T)

        p_split = split("weighted_split", arena_base, 11264, PS, 2, T)

        bank = [ctx.enter_context(nc.psum_tensor(f"bank{n}", [P, T], F32)) for n in range(8)]
        ident = const[:, C_ID:C_ID + P]
        ones = const[:, C_ONE:C_ONE + P]
        iota = const[:, C_IOTA:C_IOTA + P]
        rowmask = const[:, C_ROW:C_ROW + 1]

        def sm(name, k=0, n=1, rows=P):
            a = SMALL[name][0] + k
            return small[0:rows, a:a + n]

        consts_in_sem = sem("consts_loaded")
        x_loaded = sem("x_loaded")
        mem_loaded = sem("mem_loaded")
        bias_loaded = sem("bias_loaded")
        band_loaded = sem("band_loaded")
        tile_loaded = [sem(f"tile_loaded{n}") for n in range(RING)]
        raw_used = sem("whole_tiles_used")
        ada_used = sem("modulation_tiles_used")
        w_high = sem("before_high")
        w_ready = sem("before_split")
        w_used = sem("before_split_used")
        full_ready = sem("full_ready")
        high_ready = sem("high_ready")
        low_ready = sem("low_ready")
        bias_negated = sem("bias_negated")
        sq_ready = sem("square_ready")
        sq_summed = sem("square_summed")
        rms_ready = sem("rms_ready")
        normed = sem("normed")
        proj_done = sem("proj_done")
        evac_act = sem("evacuated_by_act")
        evac_dve = sem("evacuated_by_dve")
        act_chain = sem("act_chain")
        dve_chain = sem("dve_chain")
        logits_ready = sem("logits_ready")
        qk_done = sem("qk_done")
        prob_ready = sem("prob_ready")
        prob_turned = sem("prob_turned")
        probT_ready = sem("probT_ready")
        pv_done = sem("pv_done")
        head_out = sem("head_out")
        gates_sig = sem("gates_sigmoid")
        conv_ready = sem("conv_ready")
        cmp_hidden = sem("cmp_hidden")
        cmp_pe_ready = sem("cmp_pe_ready")
        cmp_gelu = sem("cmp_gelu")
        cmp_turned = sem("cmp_turned")
        cmp_turned_out = sem("cmp_turned_out")
        cmp_kv = sem("cmp_kv")
        cmp_done = sem("cmp_done")
        turned = sem("turned")
        turned_out = sem("turned_out")
        mrow_out = sem("mrow_out")
        eps_set = sem("eps_set")
        x3_ready = sem("x3_ready")
        cond_ready = sem("cond_ready")
        ada_done = sem("ada_done")
        conv2_acc = sem("conv2_acc")
        conv2_ready = sem("conv2_ready")
        ones_ready = sem("ones_ready")
        rows_ln = sem("rows_ln")
        rows_m = sem("rows_m")
        rows_exp = sem("rows_exp")
        cols_done = sem("cols_done")
        cols_out = sem("cols_out")
        mrow_done = sem("mrow_done")
        diag_ready = sem("diag_ready")
        decay_ready = sem("decay_ready")
        lqk_done = sem("lqk_done")
        lqk_ready = sem("lqk_ready")
        lpv_done = sem("lpv_done")
        lnum_out = sem("lnum_out")
        hb_sq = sem("hb_square_mean")
        hb_rms = sem("hb_rms")
        hb_ready = sem("hb_ready")
        score_done = sem("score_done")
        score_out = sem("score_out")
        best_ready = sem("best_ready")
        best_exp = sem("best_exp")
        chosen_ready = sem("chosen_ready")
        chosen_turned = sem("chosen_turned")
        chosen_out = sem("chosen_out")
        cur_ready = sem("cur_ready")
        hot_ready = sem("hot_ready")
        hot_used = sem("hot_used")
        staged = sem("staged")
        stored = [sem("gates_stored0"), sem("gates_stored1")]
        g_loaded = [sem("gates_loaded0"), sem("gates_loaded1")]
        w_hi_ready = sem("w_hi_ready")
        w_lo_ready = sem("w_lo_ready")
        expert_done = sem("expert_tile_done")
        gelu_ready = sem("gelu_ready")
        act_stored = [sem(f"act_stored{n}") for n in range(2)]
        act_loaded = [sem(f"act_loaded{n}") for n in range(AS)]
        weighed_ready = sem("weighed_ready")
        p_hi_ready = sem("p_hi_ready")
        p_lo_ready = sem("p_lo_ready")
        out_stored = sem("out_stored")

        PROJ = [("qk", "A" * 8, "01"), ("vtok", "A" * 4, "2345"), ("conv", "A" * 12, "01"), ("w_out", "A" * 8, "01"),
                ("mk", "A" * 2, "01"), ("mv", "A" * 2, "23"), ("mq", "A" * 2, "01"), ("mo", "A" * 8, "01"),
                ("ffn", "AF" * KF, "01"), ("wd", "A" * 8, "01"),
                ("qk2", "A" * 8, "01"), ("cv2", "A" * 8, "01"), ("if", "AA", "01"), ("og", "A" * 4, "01"),
                ("va", "A" * 4, "2345"), ("vb", "A" * 4, "2345"), ("branch", "AVVA" * KD, "0123"),
                ("w_out2", "V" * 8, "01"), ("pq", "A" * 16, "01")]
        last_tile = {"vtok": lambda n: 3, "mv": lambda n: 1, "mo": lambda n: n // 4, "wd": lambda n: 3 * n + 2,
                     "va": lambda n: 3, "vb": lambda n: 3, "branch": lambda n: n // 4 * 3 + (0, 1, 1, 2)[n % 4]}
        first, takers, bank_of, tile_of, tiles_ = {}, "", [], [], 0
        for name, who, banks in PROJ:
            first[name] = len(takers)
            takers += who
            bank_of += [int(banks[n % len(banks)]) for n in range(len(who))]
            tile_of += [tiles_ + last_tile.get(name, lambda n: n)(n) for n in range(len(who))]
            tiles_ = tile_of[-1] + 1
        assert tiles_ == KINDS.count("S")

        def taken(j):
            who = takers[j]
            if who == "F":
                return full_ready, split_base["ff"] + takers[:j + 1].count(who)
            return (evac_act if who == "A" else evac_dve), takers[:j + 1].count(who)

        NORMS = [8, 4, 4, 8, 8, 8, 8, 8, 8, 8, 8, 8]
        norm_base = [sum(NORMS[:n]) for n in range(len(NORMS) + 1)]
        SPLITS = [(0, 8), (1, 4), (2, 4), (3, 8), (5, 8), ("om", 2), (7, 8), ("ff", KF), (9, 8), ("ya", 4),
                  ("yb", 4), ("y2", 8), (10, 8)]
        split_base, at_ = {}, 0
        for name, n in SPLITS:
            split_base[name] = at_
            at_ += n
        split_count = dict(SPLITS)
        POOLED = {4: "w_out", 8: "wd", 10: "w_out2"}
        plain_norms = [0]
        for idx in range(len(NORMS)):
            plain_norms.append(plain_norms[-1] + (0 if idx in split_base else NORMS[idx]))

        def splits_before(idx):
            later = [split_base[n] for n in split_base if not isinstance(n, str) and n >= idx]
            return min(later) if later else at_

        def whole(n):
            return (rms if n % 2 == 0 else full)[:, :]

        UNITS = 96 + 16 + 32

        def nsa_unit(i):
            return i // 32, (i % 32) // NH, i % NH

        def nsa_pieces(i):
            branch, t, _ = nsa_unit(i)
            return [NCMP] if branch == 2 else [P] * (t + 1 if branch == 0 else min(t + 1, 3))

        def nsa_width(i):
            return sum(nsa_pieces(i))

        def nsa_cols(i):
            return P * len(nsa_pieces(i))

        def wait(eng, semaphore, value):
            if not isinstance(value, int) or value > 0:
                eng.wait_ge(semaphore, value)

        block = ctx.enter_context(nc.Block())

        n_tiles = weights.shape[0]
        BEFORE = n_tiles - 2 * NE
        assert BEFORE == len(KINDS)

        def freed(n):
            kind = KINDS[n]
            return {"S": w_ready, "R": raw_used, "A": ada_used}[kind], KINDS[:n + 1].count(kind)

        @block.sync
        def _(sp):

            def load(n, slot):
                sp.dma_start(ring[:, slot, :], weights[n]).then_inc(tile_loaded[slot], 16)

            sp.wait_ge(x_loaded, 16 * KD)
            for n in range(BEFORE):
                if n >= RING:
                    sp.wait_ge(*freed(n - RING))
                load(n, n % RING)
            def tile(e, i=0, used=None):
                sp.wait_ge(*(used or (w_lo_ready, i * JB + (e - RING + 1))))
                load(i * JB + (BEFORE + e), (BEFORE + e) % RING)

            def hidden(e, i=0):
                sp.wait_ge(gelu_ready, i * JB + (e + 1))
                sp.dma_start(acts_dram[i * JB + e], act[:, e % 2, :]).then_inc(act_stored[e % 2], 16)

            def act_back(e, i=0):
                wait(sp, weighed_ready, i * (2 * JB) + (e - AS + 1))
                sp.dma_start(act_in[:, e % AS, :], acts_dram[i * (2 * JB) + e]).then_inc(act_loaded[e % AS], 16)

            def gates(b, i=0):
                wait(sp, weighed_ready, i * (2 * JB) + (b - 1) * JB)
                sp.dma_start(gblk[:, b % 2], gates_dram[i * 2 + b]).then_inc(g_loaded[b % 2], 16)

            for e in range(RING):
                tile(e, used=freed(BEFORE + e - RING))
            with sp.Fori(0, NB - 1) as i:
                for e in range(JB):
                    hidden(e, i)
                    tile(e + RING, i)
            for e in range(JB):
                if e == JB - 2:
                    for n in range(2):
                        sp.wait_ge(stored[n], 16 * (T // GT // 2))
                    sp.wait_ge(hot_used, T)
                    gates(0)
                    for first_ in range(AS - 1):
                        act_back(first_)
                hidden(NE - JB + e)
                tile(NE - JB + e + RING)
            for n in range(2):
                sp.wait_ge(act_stored[n], 16 * (NE // 2))

            def second(b, i=0, last=False):
                if not last:
                    gates(b + 1, i)
                for j in range(JB):
                    e = b * JB + j
                    if not last or j < JB - AS + 1:
                        act_back(e + AS - 1, i)
                    if not last or j < JB - RING:
                        sp.wait_ge(w_lo_ready, i * (2 * JB) + (NE + e + 1))
                        load(i * (2 * JB) + (BEFORE + NE + RING + e), (BEFORE + e) % RING)

            second(0)
            second(1)
            with sp.Fori(0, NB // 2 - 2) as i:
                second(2, i)
                second(3, i)
            second(NB - 2)
            second(NB - 1, last=True)
            for k in range(KD):
                sp.wait_ge(normed, plain_norms[11] + k + 1)
                sp.dma_start(out[k], hT[:, k, :]).then_inc(out_stored, 16)
            sp.wait_ge(out_stored, 16 * KD)

        @block.gpsimd
        def _(pool):
            def negate(biases_):
                for b in biases_:
                    v = b.rearrange("p a b -> p (a b)") if len(b.shape) == 3 else b.rearrange("p a b c -> p (a b c)")
                    nc.gpsimd.tensor_scalar(v, v, -1.0, None, ALU.mult).then_inc(bias_negated, 1)

            def add_square(idx, k):
                n = norm_base[idx] + k
                pool.wait_ge(sq_ready, n + 1)
                if k > 1:
                    pool.wait_ge(sq_summed, n - 1)
                else:
                    pool.wait_ge(rms_ready, idx)
                    pool.wait_ge(low_ready, splits_before(idx))
                    pool.wait_ge(normed, plain_norms[idx])
                before = sq[:, (n - 1) % 2, :] if k == 1 else rms[:, :]
                nc.gpsimd.tensor_tensor(rms[:, :], before, sq[:, n % 2, :], ALU.add).then_inc(sq_summed, 1)

            count = 0
            for n, kind in enumerate(KINDS):
                if kind != "S":
                    continue
                if count == 24:
                    pool.wait_ge(bias_loaded, 48)
                    negate((bias_sel, bias_win, bias_cmp))
                count += 1
                pool.wait_ge(w_high, count)
                nc.gpsimd.tensor_tensor(w_split[:, (count - 1) % 2, 1, :], ring[:, n % RING, :],
                                        w_split[:, (count - 1) % 2, 0, :], ALU.subtract).then_inc(w_ready, 1)
                for idx, name in POOLED.items():
                    for k in range(1, KD):
                        if tile_of[first[name] + k] + 2 == count:
                            add_square(idx, k)

            def split_low(e, i=0):
                pool.wait_ge(w_hi_ready, i * JB + (e + 1))
                nc.gpsimd.tensor_tensor(w_split[:, e % 2, 1, :], ring[:, (BEFORE + e) % RING, :],
                                        w_split[:, e % 2, 0, :], ALU.subtract).then_inc(w_lo_ready, 1)

            with pool.Fori(0, 2 * NE // JB) as i:
                for e in range(JB):
                    split_low(e, i)

        @block.scalar
        def _(act_e):
            a = nc.scalar

            def link(ins, n=[0]):
                n[0] += 1
                ins.then_inc(act_chain, 1)
                act_e.wait_ge(act_chain, n[0])

            for k in range(KD):
                act_e.dma_start(xT[:, k, :], x_in[k]).then_inc(x_loaded, 16)
                if k == 1:
                    act_e.dma_start(const[:, :], consts_in).then_inc(consts_in_sem, 16)
                    act_e.dma_start(small[:, :], smalls_in).then_inc(consts_in_sem, 16)

            def square(idx, k, src, free=T):
                n = norm_base[idx] + k
                if n >= 2:
                    act_e.wait_ge(sq_summed, n - 1)
                a.activation(sq[:, n % 2, 0:free], src(k), ACT.Square).then_inc(sq_ready, 1)

            def root(idx, width, free=T):
                act_e.wait_ge(sq_summed, norm_base[idx + 1])
                wait(act_e, normed, plain_norms[idx])
                wait(act_e, low_ready, splits_before(idx))
                a.activation(rms[:, 0:free], bank[7][:, 0:free], ACT.Sqrt, bias=eps[:, 0:1],
                             scale=1.0 / width).then_inc(rms_ready, 1)

            def norm(idx, src, width, free=T, ready=None):
                for k in range(NORMS[idx]):
                    if ready:
                        act_e.wait_ge(*ready(k))
                    square(idx, k, src, free)
                root(idx, width, free)

            def take_and_norm(idx, name, dst, between=None):
                for k in range(KD):
                    take(first[name] + k, dst[:, k, :])
                    if k == 0 and name == "wd":
                        act_e.wait_ge(ada_done, 6)
                    act_e.wait_ge(*taken(first[name] + k))
                    square(idx, k, lambda k: dst[:, k, :])
                    if between:
                        between(k)
                root(idx, D)

            def high(name, k, dst, free=T, shift=None):
                n = split_base[name] + k
                act_e.wait_ge(full_ready, n + 1)
                if shift is not None:
                    a.activation(dst, whole(n)[:, 0:free], ACT.Identity, bias=shift(k)).then_inc(high_ready, 1)
                    return
                a.activation(dst, whole(n)[:, 0:free], ACT.Copy).then_inc(high_ready, 1)

            def highs(name, dst, free=T, shift=None):
                for k in range(split_count[name]):
                    high(name, k, dst[:, 0, k, :], free, shift)

            split_tiles = [n for n, kind in enumerate(KINDS) if kind == "S"]
            w_count = [0]

            def weight_high(j, ahead=1):
                upto = tile_of[j] + 1
                if ahead and upto < len(split_tiles) and split_tiles[upto] <= split_tiles[upto - 1] + 4:
                    upto += 1
                while w_count[0] < min(upto, len(split_tiles)):
                    s = w_count[0]
                    w_count[0] += 1
                    n = split_tiles[s]
                    act_e.wait_ge(tile_loaded[n % RING], 16 * (n // RING + 1))
                    if s >= 2:
                        act_e.wait_ge(w_used, s - 1)
                    a.activation(w_split[:, s % 2, 0, :], ring[:, n % RING, :], ACT.Copy).then_inc(w_high, 1)

            def take(j, dst, func=ACT.Copy, scale=1.0, m=P, n=T, bias=0.0):
                weight_high(j)
                act_e.wait_ge(proj_done, j + 1)
                return a.activation(dst, bank[bank_of[j]][0:m, 0:n], func, scale=scale, bias=bias).then_inc(evac_act, 1)

            def softmax(u0, units, width, scols):
                for i in range(units + 1):
                    if i < units:
                        u = u0 + i
                        w = width(i)
                        act_e.wait_ge(logits_ready, u + 1)
                        if u >= 2:
                            act_e.wait_ge(prob_turned, u - 1)
                        a.activation(prob[:, u % 2, 0:w], logit[:, u % 2, 0:w], ACT.Exp, scale=-1.0,
                                     bias=least[:, i:i + 1], accum_out=total[:, i:i + 1]).then_inc(prob_ready, 1)
                    if i >= 1:
                        u = u0 + i - 1
                        w = scols(i - 1)
                        rows_ = NCMP if width(i - 1) == NCMP else P
                        act_e.wait_ge(prob_turned, u + 1)
                        if u >= 2:
                            act_e.wait_ge(pv_done, u - 1)
                        a.activation(probT[0:rows_, u % 2, 0:w], bank[2 + u % 2][0:rows_, 0:w],
                                     ACT.Copy).then_inc(probT_ready, 1)

            act_e.wait_ge(eps_set, 1)
            act_e.wait_ge(consts_in_sem, 32)
            act_e.wait_ge(x_loaded, 16 * KD)
            norm(0, lambda k: xT[:, k, :], D)
            act_e.dma_start(bias_sel, sel_in.rearrange("p (a b) -> p a b", a=NH)).then_inc(bias_loaded, 16)
            act_e.dma_start(bias_win, win_in.rearrange("p (a b) -> p a b", a=NH)).then_inc(bias_loaded, 16)
            act_e.dma_start(bias_cmp, cmp_in.rearrange("p (a b c) -> p a b c", a=NH, b=NT)).then_inc(bias_loaded, 16)
            weight_high(0)
            highs(0, h_split)
            j = first["qk"]
            for k in range(8):
                take(j + k, qk[:, k, :], scale=QS if k < 4 else 1.0)
            j = first["vtok"]
            for t in range(NT):
                take(j + t, vtok[:, t, :], n=408)
            act_e.wait_ge(evac_act, 12)
            a.activation(gsig, vtok[:, :, 384:408], ACT.Sigmoid).then_inc(gates_sig, 1)
            j = first["conv"]
            for k in range(12):
                take(j + k, conv[:, k, :])
            norm(1, lambda k: conv[:, 3 * k, :], 512, ready=lambda k: (conv_ready, k + 1))
            for kv in range(2):
                act_e.wait_ge(cmp_hidden, kv + 1)
                for g in range(2):
                    a.activation(hid_rows[0:NCMP, 2 * kv + g, :], bank[6 - g][0:NCMP, kv * P:(kv + 1) * P],
                                 ACT.Gelu_apprx_tanh).then_inc(cmp_gelu, 1)
            act_e.wait_ge(cmp_turned, 1)
            a.activation(hid.rearrange("p a b c -> p (a b) c")[:, :, 0:NCMP],
                         bank[4][:, 0:P].rearrange("p (a c) -> p a c", a=4)[:, :, 0:NCMP],
                         ACT.Copy).then_inc(cmp_turned_out, 1)
            act_e.wait_ge(cmp_kv, 1)
            a.activation(kcmp[:, 0:NCMP], bank[2][:, 0:NCMP], ACT.Copy).then_inc(cmp_done, 1)
            a.activation(vcmp[0:NCMP, :], bank[2][0:NCMP, 128:256], ACT.Copy).then_inc(cmp_done, 1)
            weight_high(first["w_out"], ahead=0)
            for k in range(4):
                high(1, k, conv_split[:, k, 1, :])
            softmax(0, 96, nsa_width, nsa_cols)
            for c in range(4):
                act_e.wait_ge(turned, c + 1)
                a.activation(nT[:, c, :], bank[2 + c % 2][:, :], ACT.Copy).then_inc(turned_out, 1)
            act_e.wait_ge(turned_out, 4)
            act_e.dma_start(memT, mem_in.rearrange("k p m -> p k m")).then_inc(mem_loaded, 16)
            norm(2, lambda k: nT[:, k, :], 512)
            for k in range(4):
                high(2, k, merged[:, 0, k, :])
            act_e.wait_ge(mem_loaded, 16)
            norm(3, lambda k: memT[:, k, :], D, NM)
            take_and_norm(4, "w_out", yT, between=lambda k: [high(3, c, m_split[:, 0, c, :], NM)
                                                             for c in range(4 * k, 4 * k + 4) if k < 2])
            before_ = lambda k: act_e.wait_ge(normed, plain_norms[4] + k + 1)
            for k in range(2):
                take(first["mk"] + k, mk[:, k, :], n=NM)
            for k in range(2):
                before_(k)
                square(5, k, lambda k: xT[:, k, :])
            for k in range(2):
                take(first["mv"] + k, mv[:, k, :], n=NM)
            for k in range(2, KD):
                before_(k)
                square(5, k, lambda k: xT[:, k, :])
            root(5, D)
            highs(5, h_split)
            for k in range(2):
                take(first["mq"] + k, mq[:, k, :], scale=QS)
            softmax(96, 16, lambda i: NM, lambda i: NM)
            highs("om", om_split)
            take_and_norm(6, "mo", yT)
            norm(7, lambda k: xT[:, k, :], D, ready=lambda k: (normed, plain_norms[6] + k + 1))
            highs(7, h_split)
            a.activation(condT[:, :], sm("cond", 0, 8), ACT.Silu).then_inc(cond_ready, 1)
            for m in range(KF):
                j = first["ffn"] + 2 * m
                weight_high(j)
                act_e.wait_ge(proj_done, j + 1)
                if m >= 2:
                    act_e.wait_ge(full_ready, split_base["ff"] + m - 1)
                a.activation(ff_gate[:, m % 2, :], bank[bank_of[j]][:, :], ACT.Silu).then_inc(evac_act, 1)
                weight_high(j + 1)
                if m:
                    high("ff", m - 1, ff_split[:, 0, m - 1, :])
            high("ff", KF - 1, ff_split[:, 0, KF - 1, :])
            take_and_norm(8, "wd", yF)
            act_e.dma_start(bias_band, band_in.rearrange("p (a b) -> p a b", a=NH)).then_inc(band_loaded, 16)
            norm(9, lambda k: xT[:, k, :], D, ready=lambda k: (normed, plain_norms[8] + k + 1))
            highs(9, h_split, shift=lambda k: mod[:, k:k + 1])
            for k in range(8):
                take(first["qk2"] + k, qk2[:, k, :], scale=QS if k < 4 else 1.0)
            def conv2_silu(k):
                act_e.wait_ge(conv2_acc, k + 1)
                a.activation(cv2[:, k, :], conv_acc[:, k % 2, :], ACT.Silu,
                             bias=sm("conv_b2", k)).then_inc(conv2_ready, 1)

            for k in range(8):
                take(first["cv2"] + k, cv2[:, k, :])
                if k >= 2:
                    conv2_silu(k - 2)
            take(first["if"], row_i, ACT.Identity, m=BH, bias=sm("b_if", 0, 1, BH))
            take(first["if"] + 1, row_f, ACT.Identity, m=BH, bias=sm("b_if", 1, 1, BH))
            conv2_silu(6)
            conv2_silu(7)
            act_e.wait_ge(*taken(first["if"] + 1))
            link(a.activation(row_a, row_f, ACT.Abs))
            link(a.activation(row_a, row_a, ACT.Exp, scale=-1.0))
            a.activation(row_a, row_a, ACT.Ln, bias=eps[0:BH, 1:2]).then_inc(rows_ln, 1)
            for k in range(4):
                take(first["og"] + k, sig_o[:, k, :], ACT.Sigmoid)
            for t in range(NT):
                take(first["va"] + t, va[:, t, :])
            act_e.wait_ge(ones_ready, 1)
            for t in range(NT):
                j = first["vb"] + t
                weight_high(j)
                act_e.wait_ge(proj_done, j + 1)
                a.activation(vb[:, t, :, 0:P], bank[bank_of[j]][:, :].rearrange("p (h d) -> p h d", h=BH),
                             ACT.Copy).then_inc(evac_act, 1)
            act_e.wait_ge(rows_m, 1)
            a.activation(row_f, row_f, ACT.Exp, scale=-1.0).then_inc(rows_exp, 1)
            softmax(112, 32, lambda i: P * (i // NH + 1), lambda i: P * (i // NH + 1))
            act_e.wait_ge(cols_done, 1)
            a.activation(tcol[:, 0:32], bank[6][:, 0:32], ACT.Copy).then_inc(cols_out, 1)
            act_e.wait_ge(cols_out, 1)
            def take_mrow(h):
                act_e.wait_ge(mrow_done, h + 1)
                if h >= 2:
                    act_e.wait_ge(diag_ready, (h - 1) * NT)
                a.activation(mrow[:, h % 2, :], bank[4 + h % 2][:, :], ACT.Copy).then_inc(mrow_out, 1)

            take_mrow(0)
            for i in range(BH * NT):
                h, s = divmod(i, NT)
                w = T - s * P
                if s == 0:
                    if h + 1 < BH:
                        take_mrow(h + 1)
                    act_e.wait_ge(mrow_out, h + 1)
                act_e.wait_ge(diag_ready, i + 1)
                if i >= 2:
                    act_e.wait_ge(lqk_ready, i - 1)
                b_s = tcol[:, s * BH + h:s * BH + h + 1]
                last = a.activation(wdec[:, i % 2, 0:P], wdiag[:, i % 2, :], ACT.Exp, scale=-1.0, bias=b_s)
                if w > P:
                    last = a.activation(wdec[:, i % 2, P:w], mrow[:, h % 2, (s + 1) * P:T], ACT.Exp,
                                        scale=-1.0, bias=b_s)
                last.then_inc(decay_ready, 1)
            highs("ya", ya_split)
            act_e.wait_ge(hb_sq, 1)
            a.activation(den[:, 16:32], den[:, 0:16], ACT.Sqrt, bias=eps[:, 0:1], scale=1.0 / P).then_inc(hb_rms, 1)
            weight_high(first["branch"])
            highs("yb", yb_split)
            for m in range(KD):
                j = first["branch"] + 4 * m
                for g in range(2):
                    jg = j + 3 * g
                    weight_high(jg)
                    act_e.wait_ge(proj_done, jg + 1)
                    wait(act_e, full_ready, split_base["y2"] + m if m else 0)
                    a.activation(gate_ab[:, g, :], bank[bank_of[jg]][:, :], ACT.Sigmoid).then_inc(evac_act, 1)
                    if g == 0 and m:
                        high("y2", m - 1, y2_split[:, 0, m - 1, :])
            high("y2", KD - 1, y2_split[:, 0, KD - 1, :])
            for k in range(KD):
                weight_high(first["w_out2"] + k)
                act_e.wait_ge(*taken(first["w_out2"] + k))
                square(10, k, lambda k: xT[:, k, :])
            root(10, D)
            highs(10, h_split, shift=lambda k: mod[:, 24 + k:25 + k])
            for k in range(16):
                take(first["pq"] + k, pq[:, k, :])
            for n in range(4 * NT):
                t, q = divmod(n, 4)
                act_e.wait_ge(score_done, n + 1)
                a.activation(s_all[:, t, 4 * q:4 * q + 4, :], bank[2 + q].rearrange("p (a b) -> p a b", a=4),
                             ACT.Copy).then_inc(score_out, 1)

            def split_high(e, i=0, step=JB):
                n = BEFORE + e
                act_e.wait_ge(tile_loaded[n % RING], i * (16 * step // RING) + 16 * (n // RING + 1))
                wait(act_e, expert_done, i * step + (e - 1))
                a.activation(w_split[:, e % 2, 0, :], ring[:, n % RING, :], ACT.Copy).then_inc(w_hi_ready, 1)

            def gelu(e, i=0):
                act_e.wait_ge(expert_done, i * JB + (e + 1))
                wait(act_e, act_stored[e % 2], i * (16 * JB // 2) + 16 * (e // 2))
                a.activation(act[:, e % 2, :], bank[e % 2][:, :], ACT.Gelu_apprx_tanh).then_inc(gelu_ready, 1)

            act_e.wait_ge(w_used, KINDS.count("S"))
            split_high(0)
            split_high(1)
            for e in range(JB):
                split_high(e + 2)
                gelu(e)
            with act_e.Fori(0, CHOICE - 1) as i:
                for e in range(JB, 2 * JB):
                    split_high(e + 2, i)
                    gelu(e, i)
            for e in range(CHOICE * JB, (CHOICE + 1) * JB):
                split_high(e + 2)
                gelu(e)
                if e == CHOICE * JB:
                    act_e.wait_ge(best_ready, 1)
                    a.activation(expd, expd, ACT.Exp).then_inc(best_exp, 1)

            def stage_gates(n, i=0):
                half, q = n // 4 % 2, n % 4
                act_e.wait_ge(hot_used, i * (TB) + 4 * n + 4)
                if q == 0:
                    wait(act_e, stored[half], i * (16 * TB // GT // 2) + 16 * (n // 8))
                a.activation(
                    stage[:, half].rearrange("p b (t j) -> p b t j", t=GT)[:, :, 4 * q:4 * q + 4, :].rearrange(
                        "p b t j -> p t b j"),
                    bank[2 + n % 4][:, :].rearrange("p (t b j) -> p t b j", t=4, j=JB), ACT.Copy).then_inc(staged, 1)
                if q == 3:
                    act_e.wait_ge(staged, i * (TB // 4) + n + 1)
                    act_e.dma_start(
                        gates_dram.rearrange("b p t j -> p b (t j)")[
                            :, :, bass.ds(i * (TB * JB) + n // 4 * GT * JB, GT * JB)],
                        stage[:, half]).then_inc(stored[half], 16)

            def spread_block(i):
                for j in range(JB):
                    e = (CHOICE + 1) * JB + j
                    split_high(e + 2, i)
                    gelu(e, i)
                    for n in range(sum(QUADS[:j]), sum(QUADS[:j + 1])):
                        stage_gates(n, i)

            spread_block(0)
            with act_e.Fori(1, SPREAD) as i:
                spread_block(i)

            def weighted_high(e, i=0):
                act_e.wait_ge(weighed_ready, i * (2 * JB) + e + 1)
                if e >= PS:
                    act_e.wait_ge(expert_done, i * (2 * JB) + NE + e - PS + 1)
                a.activation(p_split[:, e % PS, 0, :], weighed[:, e % 2, :], ACT.Copy).then_inc(p_hi_ready, 1)

            def second(b, i=0):
                for e in range(b * JB, (b + 1) * JB):
                    if e >= 2:
                        split_high(NE + e, i, 2 * JB)
                    if e + 1 < NE:
                        weighted_high(e + 1, i)

            weighted_high(0)
            for b in range(2):
                second(b)
            with act_e.Fori(0, NB // 2 - 2) as i:
                second(2, i)
                second(3, i)
            for b in range(NB - 2, NB):
                second(b)
            norm(11, lambda k: xT[:, k, :], D, ready=lambda k: (x3_ready, min(k + 2, KD)))

        @block.vector
        def _(dve):
            v = nc.vector
            chain = [0]

            def link(ins):
                chain[0] += 1
                ins.then_inc(dve_chain, 1)
                dve.wait_ge(dve_chain, chain[0])

            v.memset(eps[:, 0:1], EPS).then_inc(dve_chain, 1)
            chain[0] += 1
            dve.wait_ge(dve_chain, 1)
            v.memset(eps[:, 1:2], 1.0).then_inc(eps_set, 1)
            dve.wait_ge(consts_in_sem, 32)

            def value(name, k, make, free=T):
                n = split_base[name] + k
                wait(dve, low_ready, n - 1)
                make(k, whole(n)[:, 0:free]).then_inc(full_ready, 1)

            def low(name, k, dst, free=T, shift=None):
                n = split_base[name] + k
                dve.wait_ge(high_ready, n + 1)
                if shift is not None:
                    v.scalar_tensor_tensor(out=dst(1), in0=whole(n)[:, 0:free], scalar=shift(k), in1=dst(0),
                                           op0=ALU.add, op1=ALU.subtract).then_inc(low_ready, 1)
                    return
                v.tensor_tensor(dst(1), whole(n)[:, 0:free], dst(0), ALU.subtract).then_inc(low_ready, 1)

            def split_all(name, make, dst, free=T, shift=None):
                for k in range(split_count[name] + 1):
                    if k < split_count[name]:
                        value(name, k, make, free)
                    if k:
                        low(name, k - 1, lambda part: dst(part, k - 1), free, shift)

            def norm(idx, src, dst, gain, free=T, shift=None, add=False):
                dve.wait_ge(rms_ready, idx + 1)
                link(v.reciprocal(rstd[:, 0:free], rms[:, 0:free]))
                if idx in split_base:
                    def one(k, out_):
                        return v.scalar_tensor_tensor(out=out_, in0=src(k), scalar=gain(k), in1=rstd[:, 0:free],
                                                      op0=ALU.mult, op1=ALU.mult)

                    split_all(idx, one, dst, free, shift)
                    return
                for k in range(NORMS[idx]):
                    one = v.scalar_tensor_tensor(out=src(k) if add else dst(k), in0=src(k), scalar=gain(k),
                                                 in1=rstd[:, 0:free], op0=ALU.mult, op1=ALU.mult)
                    if add:
                        link(one)
                        v.tensor_tensor(dst(k), dst(k), src(k), ALU.add).then_inc(normed, 1)
                    else:
                        one.then_inc(normed, 1)

            def attend(u0, units, width, bias, gate, where, adds):
                for i in range(units + 2):
                    if i < units:
                        u, w = u0 + i, width(i)
                        dve.wait_ge(qk_done, u + 1)
                        if u >= 2:
                            dve.wait_ge(prob_ready, u - 1)
                        if bias is None:
                            v.tensor_scalar(logit[:, u % 2, 0:w], bank[u % 2][:, 0:w], 0.0, 3.0e38, ALU.add, ALU.min,
                                            accum_out=least[:, i:i + 1]).then_inc(logits_ready, 1)
                        else:
                            v.tensor_tensor_reduce(logit[:, u % 2, 0:w], bank[u % 2][:, 0:w], bias(i), 1.0, 3.0e38,
                                                   ALU.add, ALU.min, least[:, i:i + 1]).then_inc(logits_ready, 1)
                    if i >= 2:
                        n = i - 2
                        u = u0 + n
                        dve.wait_ge(pv_done, u + 1)
                        link(v.reciprocal(rrec[:, n:n + 1], total[:, n:n + 1]))
                        o = bank[4 + u % 2][:, 0:HD]
                        if gate is None:
                            v.tensor_scalar(where(n), o, rrec[:, n:n + 1], None, ALU.mult).then_inc(head_out, 1)
                            continue
                        link(v.tensor_tensor(rgate[:, n:n + 1], rrec[:, n:n + 1], gate(n), ALU.mult))
                        if adds(n):
                            dve.wait_ge(head_out, u - 31)
                            v.scalar_tensor_tensor(out=where(n), in0=o, scalar=rgate[:, n:n + 1], in1=where(n),
                                                   op0=ALU.mult, op1=ALU.add).then_inc(head_out, 1)
                        else:
                            v.tensor_scalar(where(n), o, rgate[:, n:n + 1], None, ALU.mult).then_inc(head_out, 1)

            norm(0, lambda k: xT[:, k, :], lambda part, k: h_split[:, part, k, :], lambda k: sm("norm0", k))
            dve.wait_ge(*taken(first["qk"] + 5))
            for kv in range(2):
                for half in range(2):
                    one = v.tensor_tensor(placed[:, 2 * kv + half, :].rearrange("p (n j) -> p n j", j=16),
                                          qk[:, 4 + kv, :].rearrange("p (n j) -> p n j", j=16),
                                          sm("pe", 16 * half, 16).unsqueeze(1).to_broadcast([P, 32, 16]), ALU.add)
                    one.then_inc(cmp_pe_ready, 1)
            for j in range(4):
                cc, cx, cb = (conv[:, 3 * j + n, :] for n in range(3))
                y = conv_y[:, j % 2, :]
                sem_, val = taken(first["conv"] + 3 * j + 2)
                dve.wait_ge(sem_, val)
                link(v.tensor_tensor(cx, cc, cx, ALU.mult))
                link(v.tensor_scalar(y, cx, sm("conv_w", j), None, ALU.mult))
                for k in range(1, 3):
                    link(v.scalar_tensor_tensor(out=y[:, k:T], in0=cx[:, 0:T - k], scalar=sm("conv_w", 4 * k + j),
                                                in1=y[:, k:T], op0=ALU.mult, op1=ALU.add))
                v.tensor_tensor(cc, cb, y, ALU.mult).then_inc(conv_ready, 1)
            dve.wait_ge(gates_sig, 1)
            link(v.tensor_scalar(gsig[:, 0, 0:24:3], gsig[:, 0, 0:24:3], rowmask, None, ALU.mult))
            norm(1, lambda k: conv[:, 3 * k, :], lambda part, k: conv_split[:, k, 1 + part, :],
                 lambda k: sm("gn_conv", k))
            dve.wait_ge(bias_negated, 3)

            def nsa_bias(i):
                br, t, h = nsa_unit(i)
                if br == 0:
                    return bias_sel[:, h, 384 - P * t:T]
                if br == 1:
                    return bias_win[:, h, max(256 - P * t, 0):384]
                return bias_cmp[:, h, t, 0:NCMP]

            def nsa_gate(i):
                br, t, h = nsa_unit(i)
                c = 3 * h + (1, 2, 0)[br]
                return gsig[:, t, c:c + 1]

            def nsa_where(i):
                br, t, h = nsa_unit(i)
                return o_tok[:, t, h * HD:(h + 1) * HD]

            attend(0, 96, nsa_width, nsa_bias, nsa_gate, nsa_where, lambda i: nsa_unit(i)[0] > 0)
            norm(2, lambda k: nT[:, k, :], lambda part, k: merged[:, part, k, :], lambda k: sm("gn_nsa", k))
            norm(3, lambda k: memT[:, k, :], lambda part, k: m_split[:, part, k, :], lambda k: sm("mem_norm", k), NM)
            norm(4, lambda k: yT[:, k, :], lambda k: xT[:, k, :], lambda k: sm("norm1", k), add=True)
            norm(5, lambda k: xT[:, k, :], lambda part, k: h_split[:, part, k, :], lambda k: sm("norm2", k))
            attend(96, 16, lambda i: NM, None, None,
                   lambda i: om_tok[:, i // MH, (i % MH) * HD:(i % MH + 1) * HD], None)

            def turned_tile(n0):
                def make(k, out_):
                    dve.wait_ge(turned, n0 + k + 1)
                    return v.tensor_copy(out_, bank[2 + k % 2][:, :])
                return make

            split_all("om", turned_tile(4), lambda part, k: om_split[:, part, k, :])
            norm(6, lambda k: yT[:, k, :], lambda k: xT[:, k, :], lambda k: sm("norm3", k), add=True)
            norm(7, lambda k: xT[:, k, :], lambda part, k: h_split[:, part, k, :], lambda k: sm("norm4", k))
            sums = sq[:, :, :].rearrange("p a b -> p (a b)")
            ada_at = [n for n, kind in enumerate(KINDS) if kind == "A"]

            def ada_tile(c):
                n = ada_at[c]
                dve.wait_ge(tile_loaded[n % RING], 16 * (n // RING + 1))
                w = ring[:, n % RING, :]
                if c == 0:
                    dve.wait_ge(cond_ready, 1)
                    dve.wait_ge(sq_summed, norm_base[8])
                if c % KD == 0:
                    wait(dve, ada_done, c // KD)
                    ins = v.tensor_scalar(sums, w, condT[:, 0:1], None, ALU.mult)
                else:
                    dve.wait_ge(ada_used, c)
                    ins = v.scalar_tensor_tensor(out=sums, in0=w, scalar=condT[:, c % KD:c % KD + 1], in1=sums,
                                                 op0=ALU.mult, op1=ALU.add)
                ins.then_inc(ada_used, 1)

            def hidden_value(m, out_):
                j = first["ffn"] + 2 * m + 1
                dve.wait_ge(evac_act, taken(j - 1)[1])
                dve.wait_ge(proj_done, j + 1)
                return v.tensor_tensor(out_, bank[bank_of[j]][:, :], ff_gate[:, m % 2, :], ALU.mult)

            for m in range(KF):
                for c in range(ADA_AT[m], ADA_AT[m + 1]):
                    ada_tile(c)
                value("ff", m, hidden_value)
                if m:
                    low("ff", m - 1, lambda part: ff_split[:, part, m - 1, :])
            low("ff", KF - 1, lambda part: ff_split[:, part, KF - 1, :])
            dve.wait_ge(ada_done, 6)
            link(v.tensor_tensor(mod[:, :], bank[6][:, 0:48], sm("b_ada", 0, 48), ALU.add))
            link(v.scalar_tensor_tensor(out=gmod[:, 0:8], in0=mod[:, 8:16], scalar=1.0, in1=sm("norm1_2", 0, 8),
                                        op0=ALU.add, op1=ALU.mult))
            link(v.scalar_tensor_tensor(out=gmod[:, 8:16], in0=mod[:, 32:40], scalar=1.0, in1=sm("norm2_2", 0, 8),
                                        op0=ALU.add, op1=ALU.mult))
            norm(8, lambda k: yF[:, k, :], lambda k: xT[:, k, :], lambda k: sm("norm5", k), add=True)
            norm(9, lambda k: xT[:, k, :], lambda part, k: h_split[:, part, k, :], lambda k: gmod[:, k:k + 1],
                 shift=lambda k: mod[:, k:k + 1])
            v.memset(vb[:, :, :, P:P + 1], 1.0).then_inc(ones_ready, 1)
            dve.wait_ge(band_loaded, 16)
            flat_band = bias_band.rearrange("p a b -> p (a b)")
            link(v.tensor_scalar(flat_band, flat_band, -1.0, None, ALU.mult))
            for k in range(8):
                sem_, val = taken(first["cv2"] + k)
                dve.wait_ge(sem_, val)
                if k >= 2:
                    dve.wait_ge(conv2_ready, k - 1)
                y, u = conv_acc[:, k % 2, :], cv2[:, k, :]
                link(v.tensor_scalar(y, u, sm("conv_w2", 24 + k), None, ALU.mult))
                for d in range(1, 4):
                    one = v.scalar_tensor_tensor(out=y[:, d:T], in0=u[:, 0:T - d],
                                                 scalar=sm("conv_w2", 8 * (3 - d) + k), in1=y[:, d:T],
                                                 op0=ALU.mult, op1=ALU.add)
                    if d < 3:
                        link(one)
                    else:
                        one.then_inc(conv2_acc, 1)
            dve.wait_ge(rows_ln, 1)
            link(v.scalar_tensor_tensor(out=row_b, in0=row_f, scalar=0.0, in1=row_a, op0=ALU.min, op1=ALU.subtract))
            link(v.memset(row_f, 0.0))
            link(v.tensor_tensor_scan(row_a, row_b, row_f, 0.0, ALU.add, ALU.add))
            link(v.tensor_tensor(row_b, row_i, row_a, ALU.subtract))
            link(v.tensor_tensor_scan(row_i, row_b, row_b, 0.0, ALU.max, ALU.max))
            v.tensor_tensor(row_f, row_a, row_i, ALU.add).then_inc(rows_m, 1)
            attend(112, 32, lambda i: P * (i // NH + 1), lambda i: bias_band[:, i % NH, 384 - P * (i // NH):T],
                   None, lambda i: oa_tok[:, i // NH, (i % NH) * HD:(i % NH + 1) * HD], None)
            dve.wait_ge(cols_out, 1)
            scale = P ** -0.5
            for i in range(BH * NT + 1):
                if i < BH * NT:
                    h, s = divmod(i, NT)
                    w = T - s * P
                    dve.wait_ge(mrow_out, h + 1)
                    if i >= 2:
                        dve.wait_ge(decay_ready, i - 1)
                    v.tensor_tensor(wdiag[:, i % 2, :], mrow[:, h % 2, s * P:(s + 1) * P],
                                    const[:, C_TRI:C_TRI + P], ALU.add).then_inc(diag_ready, 1)
                if i >= 1:
                    n = i - 1
                    h, s = divmod(n, NT)
                    w = T - s * P
                    dve.wait_ge(decay_ready, n + 1)
                    dve.wait_ge(lqk_done, n + 1)
                    if h >= 2:
                        dve.wait_ge(lpv_done, h - 1)
                    v.scalar_tensor_tensor(out=wqk[:, h % 2, s, 0:w], in0=bank[n % 2][:, 0:w], scalar=scale,
                                           in1=wdec[:, n % 2, 0:w], op0=ALU.mult, op1=ALU.mult).then_inc(lqk_ready, 1)
                if i >= 1 and (i - 1) % NT == NT - 1:
                    h = (i - 1) // NT
                    dve.wait_ge(lpv_done, h + 1)
                    for t in range(NT):
                        o = bank[2 + t // 2][:, (t % 2) * 256:(t % 2) * 256 + P + 1]
                        d = den[:, 32 + t * BH + h:33 + t * BH + h]
                        link(v.tensor_scalar(d, o[:, P:P + 1], -1.0, tcol[:, 16 + t * BH + h:17 + t * BH + h],
                                             ALU.mult, ALU.max))
                        link(v.tensor_tensor(d, o[:, P:P + 1], d, ALU.max))
                        link(v.reciprocal(d, d))
                        v.tensor_scalar(hb_tok[:, t, h * P:(h + 1) * P], o[:, 0:P], d, None,
                                        ALU.mult).then_inc(lnum_out, 1)
            for k in range(5):
                if k < 4:
                    value("ya", k, turned_tile(6))
                if k and k < 5:
                    low("ya", k - 1, lambda part: ya_split[:, part, k - 1, :])
            dve.wait_ge(lnum_out, BH * NT)
            link(v.tensor_tensor(hsq, hb_tok, hb_tok, ALU.mult))
            v.tensor_reduce(den[:, 0:16], hsq.rearrange("p t (h d) -> p (t h) d", h=BH), AX.X, ALU.add).then_inc(hb_sq, 1)
            dve.wait_ge(hb_rms, 1)
            link(v.reciprocal(den[:, 0:16], den[:, 16:32]))
            for n in range(16):
                t, h = divmod(n, BH)
                o = hb_tok[:, t, h * P:(h + 1) * P]
                v.tensor_scalar(o, o, den[:, n:n + 1], None, ALU.mult).then_inc(hb_ready, 1)

            def yb_value(c, out_):
                dve.wait_ge(turned, 10 + c + 1)
                return v.scalar_tensor_tensor(out=out_, in0=bank[2 + c % 2][:, :], scalar=sm("mlstm_g", c),
                                              in1=sig_o[:, c, :], op0=ALU.mult, op1=ALU.mult)

            split_all("yb", yb_value, lambda part, k: yb_split[:, part, k, :])
            for m in range(KD):
                j = first["branch"] + 4 * m
                for g in range(2):
                    dve.wait_ge(evac_act, taken(j + 3 * g)[1])
                    dve.wait_ge(proj_done, j + g + 2)
                    v.tensor_tensor(gate_ab[:, 2 + g, :], bank[bank_of[j + 1 + g]][:, :], gate_ab[:, g, :],
                                    ALU.mult).then_inc(evac_dve, 1)
                dve.wait_ge(evac_dve, taken(j + 2)[1])
                value("y2", m, lambda k, out_: v.tensor_tensor(out_, gate_ab[:, 2, :], gate_ab[:, 3, :], ALU.add))
                if m:
                    low("y2", m - 1, lambda part: y2_split[:, part, m - 1, :])
            low("y2", KD - 1, lambda part: y2_split[:, part, KD - 1, :])
            for k in range(8):
                j = first["w_out2"] + k
                dve.wait_ge(proj_done, j + 1)
                v.scalar_tensor_tensor(out=xT[:, k, :], in0=bank[bank_of[j]][:, :], scalar=mod[:, 16 + k:17 + k],
                                       in1=xT[:, k, :], op0=ALU.mult, op1=ALU.add).then_inc(evac_dve, 1)
            dve.wait_ge(evac_dve, taken(first["w_out2"] + 7)[1])
            norm(10, lambda k: xT[:, k, :], lambda part, k: h_split[:, part, k, :], lambda k: gmod[:, 8 + k:9 + k],
                 shift=lambda k: mod[:, 24 + k:25 + k])

            def each(n, op):
                for g in range(n):
                    one = op(g)
                link(one)

            dve.wait_ge(score_out, 4 * NT)
            for t in range(NT):
                each(16, lambda g: v.max(s_top[:, g, 0:8], s_all[:, t, g, :]))
                each(16, lambda g: v.max_index(i_top[:, g, 0:8], s_top[:, g, 0:8], s_all[:, t, g, :]))
                each(16, lambda g: v.match_replace(s_left[:, g, :], s_top[:, g, 0:8], s_all[:, t, g, :], -3.0e38))
                each(16, lambda g: v.max(s_top[:, g, 8:16], s_left[:, g, :]))
                each(16, lambda g: v.max_index(i_top[:, g, 8:16], s_top[:, g, 8:16], s_left[:, g, :]))
                tops = s_top.rearrange("p (h b) k -> p h b k", b=2)
                shape = [P, PH, TOPK, TOPK]
                for h in range(PH):
                    one = v.tensor_tensor(cand[:, h], tops[:, h, 0, :].unsqueeze(2).to_broadcast([P, TOPK, TOPK]),
                                          tops[:, h, 1, :].unsqueeze(1).to_broadcast([P, TOPK, TOPK]), ALU.add)
                link(one)
                flat = lambda c, h: c[:, h].rearrange("p a b -> p (a b)")
                each(PH, lambda h: v.max(best[:, h, 0:8], flat(cand, h)))
                each(PH, lambda h: v.max_index(c_top[:, h, 0:8], best[:, h, 0:8], flat(cand, h)))
                each(PH, lambda h: v.match_replace(flat(cand_left, h), best[:, h, 0:8], flat(cand, h), -3.0e38))
                each(PH, lambda h: v.max(best[:, h, 8:16], flat(cand_left, h)))
                each(PH, lambda h: v.max_index(c_top[:, h, 8:16], best[:, h, 8:16], flat(cand_left, h)))
                link(v.tensor_tensor(expd[:, t].rearrange("p (h k) -> p h k", h=PH), best,
                                     best[:, :, 0:1].to_broadcast([P, PH, TOPK]), ALU.subtract))
                v.tensor_scalar(c_hi, c_top, 4, None, ALU.logical_shift_right)
                link(v.tensor_scalar(c_lo, c_top, 15, None, ALU.bitwise_and))
                v.tensor_copy(a_f, c_hi)
                v.tensor_copy(b_f, c_lo)
                link(v.tensor_copy(i_topf, i_top))
                for half, rank in ((0, a_f), (1, b_f)):
                    for h in range(PH):
                        one = v.tensor_tensor(eqs[:, h], rank[:, h, :].unsqueeze(2).to_broadcast([P, TOPK, TOPK]),
                                              iota[:, 0:TOPK].unsqueeze(1).to_broadcast([P, TOPK, TOPK]), ALU.is_equal)
                    link(one)
                    for h in range(PH):
                        one = v.tensor_tensor(eqs[:, h], eqs[:, h],
                                              i_topf[:, 2 * h + half, :].unsqueeze(1).to_broadcast([P, TOPK, TOPK]),
                                              ALU.mult)
                    link(one)
                    one = v.tensor_reduce(chosen[:, t, half * P:(half + 1) * P],
                                          eqs.rearrange("p h k a -> p (h k) a"), AX.X, ALU.add)
                    if t == NT - 1 and half:
                        one.then_inc(best_ready, 1)
                    else:
                        link(one)
            dve.wait_ge(best_exp, 1)
            by_head = lambda a: a.rearrange("p (h k) -> p h k", h=PH)
            for t in range(NT):
                one = v.tensor_reduce(gsum[:, 0, t, :], by_head(expd[:, t]), AX.X, ALU.add)
            link(one)
            link(v.reciprocal(gsum[:, 1], gsum[:, 0]))
            for t in range(NT):
                v.tensor_tensor(by_head(chosen[:, t, 2 * P:3 * P]), by_head(expd[:, t]),
                                gsum[:, 1, t, :].unsqueeze(2).to_broadcast([P, PH, TOPK]),
                                ALU.mult).then_inc(chosen_ready, 1)
            for t in range(NT):
                dve.wait_ge(chosen_turned, t + 1)
                v.tensor_copy(chosenT[:, :, t * P:(t + 1) * P],
                              bank[4 + t % 2][:, 0:3 * P].rearrange("p (a b) -> p a b", a=3)).then_inc(chosen_out, 1)
            dve.wait_ge(chosen_out, NT)

            def one_hots(i):
                many = TB
                wait(dve, hot_ready, i * (2 * many))
                v.tensor_copy(cur, chosenT[:, :, bass.ds(i * many, many)]).then_inc(cur_ready, 1)
                dve.wait_ge(cur_ready, i + 1)
                for t in range(many):
                    wait(dve, hot_used, i * many + t - HOT + 1)
                    v.tensor_scalar(hot1[:, t % HOT, :], iota, cur[:, 0, t:t + 1], None,
                                    ALU.is_equal).then_inc(hot_ready, 1)
                    v.tensor_scalar(hot2[:, t % HOT, :], iota, cur[:, 1, t:t + 1], cur[:, 2, t:t + 1],
                                    ALU.is_equal, ALU.mult).then_inc(hot_ready, 1)

            one_hots(0)
            with dve.Fori(1, SPREAD) as i:
                one_hots(i)

            def weigh(e, i=0):
                b, j = divmod(e, JB)
                if j == 0:
                    dve.wait_ge(g_loaded[b % 2], i * 16 + 16 * (b // 2 + 1))
                dve.wait_ge(act_loaded[e % AS], i * (16 * 2 * JB // AS) + 16 * (e // AS + 1))
                wait(dve, p_lo_ready, i * (2 * JB) + e - 1)
                v.tensor_tensor(weighed[:, e % 2, :], act_in[:, e % AS, :], gblk[:, b % 2, :, j],
                                ALU.mult).then_inc(weighed_ready, 1)

            def weighted_low(e, i=0):
                dve.wait_ge(p_hi_ready, i * (2 * JB) + e + 1)
                v.tensor_tensor(p_split[:, e % PS, 1, :], weighed[:, e % 2, :], p_split[:, e % PS, 0, :],
                                ALU.subtract).then_inc(p_lo_ready, 1)

            def second(b, i=0):
                for e in range(b * JB, (b + 1) * JB):
                    if e + 1 < NE:
                        weigh(e + 1, i)
                    weighted_low(e, i)

            weigh(0)
            for b in range(2):
                second(b)
            with dve.Fori(0, NB // 2 - 2) as i:
                second(2, i)
                second(3, i)
            for b in range(NB - 2, NB):
                second(b)
            dve.wait_ge(expert_done, 2 * NE)
            for k in (7, 0, 1, 2, 3, 4, 5, 6):
                v.scalar_tensor_tensor(out=xT[:, k, :], in0=bank[k][:, :], scalar=mod[:, 40 + k:41 + k],
                                       in1=xT[:, k, :], op0=ALU.mult, op1=ALU.add).then_inc(x3_ready, 1)
            dve.wait_ge(x3_ready, KD)
            norm(11, lambda k: xT[:, k, :], lambda k: hT[:, k, :], lambda k: sm("final_g", k))

        @block.tensor
        def _(pe):
            mm = nc.tensor.matmul
            tile = [0]
            split_tile = [0]
            job = [0]
            held = {w_used: 0, raw_used: 0}

            def weight():
                n = tile[0]
                tile[0] += 1
                if KINDS[n] == "R":
                    pe.wait_ge(tile_loaded[n % RING], 16 * (n // RING + 1))
                    return ring[:, n % RING, :]
                split_tile[0] += 1
                pe.wait_ge(w_ready, split_tile[0])
                return w_split[:, (split_tile[0] - 1) % 2]

            def skip(n):
                assert KINDS[tile[0]:tile[0] + n] == "A" * n
                tile[0] += n

            def square_sum(idx, k, free=T):
                n = norm_base[idx] + k
                pe.wait_ge(sq_ready, n + 1)
                if k == 0 and idx:
                    pe.wait_ge(rms_ready, idx)
                mm(bank[7][:, 0:free], ones, sq[:, n % 2, 0:free], start=(k == 0),
                   stop=(k == NORMS[idx] - 1)).then_inc(sq_summed, 1)

            def norm(idx, free=T):
                for k in range(NORMS[idx]):
                    square_sum(idx, k, free)

            def sum_over_partitions(idx):
                pe.wait_ge(sq_summed, norm_base[idx] + KD - 1)
                pe.wait_ge(rms_ready, idx)
                mm(bank[7][:, :], ones, rms[:, :], start=True, stop=True).then_inc(sq_summed, 1)

            def release(n, which=None):
                held[which or w_used] += n

            def product(*args, start, stop, last=False):
                ins = mm(*args, start=start, stop=stop)
                if not last:
                    for semaphore in held:
                        if held[semaphore]:
                            ins.then_inc(semaphore, held[semaphore])
                            held[semaphore] = 0
                            break
                return ins

            def parts_of(pair, *index):
                return [pair[(slice(None), part) + index] for part in range(2)]

            def products(out_, w, x, start=True, stop=True):
                product(out_, w[0], x[0], start=start, stop=False)
                product(out_, w[0], x[1], start=False, stop=False)
                return product(out_, w[1], x[0], start=False, stop=stop, last=stop)

            def bank_free(j):
                before = [i for i in range(j) if bank_of[i] == bank_of[j]]
                if before:
                    pe.wait_ge(*taken(before[-1]))

            def project(chunks, n=T, ready=None):
                j = job[0]
                job[0] += 1
                bank_free(j)
                for k, (w, x) in enumerate(chunks):
                    if ready:
                        ready(k)
                    last = products(bank[bank_of[j]][:, 0:n], w, x, k == 0, k == len(chunks) - 1)
                last.then_inc(proj_done, 1)

            def tile_chunks(w, x, many=KD, w0=0):
                return [([w[:, part, (w0 + k) * P:(w0 + k + 1) * P] for part in range(2)],
                         [x[:, part, k, :] for part in range(2)]) for k in range(many)]

            def after_split(name):
                return lambda k: pe.wait_ge(low_ready, split_base[name] + k + 1)

            def dense(count, x, ready=None, n=T):
                for m in range(count):
                    w = weight()
                    project(tile_chunks(w, x), n=n, ready=ready if m == 0 else None)
                    release(1)

            def token_major(x, n, tiles=NT, per=2):
                width = D // per
                j = job[0]
                job[0] += tiles
                for q in range(KD // per):
                    w = weight()
                    for t in range(tiles):
                        if q == 0:
                            bank_free(j + t)
                        for c in range(per):
                            k = q * per + c
                            last = products(bank[bank_of[j + t]][:, 0:n],
                                            [x[:, part, k, t * P:(t + 1) * P] for part in range(2)],
                                            [w[:, part, c * width:c * width + n] for part in range(2)],
                                            k == 0, k == KD - 1)
                        if k == KD - 1:
                            last.then_inc(proj_done, 1)
                    release(1)

            def attend(u0, units, q, k, width, pieces, vals):
                for i in range(units + 2):
                    if i < units:
                        u = u0 + i
                        if u >= 2:
                            pe.wait_ge(logits_ready, u - 1)
                        mm(bank[u % 2][:, 0:width(i)], q(i), k(i), start=True, stop=True).then_inc(qk_done, 1)
                    if 1 <= i <= units:
                        n, u = i - 1, u0 + i - 1
                        pe.wait_ge(prob_ready, u + 1)
                        if u >= 2:
                            pe.wait_ge(probT_ready, u - 1)
                        for c, w in enumerate(pieces(n)):
                            last = nc.tensor.transpose(bank[2 + u % 2][0:w, c * P:(c + 1) * P],
                                                       prob[:, u % 2, c * P:c * P + w], ident)
                        last.then_inc(prob_turned, 1)
                    if i >= 2:
                        n, u = i - 2, u0 + i - 2
                        pe.wait_ge(probT_ready, u + 1)
                        if u >= 2:
                            pe.wait_ge(head_out, u - 1)
                        parts = pieces(n)
                        for c, w in enumerate(parts):
                            last = mm(bank[4 + u % 2][:, 0:HD], probT[0:w, u % 2, c * P:(c + 1) * P], vals(n, c),
                                      start=(c == 0), stop=(c == len(parts) - 1))
                        last.then_inc(pv_done, 1)

            def turn_chosen(t):
                pe.wait_ge(chosen_ready, t + 1)
                wait(pe, chosen_out, t - 1)
                for n in range(3):
                    last = nc.tensor.transpose(bank[4 + t % 2][:, n * P:(n + 1) * P], chosen[:, t, n * P:(n + 1) * P], ident)
                last.then_inc(chosen_turned, 1)

            def turn(count, src, free, base):
                for c in range(count):
                    if c >= 2:
                        pe.wait_ge(free, base + c - 1)
                    for t in range(NT):
                        last = nc.tensor.transpose(bank[2 + c % 2][:, t * P:(t + 1) * P],
                                                   src[:, t, c * P:(c + 1) * P], ident)
                    last.then_inc(turned, 1)

            pe.wait_ge(consts_in_sem, 32)
            norm(0)
            dense(8, h_split, ready=after_split(0))
            token_major(h_split, 408)
            dense(12, h_split)
            pe.wait_ge(cmp_pe_ready, 4)
            for kv in range(2):
                for j in range(32):
                    if j % 8 == 0:
                        w = weight()
                    w1 = w[:, (j % 8) * P:(j % 8 + 1) * P]
                    for g in range(2):
                        rows_ = slice(g * HD, (g + 1) * HD)
                        last = product(bank[6 - g][0:NCMP, kv * P:(kv + 1) * P],
                                       placed[rows_, 2 * kv + j // 16, j:j + 16 * (NCMP - 1) + 1:16], w1[rows_],
                                       start=(j == 0), stop=(j == 31), last=(j == 31))
                    if j % 8 == 7:
                        release(1, raw_used)
                last.then_inc(cmp_hidden, 1)
            norm(1)
            for c in range(4):
                pe.wait_ge(cmp_gelu, c + 1)
                last = nc.tensor.transpose(bank[4][:, c * 32:c * 32 + NCMP], hid_rows[0:NCMP, c, :],
                                           const[0:NCMP, C_ID:C_ID + NCMP])
            last.then_inc(cmp_turned, 1)
            pe.wait_ge(cmp_turned_out, 1)
            for g in range(2):
                mm(bank[2][:, 0:NCMP], sm("w2k", g * P, P), hid[:, 0, g, 0:NCMP], start=(g == 0), stop=(g == 1))
            for g in range(2):
                last = mm(bank[2][0:NCMP, 128 + g * HD:128 + (g + 1) * HD], hid[:, 1, g, 0:NCMP], sm("w2v", 0, HD),
                          start=True, stop=True)
            last.then_inc(cmp_kv, 1)

            def nsa_q(i):
                br, t, h = nsa_unit(i)
                g = h // 4
                return qk[g * HD:(g + 1) * HD, h % 4, t * P:(t + 1) * P]

            def nsa_k(i):
                br, t, h = nsa_unit(i)
                g = h // 4
                if br == 2:
                    return kcmp[g * HD:(g + 1) * HD, 0:NCMP]
                lo = 0 if br == 0 else max(t - 2, 0)
                return qk[g * HD:(g + 1) * HD, 6 + br, lo * P:(t + 1) * P]

            def nsa_v(i, c):
                br, t, h = nsa_unit(i)
                g = h // 4
                if br == 2:
                    return vcmp[0:NCMP, g * HD:(g + 1) * HD]
                lo = 0 if br == 0 else max(t - 2, 0)
                a0 = (0, 256)[br] + g * HD
                return vtok[:, lo + c, a0:a0 + HD]

            for s_, val in (taken(first["conv"] - 1), taken(first["conv"] + 11)):
                pe.wait_ge(s_, val)
            pe.wait_ge(cmp_done, 2)
            attend(0, 96, nsa_q, nsa_k, nsa_width, nsa_pieces, nsa_v)
            pe.wait_ge(head_out, 96)
            turn(4, o_tok, turned_out, 0)
            norm(2)
            for m in range(8):
                w = weight()
                chunks = [([w[:, part, k * P:(k + 1) * P] for part in range(2)],
                           [merged[:, part, k, :] if k < 4 else conv_split[:, k - 4, 1 + part, :] for part in range(2)])
                          for k in (4, 5, 6, 7, 0, 1, 2, 3)]
                project(chunks, ready=(lambda k: pe.wait_ge(low_ready, split_base[1] + k + 1)) if m == 0 else None)
                release(1)
                if m == 0:
                    norm(3, NM)
            sum_over_partitions(4)
            dense(2, m_split, ready=after_split(3), n=NM)
            token_major(m_split, NM, tiles=2, per=4)
            norm(5)
            dense(2, h_split, ready=after_split(5))
            s_, val = taken(first["mq"] + 1)
            pe.wait_ge(s_, val)
            attend(96, 16, lambda i: mq[(i % 2) * HD:(i % 2 + 1) * HD, (i % MH) // 2, (i // MH) * P:(i // MH + 1) * P],
                   lambda i: mk[(i % 2) * HD:(i % 2 + 1) * HD, (i % MH) // 2, :], lambda i: NM,
                   lambda i: [P, P], lambda i, c: mv[:, c, (i % MH) * HD:(i % MH + 1) * HD])
            pe.wait_ge(head_out, 96 + 16)
            turn(2, om_tok, full_ready, 0)
            pe.wait_ge(low_ready, split_base["om"] + 2)
            for half in range(2):
                w = weight()
                for m in range(4):
                    project(tile_chunks(w, om_split, 2, 2 * m))
                    if m == 3:
                        release(1)
                    if half or m:
                        square_sum(6, 4 * half + m - 1)
            square_sum(6, 7)
            norm(7)
            def ada(g):
                pe.wait_ge(ada_used, (g + 1) * KD)
                for m in range(KD):
                    last = mm(bank[6][:, g * KD + m:g * KD + m + 1], sq[:, m // 4, m % 4 * P:(m % 4 + 1) * P],
                              ones[:, 0:1], start=True, stop=True)
                last.then_inc(ada_done, 1)

            for m in range(KF):
                w = weight()
                project(tile_chunks(w, h_split), ready=after_split(7) if m == 0 else None)
                release(1)
                for g in range(5):
                    if m and ADA_AT[m - 1] < (g + 1) * KD <= ADA_AT[m]:
                        ada(g)
                w = weight()
                project(tile_chunks(w, h_split))
                release(1)
                skip(ADA[m])
            pe.wait_ge(low_ready, split_base["ff"] + KF)
            for m in range(8):
                j = job[0]
                job[0] += 1
                bank_free(j)
                for k in range(KF):
                    if k % KD == 0:
                        if k:
                            release(1)
                        w = weight()
                    last = products(bank[bank_of[j]][:, :],
                                    [w[:, part, k % KD * P:(k % KD + 1) * P] for part in range(2)],
                                    [ff_split[:, part, k, :] for part in range(2)], k == 0, k == KF - 1)
                last.then_inc(proj_done, 1)
                release(1)
                if m == 0:
                    ada(5)
            sum_over_partitions(8)
            norm(9)
            dense(8, h_split, ready=after_split(9))
            dense(8, h_split)
            dense(2, h_split)
            dense(4, h_split)
            token_major(h_split, T)
            token_major(h_split, T)
            s_, val = taken(first["vb"] + 3)
            pe.wait_ge(s_, val)
            attend(112, 32, lambda i: qk2[(i % 2) * HD:(i % 2 + 1) * HD, (i % NH) // 2, (i // NH) * P:(i // NH + 1) * P],
                   lambda i: qk2[(i % 2) * HD:(i % 2 + 1) * HD, 4 + (i % NH) // 2, 0:(i // NH + 1) * P],
                   lambda i: P * (i // NH + 1), lambda i: [P] * (i // NH + 1),
                   lambda i, c: va[:, c, (i % NH) * HD:(i % NH + 1) * HD])
            pe.wait_ge(rows_m, 1)
            pe.wait_ge(rows_exp, 1)
            for src, c0 in ((row_b, 0), (row_f, 16)):
                for t in range(NT):
                    last = nc.tensor.transpose(bank[6][:, c0 + t * BH:c0 + (t + 1) * BH],
                                               src[:, t * P:(t + 1) * P], const[0:BH, C_ID:C_ID + BH])
            last.then_inc(cols_done, 1)
            pe.wait_ge(head_out, UNITS)
            pe.wait_ge(conv2_ready, 8)
            def m_row(h):
                wait(pe, mrow_out, h - 1)
                mm(bank[4 + h % 2][:, :], const[0:BH, C_SEL + h * P:C_SEL + (h + 1) * P], row_i,
                   start=True, stop=True).then_inc(mrow_done, 1)

            m_row(0)
            for h in range(BH):
                if h + 1 < BH:
                    m_row(h + 1)
                for s in range(NT):
                    n = h * NT + s
                    if n >= 2:
                        pe.wait_ge(lqk_ready, n - 1)
                    mm(bank[n % 2][:, 0:T - s * P], cv2[:, 4 + h, s * P:(s + 1) * P], cv2[:, h, s * P:T],
                       start=True, stop=True).then_inc(lqk_done, 1)
                pe.wait_ge(lqk_ready, (h + 1) * NT)
                if h:
                    pe.wait_ge(lnum_out, h * NT)
                for t in range(NT):
                    for s in range(t + 1):
                        last = mm(bank[2 + t // 2][:, (t % 2) * 256:(t % 2) * 256 + P + 1],
                                  wqk[:, h % 2, s, (t - s) * P:(t - s + 1) * P], vb[:, s, h, :],
                                  start=(s == 0), stop=(s == t))
                last.then_inc(lpv_done, 1)
            pe.wait_ge(lnum_out, BH * NT)
            turn(4, oa_tok, full_ready, split_base["ya"])
            w = weight()
            project(tile_chunks(w, h_split))
            release(1)
            w_ab = weight()
            pe.wait_ge(low_ready, split_base["ya"] + 4)
            project(tile_chunks(w_ab, ya_split, 4))
            pe.wait_ge(hb_ready, 16)
            pe.wait_ge(full_ready, split_base["ya"] + 4)
            turn(4, hb_tok, full_ready, split_base["yb"])
            pe.wait_ge(low_ready, split_base["yb"] + 4)
            for m in range(KD):
                if m:
                    w = weight()
                    project(tile_chunks(w, h_split))
                    release(1)
                    w_ab = weight()
                    project(tile_chunks(w_ab, ya_split, 4))
                project(tile_chunks(w_ab, yb_split, 4, 4))
                release(1)
                w = weight()
                project(tile_chunks(w, h_split))
                release(1)
            dense(8, y2_split, ready=after_split("y2"))
            sum_over_partitions(10)
            dense(16, h_split, ready=after_split(10))
            keys = [weight(), weight()]
            s_, val = taken(first["pq"] + 15)
            pe.wait_ge(s_, val)
            for t in range(NT):
                for q in range(4):
                    if t:
                        pe.wait_ge(score_out, 4 * (t - 1) + q + 1)
                    for j in range(4 * q, 4 * q + 4):
                        last = product(bank[2 + q][:, (j % 4) * P:(j % 4 + 1) * P], pq[:, j, t * P:(t + 1) * P],
                                       keys[j // 8][:, (j % 8) * P:(j % 8 + 1) * P], start=True, stop=True,
                                       last=(j % 4 == 3))
                    last.then_inc(score_done, 1)
            release(2, raw_used)

            def up(e, i=0):
                wait(pe, gelu_ready, i * JB + e - 1)
                pe.wait_ge(w_lo_ready, i * JB + e + 1)
                for k in range(KD):
                    w = [w_split[:, e % 2, part, k * P:(k + 1) * P] for part in range(2)]
                    x = [h_split[:, part, k, :] for part in range(2)]
                    last = products(bank[e % 2][:, :], w, x, k == 0, k == KD - 1)
                last.then_inc(expert_done, 1)

            for e in range(JB):
                up(e)
            with pe.Fori(0, CHOICE - 1) as i:
                for e in range(JB, 2 * JB):
                    up(e, i)
            for e in range(CHOICE * JB, (CHOICE + 1) * JB):
                up(e)
            for t in range(NT):
                turn_chosen(t)

            def spread(n, i):
                wait(pe, staged, i * (TB // 4) + n - 3)
                for t in range(4 * n, 4 * n + 4):
                    pe.wait_ge(hot_ready, i * (2 * TB) + 2 * (t + 1))
                    mm(bank[2 + n % 4][:, (t % 4) * P:(t % 4 + 1) * P], hot1[:, t % HOT, :], hot2[:, t % HOT, :],
                       start=True, stop=True).then_inc(hot_used, 1)

            def spread_block(i):
                for j in range(JB):
                    up((CHOICE + 1) * JB + j, i)
                    for n in range(sum(QUADS[:j]), sum(QUADS[:j + 1])):
                        spread(n, i)

            spread_block(0)
            with pe.Fori(1, SPREAD) as i:
                spread_block(i)

            def down(e, i=0):
                pe.wait_ge(w_lo_ready, i * (2 * JB) + NE + e + 1)
                pe.wait_ge(p_lo_ready, i * (2 * JB) + e + 1)
                for k in (2, 3, 4, 5, 6, 7, 0, 1):
                    if e == 0 and k == 0:
                        pe.wait_ge(gelu_ready, NE)
                    last = products(bank[k][:, :], [w_split[:, e % 2, part, k * P:(k + 1) * P] for part in range(2)],
                                    [p_split[:, e % PS, part, :] for part in range(2)], e == 0, e == NE - 1)
                last.then_inc(expert_done, 1)

            pe.wait_ge(staged, T // 4)
            for e in range(2 * JB):
                down(e)
            with pe.Fori(0, NB // 2 - 2) as i:
                for e in range(2 * JB, 4 * JB):
                    down(e, i)
            for e in range(NE - 2 * JB, NE):
                down(e)
            norm(11)


def kernel(**inputs):
    import numpy as _np
    import concourse.bacc as _bacc
    from concourse import mybir as _mybir
    from concourse.bass_utils import run_bass_kernel_spmd as _run

    i = {k: _np.asarray(v) for k, v in inputs.items()}
    sel, win, cmp, band = biases(i)
    arrays = {
        "weights": weight_stream(i),
        "x_t": i["x"][0].T.reshape(KD, P, T),
        "mem_t": i["mem"][0].T.reshape(KD, P, NM),
        "smalls": smalls(i), "consts": constants(),
        "bias_sel": sel, "bias_win": win, "bias_cmp": cmp, "bias_band": band,
    }
    arrays = {k: _np.ascontiguousarray(v) for k, v in arrays.items()}
    nc = _bacc.Bacc("TRN2", target_bir_lowering=False, num_devices=1)
    args = [nc.dram_tensor(k, v.shape, _mybir.dt.from_np(v.dtype), kind="ExternalInput").ap()
            for k, v in arrays.items()]
    result = nc.dram_tensor("out_t", (KD, P, T), _mybir.dt.float32, kind="ExternalOutput").ap()
    build(nc, *args, result)
    r = _run(nc, [arrays], core_ids=[0])
    got = r.results[0]["out_t"]
    return _np.ascontiguousarray(_np.asarray(got).reshape(D, T).T).reshape(1, T, D)
```
